# Optimizing a Trainium2 kernel written in Bass

```python
import math
import jax, jax.numpy as jnp
from jax import lax
import numpy as np

D_MODEL = 1024
BATCH = 1
SEQ = 2048
DEPTH = 1
DEC_BATCH = 8
DEC_SEQ = 8
PAST_LEN = 16384
PAGE_SIZE = 128

N_MEM = 256
MIX_WIDTH = 2 * D_MODEL
ML_WIDTH = D_MODEL
ML_HEADS = 4
ML_HEAD_DIM = ML_WIDTH // ML_HEADS
CONV_CH = D_MODEL // 2
CONV_K = 3
XA_WIDTH = D_MODEL // 2
XA_HEADS = 4
XA_HEAD_DIM = XA_WIDTH // XA_HEADS
CHUNK = 64
EPS = 1e-6
IN_SIZES = [ML_WIDTH] * 5 + [ML_HEADS, ML_HEADS] + [CONV_CH] * 4 + [XA_WIDTH] * 2
IN_COLS = sum(IN_SIZES)

kernel_name = "hybrid_mlstm_shortconv_memxattn_step"

def rms_norm(x, g):
    xf = x.astype(jnp.float32)
    r = lax.rsqrt(jnp.mean(xf * xf, axis=-1, keepdims=True) + EPS)
    return (xf * r).astype(x.dtype) * g

def split_in(p):
    idx = [int(c) for c in np.cumsum(IN_SIZES)[:-1]]
    return jnp.split(p, idx, axis=-1)

def mlstm_chunkwise(q, k, v, i_pre, logf, C0, n0, m0):
    out_dtype = q.dtype
    f32 = jnp.float32
    B, T, H, d = q.shape
    L = math.gcd(T, CHUNK)
    nc = T // L

    def to_chunks(a):
        a = a.astype(f32).reshape((B, nc, L) + a.shape[2:])
        return jnp.moveaxis(a, 1, 0)

    xs = tuple(to_chunks(a) for a in (q, k, v, i_pre, logf))
    causal = jnp.tril(jnp.ones((L, L), dtype=bool))

    def step(carry, inp):
        C, n, m = carry
        qb, kb, vb, ib, fb = inp
        F = jnp.moveaxis(jnp.cumsum(fb, axis=1), 1, 2)
        ig = jnp.moveaxis(ib, 1, 2)
        Dm = ig[:, :, None, :] + F[:, :, :, None] - F[:, :, None, :]
        Dm = jnp.where(causal, Dm, -jnp.inf)
        inter = m[:, :, None] + F
        m_t = jnp.maximum(inter, jnp.max(Dm, axis=-1))
        S = jnp.einsum('bthd,bshd->bhts', qb, kb) * jnp.exp(Dm - m_t[..., None])
        w_inter = jnp.exp(inter - m_t)
        num = (w_inter[..., None] * jnp.einsum('bthd,bhde->bhte', qb, C)
               + jnp.einsum('bhts,bshe->bhte', S, vb))
        den = w_inter * jnp.einsum('bthd,bhd->bht', qb, n) + jnp.sum(S, axis=-1)
        h = num / jnp.maximum(jnp.abs(den), jnp.exp(-m_t))[..., None]
        m_new = m_t[:, :, -1]
        F_L = F[:, :, -1]
        w_C = jnp.exp(m + F_L - m_new)
        w_s = jnp.exp(ig + F_L[..., None] - F - m_new[..., None])
        C_new = w_C[..., None, None] * C + jnp.einsum('bhs,bshd,bshe->bhde', w_s, kb, vb)
        n_new = w_C[..., None] * n + jnp.einsum('bhs,bshd->bhd', w_s, kb)
        return (C_new, n_new, m_new), jnp.moveaxis(h, 1, 2)

    (C, n, m), hs = lax.scan(step, (C0.astype(f32), n0.astype(f32), m0.astype(f32)), xs)
    h = jnp.moveaxis(hs, 0, 1).reshape(B, T, H, d)
    return (h.astype(out_dtype), C.astype(out_dtype), n.astype(out_dtype), m.astype(out_dtype))

def memory_kv(mem, g_mem, w_mem_kv):
    B = mem.shape[0]
    kv = rms_norm(mem, g_mem) @ w_mem_kv
    mk, mv = jnp.split(kv, 2, axis=-1)
    return (mk.reshape(B, N_MEM, XA_HEADS, XA_HEAD_DIM), mv.reshape(B, N_MEM, XA_HEADS, XA_HEAD_DIM))

def hybrid_layer(x, mem_k, mem_v, C0, n0, m0, conv0,
                 g_norm, w_in, b_if, g_head, conv_w, conv_b, w_out):
    B, T, _ = x.shape
    xn = rms_norm(x, g_norm)
    proj = xn @ w_in
    (q, k, v, o_pre, z_ml, i_pre, f_pre,
     b_g, c_g, xc, z_cv, q_x, z_x) = split_in(proj)

    heads = lambda a: a.reshape(B, T, ML_HEADS, ML_HEAD_DIM)
    i_pre = i_pre + b_if[:ML_HEADS]
    logf = jax.nn.log_sigmoid(f_pre + b_if[ML_HEADS:])
    h, C, n, m = mlstm_chunkwise(heads(q), heads(k) * (ML_HEAD_DIM ** -0.5), heads(v),
                                 i_pre, logf, C0, n0, m0)
    h = jax.nn.sigmoid(heads(o_pre)) * h
    h = rms_norm(h, g_head.reshape(ML_HEADS, ML_HEAD_DIM))
    y_ml = h.reshape(B, T, ML_WIDTH) * jax.nn.silu(z_ml)

    u = c_g * xc
    ext = jnp.concatenate([conv0.astype(u.dtype), u], axis=1)
    yc = conv_b + sum(conv_w[j] * ext[:, j:j + T] for j in range(CONV_K))
    y_cv = b_g * yc * jax.nn.silu(z_cv)
    conv_new = ext[:, T:]

    qx = q_x.reshape(B, T, XA_HEADS, XA_HEAD_DIM)
    s = jnp.einsum('bthd,bshd->bhts', qx, mem_k).astype(jnp.float32) * (XA_HEAD_DIM ** -0.5)
    p = jax.nn.softmax(s, axis=-1).astype(x.dtype)
    y_xa = jnp.einsum('bhts,bshd->bthd', p, mem_v).reshape(B, T, XA_WIDTH) * jax.nn.silu(z_x)

    y = jnp.concatenate([y_ml, y_cv, y_xa], axis=-1) @ w_out
    return (x + y, C, n, m, conv_new)

def setup_inputs(seed: int = 0) -> dict:
    key = jax.random.key(seed)
    ks = jax.random.split(key, 20)
    nrm = jax.random.normal
    f32 = jnp.float32
    x_prompt = nrm(ks[0], (BATCH, SEQ, D_MODEL), f32)
    x_sample = nrm(ks[1], (DEC_BATCH, DEC_SEQ, D_MODEL), f32)
    state_mlstm_C = 0.05 * nrm(ks[2], (DEPTH, DEC_BATCH, ML_HEADS, ML_HEAD_DIM, ML_HEAD_DIM), f32)
    state_mlstm_n = 0.5 * nrm(ks[3], (DEPTH, DEC_BATCH, ML_HEADS, ML_HEAD_DIM), f32)
    state_mlstm_m = jax.random.uniform(ks[4], (DEPTH, DEC_BATCH, ML_HEADS), f32, 0.0, 4.0)
    state_conv = 0.5 * nrm(ks[5], (DEPTH, DEC_BATCH, CONV_K - 1, CONV_CH), f32)
    cache_mem_k = nrm(ks[6], (DEPTH, DEC_BATCH, N_MEM, XA_HEADS, XA_HEAD_DIM), f32)
    cache_mem_v = nrm(ks[7], (DEPTH, DEC_BATCH, N_MEM, XA_HEADS, XA_HEAD_DIM), f32)
    mem_prompt = nrm(ks[8], (BATCH, N_MEM, D_MODEL), f32)
    g_norm = 1.0 + 0.05 * nrm(ks[9], (DEPTH, D_MODEL), f32)
    w_in = nrm(ks[10], (DEPTH, D_MODEL, IN_COLS), f32) * D_MODEL ** -0.5
    forget_bias = jnp.tile(jnp.linspace(3.0, 6.0, ML_HEADS, dtype=f32), (DEPTH, 1))
    b_if = jnp.concatenate([0.1 * nrm(ks[11], (DEPTH, ML_HEADS), f32),
                            forget_bias + 0.1 * nrm(ks[12], (DEPTH, ML_HEADS), f32)], axis=-1)
    g_head = 1.0 + 0.05 * nrm(ks[13], (DEPTH, ML_WIDTH), f32)
    conv_w = nrm(ks[14], (DEPTH, CONV_K, CONV_CH), f32) * CONV_K ** -0.5
    conv_b = 0.02 * nrm(ks[15], (DEPTH, CONV_CH), f32)
    g_mem = 1.0 + 0.05 * nrm(ks[16], (DEPTH, D_MODEL), f32)
    w_mem_kv = nrm(ks[17], (DEPTH, D_MODEL, 2 * XA_WIDTH), f32) * D_MODEL ** -0.5
    w_out = nrm(ks[18], (DEPTH, MIX_WIDTH, D_MODEL), f32) * MIX_WIDTH ** -0.5
    g_final = 1.0 + 0.05 * nrm(ks[19], (D_MODEL,), f32)
    return {"x_prompt": x_prompt, "x_sample": x_sample,
            "state_mlstm_C": state_mlstm_C, "state_mlstm_n": state_mlstm_n,
            "state_mlstm_m": state_mlstm_m, "state_conv": state_conv,
            "cache_mem_k": cache_mem_k, "cache_mem_v": cache_mem_v,
            "mem_prompt": mem_prompt,
            "g_norm": g_norm, "w_in": w_in, "b_if": b_if, "g_head": g_head,
            "conv_w": conv_w, "conv_b": conv_b, "g_mem": g_mem, "w_mem_kv": w_mem_kv,
            "w_out": w_out, "g_final": g_final}

def reference(x_prompt, x_sample, state_mlstm_C, state_mlstm_n, state_mlstm_m, state_conv,
              cache_mem_k, cache_mem_v, mem_prompt,
              g_norm, w_in, b_if, g_head, conv_w, conv_b, g_mem, w_mem_kv, w_out, g_final):
    Bp = x_prompt.shape[0]
    dt = x_prompt.dtype
    hp, hs = x_prompt, x_sample
    Cp_l, np_l, mp_l, cvp_l, mkp_l, mvp_l = [], [], [], [], [], []
    Cs_l, ns_l, ms_l, cvs_l = [], [], [], []
    for l in range(DEPTH):
        lw = (g_norm[l], w_in[l], b_if[l], g_head[l], conv_w[l], conv_b[l], w_out[l])
        mk_p, mv_p = memory_kv(mem_prompt, g_mem[l], w_mem_kv[l])
        C0 = jnp.zeros((Bp, ML_HEADS, ML_HEAD_DIM, ML_HEAD_DIM), dt)
        n0 = jnp.zeros((Bp, ML_HEADS, ML_HEAD_DIM), dt)
        m0 = jnp.zeros((Bp, ML_HEADS), dt)
        cv0 = jnp.zeros((Bp, CONV_K - 1, CONV_CH), dt)
        hp, Cp, np_, mp, cvp = hybrid_layer(hp, mk_p, mv_p, C0, n0, m0, cv0, *lw)
        hs, Cs, ns, ms, cvs = hybrid_layer(hs, cache_mem_k[l], cache_mem_v[l],
                                           state_mlstm_C[l], state_mlstm_n[l],
                                           state_mlstm_m[l], state_conv[l], *lw)
        Cp_l.append(Cp); np_l.append(np_); mp_l.append(mp); cvp_l.append(cvp)
        mkp_l.append(mk_p); mvp_l.append(mv_p)
        Cs_l.append(Cs); ns_l.append(ns); ms_l.append(ms); cvs_l.append(cvs)
    y_prompt = rms_norm(hp, g_final)
    y_sample = rms_norm(hs, g_final)
    return (y_prompt, y_sample,
            jnp.stack(Cp_l), jnp.stack(np_l), jnp.stack(mp_l), jnp.stack(cvp_l),
            jnp.stack(mkp_l), jnp.stack(mvp_l),
            jnp.stack(Cs_l), jnp.stack(ns_l), jnp.stack(ms_l), jnp.stack(cvs_l))


_drawn_inputs = setup_inputs


def setup_inputs(seed=0):
    import zlib

    import numpy as np

    out = dict(_drawn_inputs(seed))
    spreads = {}
    factors = {'g_head': 2.912, 'conv_b': 8.0, 'cache_mem_k': 3.737, 'cache_mem_v': 2.917}
    for name, (base, spread) in spreads.items():
        noise = np.random.default_rng([zlib.crc32(name.encode()), seed]).standard_normal(out[name].shape)
        drawn = base * np.exp(spread * noise) if base else spread * noise
        out[name] = __import__('jax').numpy.asarray(drawn.astype(out[name].dtype))
    for name, factor in factors.items():
        out[name] = (out[name] * factor).astype(out[name].dtype)
    return out
```

```python
from contextlib import ExitStack

import concourse.bass as bass
from concourse import mybir

F32 = mybir.dt.float32
F32R = mybir.dt.float32r
ALU = mybir.AluOpType
ACT = mybir.ActivationFunctionType
AX = mybir.AxisListType

P = 128
D = 1024
KD = D // P
T = 2048
DB, DT = 8, 8
TS = DB * DT
TT = T + TS
NT = T // P
H = 4
HD = 256
XD = 128
CC = 512
NM = 256
EPS = 1e-6
MASKED = -1e30
XA_SCALE = XD ** -0.5
K_SCALE = HD ** -0.5
COL_QK, COL_TM, COL_IF, COL_CV = 0, 2048, 5120, 5128
COL_XA = COL_CV + 4 * CC
CHUNKS = [(c * 384, 384) for c in range(5)] + [(1920, 192)]


class Semaphores:

    def __init__(self, nc):
        self.nc, self.made = nc, {}

    def __getitem__(self, name):
        if name not in self.made:
            self.made[name] = self.nc.alloc_semaphore(name)
        return self.made[name]

    def phase_done(self):
        self.nc.all_engine_barrier()
        self.nc.clear_and_free_semaphores(list(self.made.values()))
        self.nc.all_engine_barrier()
        self.made = {}


def wait(eng, sem, value):
    if isinstance(value, int) and value <= 0:
        return
    eng.wait_ge(sem, value)


def over_tiles(eng, n, body, last=0):
    body(0, 0)
    body(1, 1)
    pairs = (n - last) // 2
    with eng.Fori(1, pairs) as pair:
        body(2 * pair, 0)
        body(2 * pair + 1, 1)
    for t in range(2 * pairs, n):
        body(t, t % 2)


def layer(nc, x_prompt, x_sample, st_C, st_n, st_m, st_conv, mem_k, mem_v, mem_prompt,
          g_norm, w_in, b_if, g_head, conv_w, conv_b, g_mem, w_mem_kv, w_out, g_final,
          y_prompt, y_sample, C_prompt, n_prompt, m_prompt, conv_prompt, mk_prompt, mv_prompt,
          C_sample, n_sample, m_sample, conv_sample, upto=9):
    ctx = ExitStack()
    with ctx:
        S = Semaphores(nc)
        ctx.enter_context(nc.allow_non_contiguous_dma(reason="small states and gates change their layout"))

        def dram(name, shape):
            return nc.dram_tensor(name, shape, F32, kind="Internal").ap()

        def sb(c, name, shape, dt=F32):
            return c.enter_context(nc.sbuf_tensor(name, shape, dt))

        w = dict(
            qk=dram("scr_qk", (16, P, TT)), xa=dram("scr_xa", (8, P, TT)), tm=dram("scr_tm", (6, TT, 512)),
            yt=dram("scr_yt", (16, P, TT)), gate=dram("scr_gate", (8, TT)), negr=dram("scr_negr", (H, TT)),
            a=dram("scr_a", (H, TT)), g=dram("scr_g", (H, TT)), ws=dram("scr_ws", (H, TT)),
            em=dram("scr_em", (H, TT)), last=dram("scr_last", (2, H * NT)), mprev=dram("scr_mprev", (H * NT,)),
            mkT=dram("scr_mkT", (P, H, NM)),
            wc=dram("scr_wc", (H * NT + H * DB,)))
        bank = [ctx.enter_context(nc.psum_tensor(f"bank{i}", [P, 512], F32)) for i in range(8)]
        ident = sb(ctx, "ident", [P, P])

        with ExitStack() as c01:
            xh = sb(c01, "xh", [P, KD, TT], F32R)
            xl = sb(c01, "xl", [P, KD, TT], F32R)
            with ExitStack() as c:
                prep(nc, S, lambda *a: sb(c, *a), bank, ident, w, xh, xl, x_prompt, x_sample,
                     g_norm, mem_prompt, g_mem, w_mem_kv, mk_prompt, mv_prompt)
            if upto >= 1:
                with ExitStack() as c:
                    project(nc, S, lambda *a: sb(c, *a), bank, w, xh, xl, w_in, b_if, g_head, conv_w, conv_b,
                            st_conv, st_m, conv_prompt, conv_sample, m_prompt, m_sample)
        S.phase_done()
        if upto >= 2:
            with ExitStack() as c:
                mix(nc, S, lambda *a: sb(c, *a), bank, w, ident, mv_prompt, C_prompt, n_prompt)
        S.phase_done()
        if upto >= 3:
            with ExitStack() as c:
                sample(nc, S, lambda *a: sb(c, *a), bank, w, ident, st_C, st_n, mem_k, mem_v, C_sample, n_sample)
        S.phase_done()
        if upto >= 4:
            with ExitStack() as c:
                output(nc, S, lambda *a: sb(c, *a), bank, w, w_out, x_prompt, x_sample, g_final, y_prompt, y_sample)


def row_bcast(v, n):
    return v.partition_broadcast(n)


def prep(nc, S, sb, bank, ident, w, xh, xl, x_prompt, x_sample, g_norm, mem_prompt, g_mem,
         w_mem_kv, mk_prompt, mv_prompt):
    NX = NT + 1
    NR = NX + 2
    wkv = sb("wkv", [P, D])
    wkv2 = sb("wkv2", [P, D])
    xin = sb("xin", [P, 2, D])
    gx = sb("gx", [P, D])
    gm = sb("gm", [P, D])
    sq = sb("sq", [P, D])
    ss = sb("ss", [P, NR])
    ms = sb("ms", [P, NR])
    sd = sb("sd", [P, NR])
    rs = sb("rs", [P, NR])
    memT = sb("memT", [P, KD, NM])
    mkT = sb("mkT", [P, H, NM])
    kvs = sb("kvs", [P, 4, 512])
    wslice = [wkv, wkv2]
    x_rows = x_prompt[0].rearrange("(t p) d -> t p d", p=P)
    x_smp = x_sample.rearrange("b t d -> (b t) d")
    mem_rows = mem_prompt[0].rearrange("(t p) d -> t p d", p=P)
    block = nc.Block()
    ctx = ExitStack()
    block = ctx.enter_context(block)

    def rows(t):
        return TS if isinstance(t, int) and t == NT else P

    def every(eng, body):
        over_tiles(eng, NT, body)
        for t in range(NT, NR):
            body(t, t % 2)

    @block.sync
    def _(sp):
        sp.dma_start(gx[:, :], row_bcast(g_norm[0], P)).then_inc(S["g_loaded"], 16)
        sp.dma_start(gm[:, :], row_bcast(g_mem[0], P)).then_inc(S["g_loaded"], 16)

        def load(t, p):
            n = rows(t)
            wait(sp, S["x_turned"], t - 1)
            if isinstance(t, int) and t > NT:
                src = mem_rows[t - NX]
            elif isinstance(t, int) and t == NT:
                src = x_smp
            elif isinstance(t, int):
                src = x_rows[t]
            else:
                src = x_rows[bass.ds(t, 1)].rearrange("a p d -> (a p) d")
            sp.dma_start(xin[:n, p, :], src).then_inc(S[f"x_loaded{p}"], 16)
        every(sp, load)
        for k in range(KD):
            wait(sp, S["wkv_used"], k - 1)
            sp.dma_start(wslice[k % 2][:, :], w_mem_kv[0, k * P:(k + 1) * P, :]).then_inc(S[f"wkv_loaded{k % 2}"], 16)

    @block.gpsimd
    def _(pool):
        pool.memset(ident[:, :], 0.0).then_inc(S["ident_zero"], 1)
        pool.wait_ge(S["ident_zero"], 1)
        pool.affine_select(out=ident[:, :], in_=ident[:, :], compare_op=ALU.not_equal, fill=1.0, base=0,
                           pattern=[[-1, P]], channel_multiplier=1).then_inc(S["ident_ready"], 1)

    @block.scalar
    def _(act):
        def square(t, p):
            n = rows(t)
            act.wait_ge(S[f"x_loaded{p}"], 8 * (t - p) + 16)
            wait(act, S["squared"], t)
            act.activation(sq[:n, :], xin[:n, p, :], ACT.Square,
                           accum_out=ss[:n, bass.ds(t, 1)]).then_inc(S["squared"], 1)
            act.wait_ge(S["mean_ready"], t + 1)
            act.activation(sd[:n, bass.ds(t, 1)], ms[:n, bass.ds(t, 1)], ACT.Sqrt).then_inc(S["std_ready"], 1)
            for half in range(2):
                act.wait_ge(S["x_turned"], t + 1)
                dst = memT[:, 4 * half:4 * half + 4, bass.ds((t - NX) * P, P)] if isinstance(t, int) and t > NT else \
                    xh[:, 4 * half:4 * half + 4, bass.ds(t * P, n)]
                src = bank[2 * p + half].ap().rearrange("p (k n) -> p k n", k=4)[:, :, 0:n]
                act.activation(dst, src, ACT.Copy).then_inc(S["high_ready"], 1)
        every(act, square)
        for i in range(4):
            act.wait_ge(S["wkv_used"], KD)
            act.activation(kvs[:, i, :], bank[4 + i][:, :], ACT.Copy).then_inc(S["kv_copied"], 1)
        for i in range(4):
            act.wait_ge(S["kv_copied"], i + 1)
            st, kv = i // 2, i % 2
            dst = (mk_prompt, mv_prompt)[kv][0, 0].rearrange("s h d -> s (h d)")[st * P:(st + 1) * P, :]
            act.dma_start(dst, kvs[:, i, :]).then_inc(S["kv_stored"], 16)
        for st in range(2):
            act.wait_ge(S["key_turned"], st + 1)
            act.activation(mkT[:, :, st * P:(st + 1) * P], bank[st].ap().rearrange("p (h s) -> p h s", h=H),
                           ACT.Copy).then_inc(S["mkT_ready"], 1)
        act.wait_ge(S["mkT_ready"], 2)
        act.dma_start(w["mkT"], mkT[:, :, :]).then_inc(S["kv_stored"], 16)
        act.wait_ge(S["kv_stored"], 80)

    @block.vector
    def _(dve):
        dve.wait_ge(S["g_loaded"], 32)

        def norm(t, p):
            n = rows(t)
            col = bass.ds(t, 1)
            dve.wait_ge(S["squared"], t + 1)
            dve.tensor_scalar(ms[:n, col], ss[:n, col], 1.0 / D, EPS, ALU.mult, ALU.add).then_inc(S["mean_ready"], 1)
            dve.wait_ge(S["std_ready"], t + 1)
            dve.reciprocal(rs[:n, col], sd[:n, col]).then_inc(S["rstd_ready"], 1)
            dve.wait_ge(S["rstd_ready"], t + 1)
            g = gm if isinstance(t, int) and t > NT else gx
            dve.scalar_tensor_tensor(xin[:n, p, :], xin[:n, p, :], rs[:n, col], g[:n, :],
                                     ALU.mult, ALU.mult).then_inc(S["x_normed"], 1)
            if isinstance(t, int) and t > NT:
                return
            for half in range(2):
                dve.wait_ge(S["high_ready"], 2 * t + half + 1)
                src = bank[2 * p + half].ap().rearrange("p (k n) -> p k n", k=4)[:, :, 0:n]
                dve.tensor_tensor(xl[:, 4 * half:4 * half + 4, bass.ds(t * P, n)], src,
                                  xh[:, 4 * half:4 * half + 4, bass.ds(t * P, n)].bitcast(F32),
                                  ALU.subtract).then_inc(S["low_ready"], 1)
        every(dve, norm)

    @block.tensor
    def _(pe):
        pe.wait_ge(S["ident_ready"], 1)

        def turn(t, p):
            n = rows(t)
            pe.wait_ge(S["x_normed"], t + 1)
            if not isinstance(t, int) or t <= NT + 2:
                wait(pe, S["low_ready"], 2 * (t - 1))
            if isinstance(t, int) and t > NX + 1:
                pe.wait_ge(S["high_ready"], 2 * (t - 1))
            for k in range(KD):
                m = pe.transpose(bank[2 * p + k // 4][:, (k % 4) * P:(k % 4) * P + n],
                                 xin[:n, p, k * P:(k + 1) * P], ident[:n, :n])
            m.then_inc(S["x_turned"], 1)
        every(pe, turn)
        pe.wait_ge(S["high_ready"], 2 * NR)
        for k in range(KD):
            pe.wait_ge(S[f"wkv_loaded{k % 2}"], 16 * (k // 2 + 1))
            for i in range(4):
                st, kv = i // 2, i % 2
                m = pe.matmul(bank[4 + i][:, :], memT[:, k, st * P:(st + 1) * P],
                              wslice[k % 2][:, kv * 512:(kv + 1) * 512], start=(k == 0), stop=(k == KD - 1))
            m.then_inc(S["wkv_used"], 1)
        for st in range(2):
            pe.wait_ge(S["kv_copied"], 2 * st + 1)
            for h in range(H):
                m = pe.transpose(bank[st][:, h * P:(h + 1) * P], kvs[:, 2 * st, h * P:(h + 1) * P], ident[:, :])
            m.then_inc(S["key_turned"], 1)

    ctx.close()


KINDS = [("qx", 1, 24), ("gate", 1, 6), ("conv", 4, 24), ("qk", 4, 24), ("v", 2, 17), ("o", 2, 17), ("z", 2, 17),
         ("zx", 1, 24)]
RING = 4


def kind_bases():
    quads, groups, stored, out = 0, 0, [0] * RING, {}
    for kind, n, g in KINDS:
        out[kind] = (quads, groups, list(stored))
        quads, groups = quads + n, groups + n * g
        results = 6 if kind == "conv" else g
        for s in range(RING):
            stored[s] += n * len(range(s, results, RING))
    return out


BASE = kind_bases()


def ring_value(kind, i, g):
    results = 6 if kind == "conv" else dict((k, x) for k, _, x in KINDS)[kind]
    s = g % RING
    return 16 * (BASE[kind][2][s] + g // RING) + 16 * len(range(s, results, RING)) * i


class Chain:

    def __init__(self, eng, sem, base=0):
        self.eng, self.sem, self.base, self.n = eng, sem, base, 0

    def step(self, instruction):
        instruction.then_inc(self.sem, 1)
        self.n += 1

    def sync(self):
        wait(self.eng, self.sem, self.base + self.n)


def project(nc, S, sb, bank, w, xh, xl, w_in, b_if, g_head, conv_w, conv_b, st_conv, st_m,
            conv_prompt, conv_sample, m_prompt, m_sample):
    raw = sb("raw", [P, KD, 512])
    wh = sb("wh", [P, KD, 512], F32R)
    wl = sb("wl", [P, KD, 512], F32R)
    stage = sb("stage", [P, RING, 512])
    work = sb("work", [P, 1920])
    cw = sb("cw", [P, 3, 4])
    cb = sb("cb", [P, 4])
    cst = sb("cst", [P, 4, DB, 2])
    cnew_p = sb("cnew_p", [P, 4, 2])
    cnew_s = sb("cnew_s", [P, 4, DB, 2])
    bif = sb("bif", [8, 1])
    R96 = H * NT + H * DB
    gi, gf, gF, gt = (sb(n, [R96, P]) for n in ("gi", "gf", "gF", "gt"))
    gz = sb("gz", [R96, P])
    gw = work[0:R96, D:D + P]
    gm = sb("gm1", [R96, 1])
    fl, gl, mn, mprev = (sb(n, [H, NT]) for n in ("fl", "gl", "mn", "mprev"))
    cs = work[:, 0:768].rearrange("p (s n) -> p s n", s=2)
    th = work[:, 768:1536].rearrange("p (s n) -> p s n", s=2)
    ut = sb("ut", [P, 2, 386])
    us = sb("us", [P, DB, 10])
    yc = sb("yc", [P, 384])
    sil = work[:, 1536:1920]
    ghb = work[:, 0:D]
    TMK = {"v": 0, "o": 2, "z": 4}
    ng = {k: g for k, _, g in KINDS}
    ctx = ExitStack()
    block = ctx.enter_context(nc.Block())

    def quads(eng, kind, body):
        n = dict((k, x) for k, x, _ in KINDS)[kind]
        if n == 1:
            body(0)
        else:
            with eng.Fori(0, n) as i:
                body(i)

    def weights_ap(kind, i, k):
        rows = w_in[0, k * P:(k + 1) * P, :]
        if kind == "gate":
            return rows[:, COL_IF:COL_IF + P]
        if kind == "conv":
            return rows[:, COL_CV:COL_CV + 4 * CC].rearrange("p (a c) -> p a c", a=4)[:, :, bass.ds(i * P, P)]
        col = {"qk": COL_QK, "v": COL_TM, "o": COL_TM + D, "z": COL_TM + 2 * D, "qx": COL_XA,
               "zx": COL_XA + 512}[kind]
        return rows[:, bass.ds(col + 512 * i, 512)]

    @block.sync
    def _(sp):
        sp.dma_start(bif[:, :], b_if[0].rearrange("(a b) -> a b", b=1)).then_inc(S["small_loaded"], 16)
        for j in range(3):
            sp.dma_start(cw[:, j, :], conv_w[0, j].rearrange("(j p) -> p j", p=P)).then_inc(S["small_loaded"], 16)
        sp.dma_start(cb[:, :], conv_b[0].rearrange("(j p) -> p j", p=P)).then_inc(S["small_loaded"], 16)
        for j in range(4):
            sp.dma_start(cst[:, j, :, :],
                         st_conv[0, :, :, j * P:(j + 1) * P].rearrange("b w p -> p b w")).then_inc(S["small_loaded"], 16)
        for kind, n, _ in KINDS:
            if kind == "v":
                sp.wait_ge(S["conv_kept"], 4)
                sp.dma_start(ghb, row_bcast(g_head[0], P)).then_inc(S["gain_loaded"], 16)

            def load(i, kind=kind):
                q = BASE[kind][0] + i
                for k in range(KD):
                    wait(sp, S["low_split"], 8 * (q - 1) + k + 1)
                    dst = raw[:, k, :]
                    if kind == "gate":
                        dst = raw[:, k, 0:P]
                    if kind == "conv":
                        dst = dst.rearrange("p (a c) -> p a c", a=4)
                    sp.dma_start(dst, weights_ap(kind, i, k)).then_inc(S[f"raw_loaded{k}"], 16)
            quads(sp, kind, load)
        sp.wait_ge(S["conv_kept"], 4)
        for j in range(4):
            sp.dma_start(conv_prompt[0, 0, :, j * P:(j + 1) * P].rearrange("w p -> p w"),
                         cnew_p[:, j, :]).then_inc(S["conv_state_stored"], 16)
            sp.dma_start(conv_sample[0, :, :, j * P:(j + 1) * P].rearrange("b w p -> p b w"),
                         cnew_s[:, j, :, :]).then_inc(S["conv_state_stored"], 16)
        sp.wait_ge(S["conv_state_stored"], 8 * 16)

    def split(dve, q, groups, cols=512):
        def low(k):
            dve.wait_ge(S["high_split"], 8 * q + k + 1)
            dve.tensor_tensor(wl[:, k, 0:cols], raw[:, k, 0:cols], wh[:, k, 0:cols].bitcast(F32),
                              ALU.subtract).then_inc(S["low_split"], 1)
        for k in range(KD):
            dve.wait_ge(S[f"raw_loaded{k}"], 16 * (q + 1))
            if k < KD - 1:
                wait(dve, S["weights_used"], 7 * (q - 1) + k + 1)
            else:
                wait(dve, S["summed"], groups)
            dve.tensor_copy(wh[:, k, 0:cols], raw[:, k, 0:cols]).then_inc(S["high_split"], 1)
            if k:
                low(k - 1)
        low(KD - 1)

    def split_next(dve, kind, i):
        split(dve, BASE[kind][0] + i + 1, BASE[kind][1] + ng[kind] * (i + 1))

    @block.tensor
    def _(pe):
        for kind, n, G in KINDS:
            wait(pe, S["bank_free"], BASE[kind][1])

            def quad(i, kind=kind, G=G):
                q, g0 = BASE[kind][0] + i, BASE[kind][1] + G * i
                for g in range(G):
                    if g >= 8:
                        pe.wait_ge(S["bank_free"], g0 + g - 7)
                    elif not isinstance(i, int):
                        last = max(x for x in range(G) if x % 8 == g)
                        pe.wait_ge(S["bank_free"], g0 + last + 1 - G)
                    for k in range(KD):
                        if g == 0:
                            pe.wait_ge(S["low_split"], 8 * q + k + 1)
                        if kind in ("v", "o", "z"):
                            at = min(g * P, TT - P)
                            out = bank[g % 8][:, :]
                            ah, al = xh[:, k, at:at + P], xl[:, k, at:at + P]
                            bh, bl = wh[:, k, :], wl[:, k, :]
                        else:
                            (at, m), j = (CHUNKS[g], 0) if kind == "gate" else (CHUNKS[g // 4], g % 4)
                            out = bank[g % 8][:, 0:m]
                            ah, al = wh[:, k, j * P:(j + 1) * P], wl[:, k, j * P:(j + 1) * P]
                            bh, bl = xh[:, k, at:at + m], xl[:, k, at:at + m]
                        pe.matmul(out, ah, bh, start=(k == 0), stop=False)
                        pe.matmul(out, ah, bl, start=False, stop=False)
                        mm = pe.matmul(out, al, bh, start=False, stop=(k == KD - 1))
                        if g == G - 1 and k < KD - 1:
                            mm.then_inc(S["weights_used"], 1)
                    mm.then_inc(S["summed"], 1)
            quads(pe, kind, quad)

    def result(kind, i, g):
        s = g % RING
        if kind in ("v", "o", "z"):
            quad = w["tm"][bass.ds(TMK[kind] + i, 1)].rearrange("a t n -> (a t) n")
            if g < NT:
                return stage[:, s, :], quad[g * P:(g + 1) * P, :]
            return stage[P - TS:, s, :], quad[T:TT, :]
        if kind == "gate":
            at, m = CHUNKS[g]
            return stage[0:8, s, 0:m], w["gate"][:, at:at + m]
        if kind == "conv":
            at, m = CHUNKS[g]
            rows = w["yt"][bass.ds(8 + i, 1)]
        else:
            at, m = CHUNKS[g // 4]
            to, b = {"qk": (w["qk"], 4 * i), "qx": (w["xa"], 0), "zx": (w["xa"], 4)}[kind]
            rows = to[bass.ds(b + g % 4, 1)]
        return stage[:, s, 0:m], rows.rearrange("a p t -> (a p) t")[:, at:at + m]

    @block.scalar
    def _(act):
        def store(kind, i, g, ready, value):
            act.wait_ge(S[ready], value)
            src, dst = result(kind, i, g)
            act.dma_start(dst, src).then_inc(S[f"stored{g % RING}"], 16)

        def copy_kind(kind):
            def quad(i):
                G = ng[kind]
                g0 = BASE[kind][1] + G * i
                for g in range(G):
                    act.wait_ge(S["summed"], g0 + g + 1)
                    wait(act, S[f"stored{g % RING}"], ring_value(kind, i, g))
                    if kind == "gate":
                        m = CHUNKS[g][1]
                        act.activation(stage[0:8, g % RING, 0:m], bank[g % 8][0:8, 0:m], ACT.Identity,
                                       bias=bif[:, 0:1]).then_inc(S["bank_free"], 1)
                    elif kind == "o":
                        act.activation(stage[:, g % RING, :], bank[g % 8][:, :], ACT.Tanh,
                                       scale=0.5).then_inc(S["bank_free"], 1)
                    else:
                        m = 512 if kind == "v" else CHUNKS[g // 4][1]
                        act.activation(stage[:, g % RING, 0:m], bank[g % 8][:, 0:m],
                                       ACT.Copy).then_inc(S["bank_free"], 1)
                    if g:
                        store(kind, i, g - 1, "bank_free", g0 + g)
                store(kind, i, G - 1, "bank_free", g0 + G)
            quads(act, kind, quad)

        def gated_kind(kind):
            def quad(i):
                G = ng[kind]
                g0 = BASE[kind][1] + G * i
                ready, c0 = ("silu_ready", G * i) if kind == "z" else ("bank_free", g0)
                for g in range(G):
                    act.wait_ge(S["summed"], g0 + g + 1)
                    wait(act, S[f"stored{g % RING}"], ring_value(kind, i, g))
                    m = 512 if kind == "z" else CHUNKS[g // 4][1]
                    act.activation(stage[:, g % RING, 0:m], bank[g % 8][:, 0:m], ACT.Tanh,
                                   scale=0.5).then_inc(S["tanh_ready"], 1)
                    if g:
                        store(kind, i, g - 1, ready, c0 + g)
                store(kind, i, G - 1, ready, c0 + G)
            quads(act, kind, quad)

        act.wait_ge(S["small_loaded"], 16 * 9)
        copy_kind("qx")
        copy_kind("gate")
        act.wait_ge(S["gate_abs"], 1)
        act.activation(gt[:, :], gt[:, :], ACT.Exp, scale=-1.0).then_inc(S["gate_exp"], 1)
        act.wait_ge(S["gate_exp"], 1)
        act.activation(gt[:, :], gt[:, :], ACT.Ln, bias=1.0).then_inc(S["gate_log"], 1)

        def conv(i):
            g0 = BASE["conv"][1] + 24 * i
            for c, (at, m) in enumerate(CHUNKS):
                g = 4 * c
                act.wait_ge(S["summed"], g0 + g + 2)
                act.wait_ge(S["bank_free"], g0 + g - 4)
                act.activation(cs[:, c % 2, 0:m], bank[(g + 1) % 8][:, 0:m], ACT.Copy).then_inc(S["conv_c_ready"], 1)
                act.wait_ge(S["summed"], g0 + g + 4)
                act.activation(th[:, c % 2, 0:m], bank[(g + 3) % 8][:, 0:m], ACT.Tanh,
                               scale=0.5).then_inc(S["conv_t_ready"], 1)
                if c:
                    store("conv", i, c - 1, "conv_y_ready", 6 * i + c)
            store("conv", i, 5, "conv_y_ready", 6 * i + 6)
        quads(act, "conv", conv)
        act.wait_ge(S["gate_r"], 2)
        act.wait_ge(S["conv_kept"], 4)
        act.activation(gf[:, :], gz[:, :], ACT.Exp, bias=gm[:, 0:1]).then_inc(S["gate_a"], 1)
        act.activation(gt[:, :], gF[:, :], ACT.Exp, scale=-1.0).then_inc(S["gate_em"], 1)
        act.activation(gw, gi[:, :], ACT.Exp, bias=gz[:, P - 1:P]).then_inc(S["gate_ws"], 1)
        copy_kind("qk")
        copy_kind("v")
        copy_kind("o")
        gated_kind("z")
        gated_kind("zx")
        for s in range(RING):
            act.wait_ge(S[f"stored{s}"], ring_value("zx", 0, s) + 16 * (ng["zx"] // RING))

    @block.vector
    def _(dve):
        split(dve, 0, 0)
        split(dve, 1, BASE["gate"][1], P)
        split_next(dve, "gate", 0)
        gates = Chain(dve, S["gate_step"])
        gates.step(dve.memset(gi[:, :], MASKED))
        gates.step(dve.memset(gf[:, :], 0.0))
        gates.step(dve.memset(gz[:, :], 0.0))
        dve.wait_ge(S["gate_loaded"], 16 * 20)
        gates.sync()
        dve.scalar_tensor_tensor(gt[:, :], gf[:, :], -1.0, gf[:, :], ALU.mult, ALU.max).then_inc(S["gate_abs"], 1)
        dve.wait_ge(S["gate_log"], 1)
        gates.step(dve.scalar_tensor_tensor(gf[:, :], gf[:, :], 0.0, gt[:, :], ALU.min, ALU.subtract))
        gates.sync()
        gates.step(dve.memset(gf[H * NT:R96, DT:P], 0.0))
        gates.sync()
        gates.step(dve.tensor_tensor_scan(gF[:, :], gf[:, :], gz[:, :], 0.0, ALU.add, ALU.add))
        gates.sync()
        gates.step(dve.tensor_tensor(gi[:, :], gi[:, :], gF[:, :], ALU.subtract))
        gates.sync()
        dve.tensor_tensor_scan(gt[:, :], gi[:, :], gz[:, :], -3.0e38, ALU.max, ALU.add).then_inc(S["gate_scanned"], 1)
        dve.wait_ge(S["last_loaded"], 32)
        gates.step(dve.tensor_tensor_scan(mn[:, :], gl[:, :], fl[:, :], 0.0, ALU.max, ALU.add))
        gates.step(dve.memset(mprev[:, :], 0.0))
        gates.sync()
        dve.tensor_copy(mprev[:, 1:NT], mn[:, 0:NT - 1]).then_inc(S["m_ready"], 1)
        dve.wait_ge(S["m_loaded"], 16)
        gates.step(dve.tensor_scalar(gt[:, :], gt[:, :], gm[:, 0:1], None, ALU.max))
        gates.sync()
        dve.tensor_scalar(gz[:, :], gt[:, :], -1.0, None, ALU.mult).then_inc(S["gate_r"], 1)
        dve.tensor_tensor(gF[:, :], gF[:, :], gt[:, :], ALU.add).then_inc(S["gate_r"], 1)

        def conv(i):
            ch = Chain(dve, S["conv_step"], 42 * i)
            j = bass.ds(i, 1)
            for c, (at, m) in enumerate(CHUNKS):
                p, g = c % 2, 4 * c
                if c == 5:
                    split_next(dve, "conv", i)
                mp = min(m, T - at)
                u = ut[:, p, :]
                dve.wait_ge(S["conv_c_ready"], 6 * i + c + 1)
                dve.wait_ge(S["summed"], BASE["conv"][1] + 24 * i + g + 3)
                ch.step(dve.tensor_tensor(u[:, 2:2 + mp], cs[:, p, 0:mp], bank[(g + 2) % 8][:, 0:mp], ALU.mult))
                if c == 0:
                    ch.step(dve.memset(u[:, 0:2], 0.0))
                else:
                    ch.step(dve.tensor_copy(u[:, 0:2], ut[:, 1 - p, 384:386]))
                if m > mp:
                    ch.step(dve.tensor_tensor(us[:, :, 2:2 + DT], cs[:, p, mp:m].rearrange("p (b t) -> p b t", b=DB),
                                              bank[(g + 2) % 8][:, mp:m].rearrange("p (b t) -> p b t", b=DB), ALU.mult))
                    ch.step(dve.tensor_copy(us[:, :, 0:2], cst[:, j].rearrange("p a b w -> p (a b) w")))
                dve.wait_ge(S["conv_t_ready"], 6 * i + c + 1)
                ch.step(dve.scalar_tensor_tensor(sil[:, 0:m], th[:, p, 0:m], 1.0, bank[(g + 3) % 8][:, 0:m],
                                                 ALU.add, ALU.mult))
                ch.sync()
                y = yc[:, 0:mp]
                ys = yc[:, P:P + TS].rearrange("p (b t) -> p b t", b=DB)
                for tap in range(3):
                    wt = cw[:, tap, j]
                    if tap:
                        ch.step(dve.scalar_tensor_tensor(y, u[:, tap:tap + mp], wt, y, ALU.mult, ALU.add))
                    else:
                        ch.step(dve.tensor_scalar(y, u[:, 0:mp], wt, cb[:, j], ALU.mult, ALU.add))
                    if m > mp:
                        if tap:
                            ch.step(dve.scalar_tensor_tensor(ys, us[:, :, tap:tap + DT], wt, ys, ALU.mult, ALU.add))
                        else:
                            ch.step(dve.tensor_scalar(ys, us[:, :, 0:DT], wt, cb[:, j], ALU.mult, ALU.add))
                    ch.sync()
                dve.scalar_tensor_tensor(yc[:, 0:m], yc[:, 0:m], 0.5, bank[g % 8][:, 0:m],
                                         ALU.mult, ALU.mult).then_inc(S["bank_free"], 4)
                dve.wait_ge(S["bank_free"], BASE["conv"][1] + 24 * i + g + 4)
                wait(dve, S[f"stored{c % RING}"], ring_value("conv", i, c))
                dve.tensor_tensor(stage[:, c % RING, 0:m], yc[:, 0:m], sil[:, 0:m],
                                  ALU.mult).then_inc(S["conv_y_ready"], 1)
                if c < 5:
                    dve.wait_ge(S["conv_y_ready"], 6 * i + c + 1)
            ch.step(dve.tensor_copy(cnew_p[:, j, :].rearrange("p a w -> p (a w)"), ut[:, 1, P:P + 2]))
            dve.tensor_copy(cnew_s[:, j].rearrange("p a b w -> p (a b) w"), us[:, :, DT:DT + 2]).then_inc(S["conv_kept"], 1)
            dve.wait_ge(S["conv_y_ready"], 6 * i + 6)
            dve.wait_ge(S["conv_kept"], i + 1)
            ch.sync()
            assert ch.n == 42, ch.n
        quads(dve, "conv", conv)
        dve.wait_ge(S["gate_ws"], 1)
        dve.tensor_scalar(gw, gw, K_SCALE, None, ALU.mult).then_inc(S["gate_ws_scaled"], 1)
        for kind in ("qk", "v", "o"):
            quads(dve, kind, lambda i, kind=kind: split_next(dve, kind, i))

        def gate_by_silu(kind, i, g):
            G = ng[kind]
            n = (0 if kind == "z" else 2 * ng["z"]) + G * i + g
            m = 512 if kind == "z" else CHUNKS[g // 4][1]
            s = stage[:, g % RING, 0:m]
            dve.wait_ge(S["tanh_ready"], n + 1)
            r = dve.scalar_tensor_tensor(s, s, 1.0, bank[g % 8][:, 0:m], ALU.add, ALU.mult)
            r.then_inc(S["bank_free"], 1)
            if kind == "z":
                dve.wait_ge(S["bank_free"], BASE[kind][1] + G * i + g + 1)
                dve.tensor_tensor(s, s, ghb[:, bass.ds(512 * i, 512)], ALU.mult).then_inc(S["silu_ready"], 1)

        def z(i):
            for g in range(NT):
                gate_by_silu("z", i, g)
            split_next(dve, "z", i)
            gate_by_silu("z", i, NT)
        dve.wait_ge(S["gain_loaded"], 16)
        quads(dve, "z", z)
        for g in range(ng["zx"]):
            gate_by_silu("zx", 0, g)

    @block.gpsimd
    def _(pool):
        def by_head(src_or_dst, tile, rows):
            for h in range(H):
                d = src_or_dst[rows + h]
                yield tile[h * NT:(h + 1) * NT, :], d[0:T].rearrange("(c t) -> c t", t=P)
                r = H * NT + h * DB
                yield tile[r:r + DB, 0:DT], d[T:TT].rearrange("(b t) -> b t", t=DT)

        for s in range(RING):
            pool.wait_ge(S[f"stored{s}"], ring_value("conv", 0, s))
        pool.wait_ge(S["gate_step"], 3)
        for tile, row in ((gi, 0), (gf, H)):
            for part, d in by_head(w["gate"], tile, row):
                pool.dma_start(part, d).then_inc(S["gate_loaded"], 16)
        for h in range(H):
            r = H * NT + h * DB
            pool.dma_start(gm[r:r + DB, :], st_m[0, :, h:h + 1]).then_inc(S["gate_loaded"], 16)
        pool.wait_ge(S["gate_scanned"], 1)
        pool.dma_start(w["last"][0:1, :].rearrange("a r -> r a"), gF[0:H * NT, P - 1:P]).then_inc(S["last_stored"], 16)
        pool.dma_start(w["last"][1:2, :].rearrange("a r -> r a"), gt[0:H * NT, P - 1:P]).then_inc(S["last_stored"], 16)
        pool.wait_ge(S["last_stored"], 32)
        pool.dma_start(fl[:, :], w["last"][0].rearrange("(h c) -> h c", h=H)).then_inc(S["last_loaded"], 16)
        pool.dma_start(gl[:, :], w["last"][1].rearrange("(h c) -> h c", h=H)).then_inc(S["last_loaded"], 16)
        pool.wait_ge(S["m_ready"], 1)
        pool.dma_start(m_prompt.rearrange("a b h -> h (a b)"), mn[:, NT - 1:NT]).then_inc(S["m_stored"], 16)
        pool.dma_start(w["mprev"].rearrange("(h c) -> h c", h=H), mprev[:, :]).then_inc(S["mprev_stored"], 16)
        pool.wait_ge(S["mprev_stored"], 16)
        pool.dma_start(gm[0:H * NT, :], w["mprev"].rearrange("(r a) -> r a", a=1)).then_inc(S["m_loaded"], 16)
        pool.wait_ge(S["gate_r"], 2)
        n = 0
        for h in range(H):
            r = H * NT + h * DB
            pool.dma_start(m_sample[0, :, h:h + 1], gF[r:r + DB, DT - 1:DT]).then_inc(S["gate_stored"], 16)
            n += 1
        for name, tile, ready in (("negr", gz, "gate_r"), ("a", gf, "gate_a"), ("em", gt, "gate_em"),
                                  ("g", gi, "gate_scanned"), ("ws", gw, "gate_ws_scaled")):
            if name != "negr":
                pool.wait_ge(S[ready], 1)
            for part, d in by_head(w[name], tile, 0):
                pool.dma_start(d, part).then_inc(S["gate_stored"], 16)
                n += 1
            if name == "a":
                pool.dma_start(w["wc"].rearrange("(r a) -> r a", a=1), gf[:, P - 1:P]).then_inc(S["gate_stored"], 16)
                n += 1
        pool.wait_ge(S["m_stored"], 16)
        pool.wait_ge(S["gate_stored"], 16 * n)

    ctx.close()


def mix(nc, S, sb, bank, w, ident, mv_prompt, C_prompt, n_prompt):
    qk = sb("qk", [P, 2, 16, P])
    tm = sb("tm", [P, 2, 6, 512])
    xa = sb("xa", [P, 2, 8, P])
    br = sb("br", [P, 2, 2, H, P])
    gc = sb("gc", [P, H, NT])
    wsc = sb("wsc", [P, H, NT])
    emc = sb("emc", [P, H, NT])
    wcb = sb("wcb", [P, H * NT])
    mkT = sb("mkT2", [P, H, NM])
    mv = sb("mv", [P, NM // P, H * XD])
    mask = sb("mask", [P, P])
    half, share, eps = (sb(x, [P, H]) for x in ("half", "share", "eps"))
    ones = sb("ones", [P, 1])
    C = sb("C", [P, H, 2, HD])
    n = sb("n", [P, H, 2])
    nm = sb("nm", [P, H, P])
    W = sb("W", [P, H, P])
    sw = sb("sw", [P, H, P])
    qs = sb("qs", [P, 8, P])
    kw = sb("kw", [P, H, HD])
    yml = sb("yml", [P, 2, H, HD])
    yst = sb("yst", [P, 8, P])
    xst = sb("xst", [P, H, P])
    pr = sb("pr", [P, H, NM])
    pT = sb("pT", [P, H, 2, P])
    mx, nb, sums, rsum, den, rden, ssq, msq, rinv, coef = (
        sb(x, [P, H]) for x in ("mx", "nb", "sums", "rsum", "den", "rden", "ssq", "msq", "rinv", "coef"))
    junk = sb("junk", [P, HD])
    ctx = ExitStack()
    block = ctx.enter_context(nc.Block())
    LOADS = 5

    def loaded(t, p):
        return 16 * LOADS // 2 * (t - p) + 16 * LOADS

    def col(t):
        return bass.ds(t * P, P)

    @block.sync
    def _(sp):
        for tile, name in ((gc, "g"), (wsc, "ws"), (emc, "em")):
            for h in range(H):
                sp.dma_start(tile[:, h, :], w[name][h, 0:T].rearrange("(c t) -> t c", t=P)).then_inc(S["columns_loaded"], 16)
        sp.dma_start(wcb[:, :], row_bcast(w["wc"][0:H * NT], P)).then_inc(S["columns_loaded"], 16)
        sp.dma_start(mkT[:, :, :], w["mkT"]).then_inc(S["columns_loaded"], 16)
        sp.dma_start(mv[:, :, :], mv_prompt[0, 0].rearrange("(a s) h d -> s a (h d)", s=P)).then_inc(S["columns_loaded"], 16)

        def load(t, p):
            wait(sp, S["xa_ready"], t - 1)
            sem = S[f"tile_loaded{p}"]
            sp.dma_start(qk[:, p, :, :], w["qk"][:, :, col(t)].rearrange("f p t -> p f t")).then_inc(sem, 16)
            sp.dma_start(br[:, p, 0, :, :], w["negr"][:, col(t)].partition_broadcast(P)).then_inc(sem, 16)
            sp.dma_start(br[:, p, 1, :, :], w["a"][:, col(t)].partition_broadcast(P)).then_inc(sem, 16)
            sp.dma_start(xa[:, p, :, :], w["xa"][:, :, col(t)].rearrange("f p t -> p f t")).then_inc(sem, 16)
            sp.dma_start(tm[:, p, :, :], w["tm"][:, col(t), :].rearrange("a t n -> t a n")).then_inc(sem, 16)
        over_tiles(sp, NT, load)
        sp.wait_ge(S["n_updated"], 4 * NT)
        sp.dma_start(C_prompt[0, 0].rearrange("h (a p) e -> p h a e", p=P), C[:, :, :, :]).then_inc(S["state_stored"], 16)
        sp.dma_start(n_prompt[0, 0].rearrange("h (a p) -> p h a", p=P), n[:, :, :]).then_inc(S["state_stored"], 16)
        sp.wait_ge(S["state_stored"], 32)

    @block.gpsimd
    def _(pool):
        pool.memset(mask[:, :], 0.0).then_inc(S["mask_zero"], 1)
        pool.memset(half[:, :], -0.5).then_inc(S["mask_zero"], 1)
        pool.memset(share[:, :], 0.25 / HD).then_inc(S["mask_zero"], 1)
        pool.memset(eps[:, :], EPS).then_inc(S["mask_zero"], 1)
        pool.memset(ones[:, :], 1.0).then_inc(S["ones_ready"], 1)
        pool.memset(C[:, :, :, :], 0.0).then_inc(S["state_zero"], 1)
        pool.memset(n[:, :, :], 0.0).then_inc(S["state_zero"], 1)
        pool.wait_ge(S["mask_zero"], 4)
        pool.affine_select(out=mask[:, :], in_=mask[:, :], compare_op=ALU.is_ge, fill=MASKED, base=0,
                           pattern=[[1, P]], channel_multiplier=-1).then_inc(S["mask_ready"], 1)
        pool.wait_ge(S["mask_ready"], 1)

        def ahead(t, p):
            pool.wait_ge(S[f"tile_loaded{p}"], loaded(t, p))
            wait(pool, S["w_ready"], 4 * t)
            pool.tensor_tensor(nm[:, :, :], br[:, p, 0, :, :], mask[:, :].unsqueeze(1).broadcast_to([P, H, P]),
                               ALU.add).then_inc(S["nm_ready"], 1)
            wait(pool, S["num_summed"], 4 * t)
            for h in range(H):
                pool.tensor_tensor(qs[:, 2 * h:2 * h + 2, :], qk[:, p, 2 * h:2 * h + 2, :],
                                   br[:, p, 1, h, :].unsqueeze(1).broadcast_to([P, 2, P]),
                                   ALU.mult).then_inc(S["qs_ready"], 1)
        ahead(0, 0)

        def tile(t, p):
            if not (isinstance(t, int) and t == NT - 1):
                ahead(t + 1, 1 - p)
            pool.wait_ge(S["squares_ready"], 4 * t + 4)
            pool.tensor_tensor(rinv[:, :], ssq[:, :], share[:, :], ALU.mult).then_inc(S["msq_ready"], 1)
            pool.wait_ge(S["msq_ready"], 2 * t + 1)
            pool.tensor_tensor(msq[:, :], rinv[:, :], eps[:, :], ALU.add).then_inc(S["msq_ready"], 1)
            pool.wait_ge(S["msq_ready"], 2 * t + 2)
            pool.tensor_tensor(rinv[:, :], msq[:, :], half[:, :], ALU.pow).then_inc(S["rinv_ready"], 1)
        over_tiles(pool, NT, tile, last=2)

    @block.tensor
    def _(pe):
        pe.wait_ge(S["ones_ready"], 1)
        pe.wait_ge(S["state_zero"], 2)
        pe.wait_ge(S["columns_loaded"], 16 * 15)

        def turn_y(t, p):
            pe.wait_ge(S["y_ready"], 4 * t + 4)
            for i in range(8):
                m = pe.transpose(bank[2 + i // 4][:, (i % 4) * P:(i % 4 + 1) * P],
                                 yml[:, p, i // 2, (i % 2) * P:(i % 2 + 1) * P], ident[:, :])
            m.then_inc(S["y_turned"], 1)

        def tile(t, p):
            pe.wait_ge(S[f"tile_loaded{p}"], loaded(t, p))
            wait(pe, S["xa_ready"], t)
            for h in range(H):
                for d in range(2):
                    m = pe.matmul(bank[0][:, h * P:(h + 1) * P], qk[:, p, 8 + 2 * h + d, :], qk[:, p, 2 * h + d, :],
                                  start=(d == 0), stop=(d == 1))
            m.then_inc(S["st_summed"], 1)
            wait(pe, S["C_updated"], 4 * t)
            for i in range(8):
                m = pe.transpose(bank[(1, 4)[i // 4]][:, (i % 4) * P:(i % 4 + 1) * P], qk[:, p, 8 + i, :], ident[:, :])
                if i % 4 == 3:
                    m.then_inc(S["k_turned"], 1)
            wait(pe, S["pT_ready"], 2 * t)
            for h in range(H):
                m = pe.matmul(bank[6 + h // 2][:, (h % 2) * NM:(h % 2 + 1) * NM], xa[:, p, h, :], mkT[:, h, :],
                              start=True, stop=True)
                if h % 2:
                    m.then_inc(S["scores_summed"], 1)
            if not (isinstance(t, int) and t == 0):
                turn_y(t - 1, 1 - p)
            wait(pe, S["yT_ready"], 2 * t)
            wait(pe, S["den_read"], t)
            pe.wait_ge(S["sw_ready"], t + 1)
            wait(pe, S["n_updated"], 4 * t)
            for h in range(H):
                num, dn = bank[2 + h // 2][:, (h % 2) * HD:(h % 2 + 1) * HD], bank[5][:, h:h + 1]
                pe.wait_ge(S["qs_ready"], 4 * t + h + 1)
                for d in range(2):
                    pe.matmul(num, qs[:, 2 * h + d, :], C[:, h, d, :], start=(d == 0), stop=False)
                    pe.matmul(dn, qs[:, 2 * h + d, :], n[:, h, d:d + 1], start=(d == 0), stop=False)
                pe.matmul(dn, sw[:, h, :], ones[:, :], start=False, stop=True)
                pe.matmul(num, sw[:, h, :], tm[:, p, h // 2, (h % 2) * HD:(h % 2 + 1) * HD], start=False,
                          stop=True).then_inc(S["num_summed"], 1)
            for h in range(H):
                pe.wait_ge(S["kw_ready"], 4 * t + (4 if h == 0 else h + 1))
                wait(pe, S["C_updated"], 4 * t + h - 1)
                for d in range(2):
                    k_d = kw[:, h, d * P:(d + 1) * P]
                    pe.matmul(bank[0][:, 2 * h + d:2 * h + d + 1], k_d, ones[:, :], start=True, stop=True)
                    m = pe.matmul(bank[(4, 1)[h % 2]][:, d * HD:(d + 1) * HD], k_d,
                                  tm[:, p, h // 2, (h % 2) * HD:(h % 2 + 1) * HD], start=True, stop=True)
                m.then_inc(S["dC_summed"], 1)
            for h in range(H):
                pe.wait_ge(S["p_ready"], 4 * t + h + 1)
                if h == 0:
                    pe.wait_ge(S["exp_ready"], 4 * t + 4)
                for s in range(2):
                    m = pe.transpose(bank[6 + h // 2][:, (h % 2) * NM + s * P:(h % 2) * NM + (s + 1) * P],
                                     pr[:, h, s * P:(s + 1) * P], ident[:, :])
                if h % 2:
                    m.then_inc(S["p_turned"], 1)
            pe.wait_ge(S["n_updated"], 4 * t + 4)
            for h in range(H):
                pe.wait_ge(S["pT_ready"], 2 * t + h // 2 + 1)
                for s in range(2):
                    m = pe.matmul(bank[0][:, h * P:(h + 1) * P], mv[:, s, h * XD:(h + 1) * XD], pT[:, h, s, :],
                                  start=(s == 0), stop=(s == 1))
            m.then_inc(S["pv_summed"], 1)
        over_tiles(pe, NT, tile)
        turn_y(NT - 1, 1)

    @block.scalar
    def _(act):
        act.wait_ge(S["columns_loaded"], 16 * 15)

        def y_out(t):
            for i in range(2):
                act.wait_ge(S["y_turned"], t + 1)
                if i == 0:
                    wait(act, S["y_stored"], 16 * t)
                act.activation(yst[:, 4 * i:4 * i + 4, :], bank[2 + i].ap().rearrange("p (f t) -> p f t", f=4),
                               ACT.Copy).then_inc(S["yT_ready"], 1)
            act.wait_ge(S["yT_ready"], 2 * t + 2)
            act.dma_start(w["yt"][0:8, :, col(t)].rearrange("f p t -> p f t"), yst[:, :, :]).then_inc(S["y_stored"], 16)

        def x_out(t):
            act.wait_ge(S["xa_ready"], t + 1)
            act.dma_start(w["yt"][12:16, :, col(t)].rearrange("f p t -> p f t"), xst[:, :, :]).then_inc(S["xa_stored"], 16)

        def tile(t, p):
            act.wait_ge(S["nm_ready"], t + 1)
            wait(act, S["sw_ready"], t)
            for h in range(H):
                act.activation(W[:, h, :], nm[:, h, :], ACT.Exp, bias=gc[:, h, bass.ds(t, 1)]).then_inc(S["w_ready"], 1)
            wait(act, S["dC_summed"], 4 * t)
            for h in range(H):
                act.wait_ge(S["k_turned"], 2 * t + h // 2 + 1)
                act.activation(kw[:, h, :], bank[(1, 4)[h // 2]][:, (h % 2) * HD:(h % 2 + 1) * HD], ACT.Copy,
                               scale=wsc[:, h, bass.ds(t, 1)]).then_inc(S["kw_ready"], 1)
            act.wait_ge(S["nb_ready"], t + 1)
            wait(act, S["p_turned"], 2 * t)
            for h in range(H):
                act.activation(pr[:, h, :], bank[6 + h // 2][:, (h % 2) * NM:(h % 2 + 1) * NM], ACT.Exp,
                               bias=nb[:, h:h + 1], scale=XA_SCALE, accum_out=sums[:, h:h + 1]).then_inc(S["exp_ready"], 1)
            if not (isinstance(t, int) and t == 0):
                y_out(t - 1)
                x_out(t - 1)
            act.wait_ge(S["t1_ready"], 2 * t + 2)
            wait(act, S["msq_ready"], 2 * t)
            for h in range(H):
                wait(act, S["squares_ready"], 4 * t + h)
                act.activation(junk[:, :], tm[:, p, 2 + h // 2, (h % 2) * HD:(h % 2 + 1) * HD], ACT.Square,
                               scale=rden[:, h:h + 1], accum_out=ssq[:, h:h + 1]).then_inc(S["squares_ready"], 1)
            for i in range(2):
                act.wait_ge(S["p_turned"], 2 * t + i + 1)
                wait(act, S["pv_summed"], t)
                act.activation(pT[:, 2 * i:2 * i + 2, :, :],
                               bank[6 + i].ap().rearrange("p (h s t) -> p h s t", h=2, s=2), ACT.Copy).then_inc(S["pT_ready"], 1)
        over_tiles(act, NT, tile)
        y_out(NT - 1)
        x_out(NT - 1)
        act.wait_ge(S["y_stored"], 16 * NT)
        act.wait_ge(S["xa_stored"], 16 * NT)

    @block.vector
    def _(dve):
        dve.wait_ge(S["columns_loaded"], 16 * 15)
        dve.wait_ge(S["state_zero"], 2)
        STEPS = 7

        def tile(t, p):
            ch = Chain(dve, S["mix_step"], STEPS * t)
            dve.wait_ge(S["w_ready"], 4 * t + 4)
            dve.wait_ge(S["st_summed"], t + 1)
            wait(dve, S["num_summed"], 4 * t)
            dve.scalar_tensor_tensor(sw[:, :, :], bank[0].ap().rearrange("p (h t) -> p h t", h=H), K_SCALE, W[:, :, :],
                                     ALU.mult, ALU.mult).then_inc(S["sw_ready"], 1)
            for i in range(2):
                dve.wait_ge(S["scores_summed"], 2 * t + i + 1)
                ch.step(dve.tensor_reduce(mx[:, 2 * i:2 * i + 2], bank[6 + i].ap().rearrange("p (h s) -> p h s", h=2),
                                          AX.X, ALU.max))
            ch.sync()
            wait(dve, S["exp_ready"], 4 * t)
            dve.tensor_scalar(nb[:, :], mx[:, :], -XA_SCALE, None, ALU.mult).then_inc(S["nb_ready"], 1)
            dve.wait_ge(S["num_summed"], 4 * t + 4)
            ch.step(dve.tensor_copy(den[:, :], bank[5][:, 0:H]))
            ch.sync()
            wait(dve, S["squares_ready"], 4 * t)
            ch.step(dve.scalar_tensor_tensor(rden[:, :], den[:, :], -1.0, den[:, :], ALU.mult, ALU.max))
            ch.sync()
            ch.step(dve.tensor_tensor(den[:, :], rden[:, :], emc[:, :, bass.ds(t, 1)].rearrange("p h a -> p (h a)"),
                                      ALU.max))
            ch.sync()
            dve.reciprocal(rden[:, :], den[:, :]).then_inc(S["den_read"], 1)
            for i in range(2):
                th = tm[:, p, 2 + i, :]
                dve.scalar_tensor_tensor(th, th, 1.0, bank[2 + i][:, :], ALU.add, ALU.mult).then_inc(S["t1_ready"], 1)
            dve.wait_ge(S["exp_ready"], 4 * t + 4)
            ch.step(dve.reciprocal(rsum[:, :], sums[:, :]))
            ch.sync()
            for h in range(H):
                dve.tensor_scalar(pr[:, h, :], pr[:, h, :], rsum[:, h:h + 1], None, ALU.mult).then_inc(S["p_ready"], 1)
            for h in range(H):
                keep = wcb[:, bass.ds(h * NT + t, 1)]
                dve.wait_ge(S["dC_summed"], 4 * t + h + 1)
                c_h = C[:, h, :, :].rearrange("p d e -> p (d e)")
                dve.scalar_tensor_tensor(c_h, c_h, keep, bank[(4, 1)[h % 2]][:, :], ALU.mult,
                                         ALU.add).then_inc(S["C_updated"], 1)
            for h in range(H):
                dve.scalar_tensor_tensor(n[:, h, :], n[:, h, :], wcb[:, bass.ds(h * NT + t, 1)],
                                         bank[0][:, 2 * h:2 * h + 2], ALU.mult, ALU.add).then_inc(S["n_updated"], 1)
            dve.wait_ge(S["rinv_ready"], t + 1)
            ch.step(dve.scalar_tensor_tensor(coef[:, :], rden[:, :], 0.25, rinv[:, :], ALU.mult, ALU.mult))
            ch.sync()
            wait(dve, S["y_turned"], t - 1)
            for h in range(H):
                s = slice((h % 2) * HD, (h % 2 + 1) * HD)
                dve.wait_ge(S["t1_ready"], 2 * t + 2)
                dve.scalar_tensor_tensor(yml[:, p, h, :], tm[:, p, 2 + h // 2, s], coef[:, h:h + 1],
                                         tm[:, p, 4 + h // 2, s], ALU.mult, ALU.mult).then_inc(S["y_ready"], 1)
            dve.wait_ge(S["pv_summed"], t + 1)
            wait(dve, S["xa_stored"], 16 * t)
            dve.scalar_tensor_tensor(xst[:, :, :], bank[0].ap().rearrange("p (h t) -> p h t", h=H), 0.5,
                                     xa[:, p, 4:8, :], ALU.mult, ALU.mult).then_inc(S["xa_ready"], 1)
            dve.wait_ge(S["y_ready"], 4 * t + 4)
            assert ch.n == STEPS, ch.n
        over_tiles(dve, NT, tile)

    ctx.close()


def sample(nc, S, sb, bank, w, ident, st_C, st_n, mem_k, mem_v, C_sample, n_sample):
    BW = TS + DT
    qk = sb("s_qk", [P, 16, TS])
    tm = sb("s_tm", [TS, 6, 512])
    xa = sb("s_xa", [P, 8, TS])
    nr = sb("s_nr", [TS, H, TS])
    ab = sb("s_ab", [P, H, TS])
    gc, wsc, emc = (sb(x, [TS, H]) for x in ("s_gc", "s_wsc", "s_emc"))
    wcb = sb("s_wcb", [P, H, DB])
    C = sb("s_C", [P, DB, H, 2, HD])
    nrow = sb("s_nrow", [DB * H, HD])
    n0 = sb("s_n0", [P, 2, DB, H])
    K = sb("s_K", [P, 2, 2, H * XD])
    V = sb("s_V", [P, DB, 2, H * XD])
    KT = sb("s_KT", [P, DB, H, NM])
    mask = sb("s_mask", [TS, DB, DT])
    own = sb("s_own", [TS, DB])
    ones = sb("s_ones", [TS, 1])
    half = sb("s_half", [TS, H])
    qm = sb("s_qm", [P, H, 2, DB * BW])
    qxm = sb("s_qxm", [P, H, DB * BW])
    sw = sb("s_sw", [TS, H, TS])
    kw = sb("s_kw", [TS, H * HD])
    kwm = sb("s_kwm", [TS, 2, H * HD])
    yst = qk[:, 0:8, :]
    xst = xa[:, 0:4, :]
    pr = sb("s_pr", [TS, H, NM])
    pT = sb("s_pT", [P, H, 2, TS])
    mx, nb, sums, rsum, den, den2, rden, ssq, msq, rinv, coef = (
        sb("s_" + x, [TS, H]) for x in ("mx", "nb", "sums", "rsum", "den", "den2", "rden", "ssq", "msq", "rinv", "coef"))
    junk = sb("s_junk", [TS, HD])
    ctx = ExitStack()
    block = ctx.enter_context(nc.Block())
    SMALL = 10

    def by_seq(ap):
        return ap.rearrange("p (b t) -> p b t", b=DB)

    def own_part(flat):
        return flat.rearrange("p (b x) -> p b x", x=BW)[:, :, 0:DT]

    @block.sync
    def _(sp):
        sp.dma_start(qk[:, :, :], w["qk"][:, :, T:TT].rearrange("f p t -> p f t")).then_inc(S["s_loaded"], 16)
        sp.dma_start(tm[:, :, :], w["tm"][:, T:TT, :].rearrange("a t n -> t a n")).then_inc(S["s_loaded"], 16)
        sp.dma_start(xa[:, :, :], w["xa"][:, :, T:TT].rearrange("f p t -> p f t")).then_inc(S["s_loaded"], 16)
        sp.dma_start(nr[:, :, :], w["negr"][:, T:TT].partition_broadcast(TS)).then_inc(S["s_loaded"], 16)
        sp.dma_start(ab[:, :, :], w["a"][:, T:TT].partition_broadcast(P)).then_inc(S["s_loaded"], 16)
        for tile, name in ((gc, "g"), (wsc, "ws"), (emc, "em")):
            sp.dma_start(tile[:, :], w[name][:, T:TT].rearrange("h t -> t h")).then_inc(S["s_loaded"], 16)
        sp.dma_start(wcb[:, :, :], w["wc"][H * NT:].rearrange("(h b) -> h b", h=H).partition_broadcast(P)).then_inc(S["s_loaded"], 16)
        sp.dma_start(nrow[:, :], st_n[0].rearrange("b h d -> (b h) d")).then_inc(S["s_loaded"], 16)
        for b in range(DB):
            wait(sp, S["s_K_turned"], b - 1)
            sp.dma_start(K[:, b % 2, :, :],
                         mem_k[0, b].rearrange("(a s) h d -> s a (h d)", s=P)).then_inc(S[f"s_K_loaded{b % 2}"], 16)
        for b in range(DB):
            sp.dma_start(C[:, b, :, :, :],
                         st_C[0, b].rearrange("h (a p) e -> p h a e", p=P)).then_inc(S["s_C_loaded"], 16)
        for b in range(DB):
            sp.dma_start(V[:, b, :, :], mem_v[0, b].rearrange("(a s) h d -> s a (h d)", s=P)).then_inc(S["s_V_loaded"], 16)
        for b in range(DB):
            sp.wait_ge(S["s_C_updated"], H * (b + 1))
            sp.dma_start(C_sample[0, b].rearrange("h (a p) e -> p h a e", p=P),
                         C[:, b, :, :, :]).then_inc(S["s_out"], 16)
        sp.wait_ge(S["s_n_ready"], 1)
        sp.dma_start(n_sample[0].rearrange("b h d -> (b h) d"), nrow[:, :]).then_inc(S["s_out"], 16)
        sp.wait_ge(S["s_y_out"], 1)
        sp.dma_start(w["yt"][0:8, :, T:TT].rearrange("f p t -> p f t"), yst[:, :, :]).then_inc(S["s_out"], 16)
        sp.wait_ge(S["s_x_out"], 1)
        sp.dma_start(w["yt"][12:16, :, T:TT].rearrange("f p t -> p f t"), xst[:, :, :]).then_inc(S["s_out"], 16)
        sp.wait_ge(S["s_out"], 16 * (DB + 3))

    @block.gpsimd
    def _(pool):
        pool.memset(mask[:, :, :], 0.0).then_inc(S["s_set"], 1)
        pool.memset(own[:, :], 1.0).then_inc(S["s_set"], 1)
        pool.memset(ones[:, :], 1.0).then_inc(S["s_set"], 1)
        pool.memset(half[:, :], -0.5).then_inc(S["s_set"], 1)
        pool.memset(qm[:, :, :, :], 0.0).then_inc(S["s_set"], 1)
        pool.memset(qxm[:, :, :], 0.0).then_inc(S["s_set"], 1)
        pool.wait_ge(S["s_set"], 6)
        pool.affine_select(out=mask[:, :, :], in_=mask[:, :, :], compare_op=ALU.is_ge, fill=MASKED, base=0,
                           pattern=[[DT, DB], [1, DT]], channel_multiplier=-1).then_inc(S["s_set"], 1)
        pool.affine_select(out=own[:, :], in_=own[:, :], compare_op=ALU.is_ge, fill=0.0, base=0,
                           pattern=[[-DT, DB]], channel_multiplier=1).then_inc(S["s_set"], 1)
        pool.wait_ge(S["s_set"], 8)
        pool.affine_select(out=mask[:, :, :], in_=mask[:, :, :], compare_op=ALU.is_ge, fill=MASKED, base=0,
                           pattern=[[-DT, DB], [0, DT]], channel_multiplier=1).then_inc(S["s_set"], 1)
        pool.affine_select(out=own[:, :], in_=own[:, :], compare_op=ALU.is_ge, fill=0.0, base=DT - 1,
                           pattern=[[DT, DB]], channel_multiplier=-1).then_inc(S["s_set"], 1)
        pool.wait_ge(S["s_squares"], H)
        pool.tensor_scalar(msq[:, :], ssq[:, :], 0.25 / HD, EPS, ALU.mult, ALU.add).then_inc(S["s_msq"], 1)
        pool.wait_ge(S["s_msq"], 1)
        pool.tensor_tensor(rinv[:, :], msq[:, :], half[:, :], ALU.pow).then_inc(S["s_rinv"], 1)

    @block.tensor
    def _(pe):
        pe.wait_ge(S["s_loaded"], 16 * SMALL)
        pe.wait_ge(S["s_set"], 10)
        for d in range(2):
            m = pe.transpose(bank[5][:, d * DB * H:(d + 1) * DB * H], nrow[:, d * P:(d + 1) * P], ident[:DB * H, :DB * H])
        m.then_inc(S["s_n_turned"], 1)
        for h in range(H):
            for d in range(2):
                m = pe.matmul(bank[0][:TS, h * TS:(h + 1) * TS], qk[:, 8 + 2 * h + d, :], qk[:, 2 * h + d, :],
                              start=(d == 0), stop=(d == 1))
        m.then_inc(S["s_st_summed"], 1)
        for i in range(8):
            m = pe.transpose(bank[(1, 4)[i // 4]][:TS, (i % 4) * P:(i % 4 + 1) * P], qk[:, 8 + i, :], ident[:, :])
        m.then_inc(S["s_k_turned"], 1)
        for b in range(DB):
            pe.wait_ge(S[f"s_K_loaded{b % 2}"], 16 * (b // 2 + 1))
            wait(pe, S["s_KT_ready0"], b - 1)
            wait(pe, S["s_KT_ready1"], b - 1)
            for h in range(H):
                for s in range(2):
                    m = pe.transpose(bank[((2, 6)[b % 2]) + h // 2][:, (h % 2) * NM + s * P:(h % 2) * NM + (s + 1) * P],
                                     K[:, b % 2, s, h * XD:(h + 1) * XD], ident[:, :])
            m.then_inc(S["s_K_turned"], 1)
        pe.wait_ge(S["s_KT_ready0"], DB)
        pe.wait_ge(S["s_KT_ready1"], DB)
        pe.wait_ge(S["s_q_masked"], 1)
        for h in range(H):
            for b in range(DB):
                m = pe.matmul(bank[6 + h // 2][:TS, (h % 2) * NM:(h % 2 + 1) * NM], qxm[:, h, b * TS:(b + 1) * TS],
                              KT[:, b, h, :], start=(b == 0), stop=(b == DB - 1))
            m.then_inc(S["s_scores"], 1)
        pe.wait_ge(S["s_sw_ready"], 1)
        pe.wait_ge(S["s_n_copied"], 1)
        pe.wait_ge(S["s_C_loaded"], 16 * DB)
        for h in range(H):
            num, dn = bank[2 + h // 2][:TS, (h % 2) * HD:(h % 2 + 1) * HD], bank[5][:TS, h:h + 1]
            for b in range(DB):
                for d in range(2):
                    q = qm[:, h, d, b * TS:(b + 1) * TS]
                    pe.matmul(num, q, C[:, b, h, d, :], start=(b + d == 0), stop=False)
                    pe.matmul(dn, q, n0[:, d, b, h:h + 1], start=(b + d == 0), stop=False)
            pe.matmul(dn, sw[:, h, :], ones[:, :], start=False, stop=True)
            m = pe.matmul(num, sw[:, h, :], tm[:, h // 2, (h % 2) * HD:(h % 2 + 1) * HD], start=False, stop=True)
        m.then_inc(S["s_num_summed"], 1)
        pe.wait_ge(S["s_p_ready"], 1)
        for h in range(H):
            for s in range(2):
                m = pe.transpose(bank[6][:, (2 * h + s) * TS:(2 * h + s + 1) * TS], pr[:, h, s * P:(s + 1) * P],
                                 ident[:TS, :TS])
        m.then_inc(S["s_p_turned"], 1)
        for b in range(DB):
            pe.wait_ge(S["s_kw_masked"], b + 1)
            for h in range(H):
                i = b * H + h
                wait(pe, S["s_C_updated"], i - 1)
                for d in range(2):
                    k_d = kwm[:, b % 2, h * HD + d * P:h * HD + (d + 1) * P]
                    pe.matmul(bank[0][:, d * DB * H + i:d * DB * H + i + 1], k_d, ones[:, :], start=True, stop=True)
                    m = pe.matmul(bank[(4, 1)[i % 2]][:, d * HD:(d + 1) * HD], k_d,
                                  tm[:, h // 2, (h % 2) * HD:(h % 2 + 1) * HD], start=True, stop=True)
                m.then_inc(S["s_dC_summed"], 1)
        pe.wait_ge(S["s_pT_ready"], 1)
        pe.wait_ge(S["s_V_loaded"], 16 * DB)
        for h in range(H):
            for b in range(DB):
                for s in range(2):
                    m = pe.matmul(bank[7][:, h * TS + b * DT:h * TS + (b + 1) * DT], V[:, b, s, h * XD:(h + 1) * XD],
                                  pT[:, h, s, b * DT:(b + 1) * DT], start=(s == 0), stop=(s == 1))
        m.then_inc(S["s_pv_summed"], 1)
        pe.wait_ge(S["s_y_ready"], 1)
        for i in range(8):
            m = pe.transpose(bank[2][:, i * TS:(i + 1) * TS], tm[:, 4 + i // 4, (i % 4) * P:(i % 4 + 1) * P], ident[:TS, :TS])
        m.then_inc(S["s_y_turned"], 1)
        pe.wait_ge(S["s_n_updated"], 1)
        for d in range(2):
            m = pe.transpose(bank[3][:DB * H, d * P:(d + 1) * P], n0[:, d].rearrange("p b h -> p (b h)"), ident[:, :])
        m.then_inc(S["s_n_back"], 1)

    @block.scalar
    def _(act):
        act.wait_ge(S["s_loaded"], 16 * SMALL)
        act.wait_ge(S["s_n_turned"], 1)
        act.activation(n0.ap().rearrange("p d b h -> p (d b h)"), bank[5][:, 0:2 * DB * H],
                       ACT.Copy).then_inc(S["s_n_copied"], 1)
        act.wait_ge(S["s_nm_ready"], 1)
        for h in range(H):
            act.activation(nr[:, h, :], nr[:, h, :], ACT.Exp, bias=gc[:, h:h + 1]).then_inc(S["s_w_ready"], 1)
        act.wait_ge(S["s_k_turned"], 1)
        for h in range(H):
            act.activation(kw[:, h * HD:(h + 1) * HD], bank[(1, 4)[h // 2]][:TS, (h % 2) * HD:(h % 2 + 1) * HD],
                           ACT.Copy, scale=wsc[:, h:h + 1]).then_inc(S["s_kw_ready"], 1)
        for b in range(DB):
            act.wait_ge(S["s_K_turned"], b + 1)
            act.activation(KT[:, b, 2:4, :], bank[(2, 6)[b % 2] + 1].ap().rearrange("p (h s) -> p h s", h=2),
                           ACT.Copy).then_inc(S["s_KT_ready1"], 1)
        act.wait_ge(S["s_nb_ready"], 1)
        for h in range(H):
            act.activation(pr[:, h, :], bank[6 + h // 2][:TS, (h % 2) * NM:(h % 2 + 1) * NM], ACT.Exp,
                           bias=nb[:, h:h + 1], scale=XA_SCALE, accum_out=sums[:, h:h + 1]).then_inc(S["s_exp_ready"], 1)
        act.wait_ge(S["s_t1_ready"], 2)
        for h in range(H):
            wait(act, S["s_squares"], h)
            act.activation(junk[:, :], tm[:, 2 + h // 2, (h % 2) * HD:(h % 2 + 1) * HD], ACT.Square,
                           scale=rden[:, h:h + 1], accum_out=ssq[:, h:h + 1]).then_inc(S["s_squares"], 1)
        act.wait_ge(S["s_p_turned"], 1)
        act.activation(pT.ap().rearrange("p h s t -> p (h s t)"), bank[6][:, :], ACT.Copy).then_inc(S["s_pT_ready"], 1)
        act.wait_ge(S["s_y_turned"], 1)
        act.activation(yst.rearrange("p f t -> p (f t)"), bank[2][:, :], ACT.Copy).then_inc(S["s_y_out"], 1)
        act.wait_ge(S["s_n_back"], 1)
        act.activation(nrow[:, :], bank[3][:DB * H, 0:HD], ACT.Copy).then_inc(S["s_n_ready"], 1)

    @block.vector
    def _(dve):
        dve.wait_ge(S["s_loaded"], 16 * SMALL)
        dve.wait_ge(S["s_set"], 10)
        ch = Chain(dve, S["s_step"])
        dve.tensor_tensor(nr[:, :, :], nr[:, :, :],
                          mask.ap().rearrange("p b t -> p (b t)").unsqueeze(1).broadcast_to([TS, H, TS]),
                          ALU.add).then_inc(S["s_nm_ready"], 1)
        for h in range(H):
            for d in range(2):
                ch.step(dve.tensor_tensor(own_part(qm[:, h, d, :]), by_seq(qk[:, 2 * h + d, :]), by_seq(ab[:, h, :]),
                                          ALU.mult))
        for h in range(H):
            ch.step(dve.tensor_copy(own_part(qxm[:, h, :]), by_seq(xa[:, h, :])))
        ch.sync()
        dve.tensor_copy(mx[:, :], gc[:, :]).then_inc(S["s_q_masked"], 1)
        dve.wait_ge(S["s_w_ready"], H)
        dve.wait_ge(S["s_st_summed"], 1)
        dve.scalar_tensor_tensor(sw[:, :, :], bank[0][:TS, 0:H * TS].rearrange("p (h t) -> p h t", h=H), K_SCALE,
                                 nr[:, :, :], ALU.mult, ALU.mult).then_inc(S["s_sw_ready"], 1)
        for b in range(DB):
            dve.wait_ge(S["s_K_turned"], b + 1)
            dve.tensor_copy(KT[:, b, 0:2, :], bank[(2, 6)[b % 2]].ap().rearrange("p (h s) -> p h s", h=2)).then_inc(S["s_KT_ready0"], 1)
        dve.wait_ge(S["s_q_masked"], 1)
        dve.wait_ge(S["s_scores"], H)
        for i in range(2):
            ch.step(dve.tensor_reduce(mx[:, 2 * i:2 * i + 2], bank[6 + i][:TS, :].rearrange("p (h s) -> p h s", h=2),
                                      AX.X, ALU.max))
        ch.sync()
        dve.tensor_scalar(nb[:, :], mx[:, :], -XA_SCALE, None, ALU.mult).then_inc(S["s_nb_ready"], 1)
        dve.wait_ge(S["s_exp_ready"], H)
        ch.step(dve.reciprocal(rsum[:, :], sums[:, :]))
        ch.sync()
        for h in range(H):
            ch.step(dve.tensor_scalar(pr[:, h, :], pr[:, h, :], rsum[:, h:h + 1], None, ALU.mult))
        ch.sync()
        dve.tensor_copy(mx[:, :], gc[:, :]).then_inc(S["s_p_ready"], 1)
        dve.wait_ge(S["s_num_summed"], 1)
        ch.step(dve.tensor_copy(den[:, :], bank[5][:TS, 0:H]))
        ch.sync()
        ch.step(dve.scalar_tensor_tensor(den2[:, :], den[:, :], -1.0, den[:, :], ALU.mult, ALU.max))
        ch.sync()
        ch.step(dve.tensor_tensor(den[:, :], den2[:, :], emc[:, :], ALU.max))
        ch.sync()
        ch.step(dve.reciprocal(rden[:, :], den[:, :]))
        ch.sync()
        for i in range(2):
            th = tm[:, 2 + i, :]
            dve.scalar_tensor_tensor(th, th, 1.0, bank[2 + i][:TS, :], ALU.add, ALU.mult).then_inc(S["s_t1_ready"], 1)
        dve.wait_ge(S["s_kw_ready"], H)

        def kw_mask(b):
            if b >= 2:
                dve.wait_ge(S["s_dC_summed"], H * (b - 1))
            dve.tensor_scalar(kwm[:, b % 2, :], kw[:, :], own[:, b:b + 1], None, ALU.mult).then_inc(S["s_kw_masked"], 1)

        kw_mask(0)
        for b in range(DB):
            if b + 1 < DB:
                kw_mask(b + 1)
            for h in range(H):
                dve.wait_ge(S["s_dC_summed"], b * H + h + 1)
                c = C[:, b, h, :, :].rearrange("p d e -> p (d e)")
                dve.scalar_tensor_tensor(c, c, wcb[:, h, b:b + 1], bank[(4, 1)[(b * H + h) % 2]][:, :], ALU.mult,
                                         ALU.add).then_inc(S["s_C_updated"], 1)
        keep = wcb.ap().rearrange("p h b -> p b h")
        for d in range(2):
            ch.step(dve.tensor_tensor(n0[:, d], n0[:, d], keep, ALU.mult))
        ch.sync()
        for d in range(2):
            ch.step(dve.tensor_tensor(n0[:, d], n0[:, d],
                                      bank[0][:, d * DB * H:(d + 1) * DB * H].rearrange("p (b h) -> p b h", b=DB), ALU.add))
        ch.sync()
        dve.tensor_copy(mx[:, :], gc[:, :]).then_inc(S["s_n_updated"], 1)
        dve.wait_ge(S["s_rinv"], 1)
        ch.step(dve.scalar_tensor_tensor(coef[:, :], rden[:, :], 0.25, rinv[:, :], ALU.mult, ALU.mult))
        ch.sync()
        dve.wait_ge(S["s_t1_ready"], 2)
        for h in range(H):
            s = slice((h % 2) * HD, (h % 2 + 1) * HD)
            ch.step(dve.scalar_tensor_tensor(tm[:, 4 + h // 2, s], tm[:, 2 + h // 2, s], coef[:, h:h + 1], tm[:, 4 + h // 2, s],
                                             ALU.mult, ALU.mult))
        ch.sync()
        dve.wait_ge(S["s_n_updated"], 1)
        dve.tensor_copy(mx[:, :], gc[:, :]).then_inc(S["s_y_ready"], 1)
        dve.wait_ge(S["s_pv_summed"], 1)
        dve.scalar_tensor_tensor(xst[:, :, :], bank[7][:, 0:H * TS].rearrange("p (h t) -> p h t", h=H), 0.5,
                                 xa[:, 4:8, :], ALU.mult, ALU.mult).then_inc(S["s_x_out"], 1)

    ctx.close()


def output(nc, S, sb, bank, w, w_out, x_prompt, x_sample, g_final, y_prompt, y_sample):
    KO = 16
    wh = sb("o_wh", [P, KO, D], F32R)
    wl = sb("o_wl", [P, KO, D], F32R)
    raw = sb("o_raw", [P, 4, D])
    yt = sb("o_yt", [P, 2, KO, P])
    yh = sb("o_yh", [P, KO, P], F32R)
    yl = sb("o_yl", [P, KO, P], F32R)
    x = sb("o_x", [P, 2, D])
    gf = sb("o_gf", [P, D])
    xsq = sb("o_xsq", [P, D])
    ss, ms, sd, rs = (sb("o_" + n, [P, NT + 1]) for n in ("ss", "ms", "sd", "rs"))
    NX = NT + 1
    ctx = ExitStack()
    block = ctx.enter_context(nc.Block())
    x_rows = x_prompt[0].rearrange("(t p) d -> t p d", p=P)
    y_rows = y_prompt[0].rearrange("(t p) d -> t p d", p=P)
    x_smp = x_sample.rearrange("b t d -> (b t) d")
    y_smp = y_sample.rearrange("b t d -> (b t) d")

    def last(t):
        return isinstance(t, int) and t == NT

    def at(t):
        return TT - P if last(t) else t * P

    def rows(ap, t):
        return ap[bass.ds(t, 1)].rearrange("a p d -> (a p) d")

    @block.sync
    def _(sp):
        sp.dma_start(gf[:, :], row_bcast(g_final, P)).then_inc(S["gf_loaded"], 16)

        def load(t, p):
            wait(sp, S["y_split"], 2 * (t - 1))
            sp.dma_start(yt[:, p, :, :], w["yt"][:, :, bass.ds(at(t), P)].rearrange("f p t -> p f t")).then_inc(S[f"yt_loaded{p}"], 16)
            wait(sp, S[f"y_out{p}"], 8 * (t - p))
            if last(t):
                sp.dma_start(x[TS:P, p, :], x_smp).then_inc(S[f"res_loaded{p}"], 16)
            else:
                sp.dma_start(x[:, p, :], rows(x_rows, t)).then_inc(S[f"res_loaded{p}"], 16)

        def weights(k):
            wait(sp, S["out_low_split"], k - 3)
            sp.dma_start(raw[:, k % 4, :], w_out[0, k * P:(k + 1) * P, :]).then_inc(S[f"wout_loaded{k % 4}"], 16)
        for k in range(4):
            weights(k)
        load(0, 0)
        for k in range(4, KO):
            weights(k)
        load(1, 1)
        with sp.Fori(1, NT // 2) as pair:
            load(2 * pair, 0)
            load(2 * pair + 1, 1)
        load(NT, 0)

    @block.tensor
    def _(pe):
        def tile(t, p):
            for k in range(KO):
                if isinstance(t, int) and t == 0:
                    pe.wait_ge(S["out_low_split"], k + 1)
                if k % 8 == 0:
                    pe.wait_ge(S["y_split"], 2 * t + k // 8 + 1)
                    if k == 0:
                        wait(pe, S["res_added"], 2 * (t - 1))
                for n in range(2):
                    out, c = bank[2 * p + n][:, :], slice(512 * n, 512 * (n + 1))
                    pe.matmul(out, yh[:, k, :], wh[:, k, c], start=(k == 0), stop=False)
                    pe.matmul(out, yh[:, k, :], wl[:, k, c], start=False, stop=False)
                    m = pe.matmul(out, yl[:, k, :], wh[:, k, c], start=False, stop=(k == KO - 1))
                if k % 8 == 7:
                    m.then_inc(S["y_half_used"], 1)
        over_tiles(pe, NX, tile)

    @block.scalar
    def _(act):
        def high(t, p):
            act.wait_ge(S[f"yt_loaded{p}"], 8 * (t - p) + 16)
            for i in range(2):
                wait(act, S["y_half_used"], 2 * (t - 1) + i + 1)
                s = slice(8 * i, 8 * i + 8)
                act.activation(yh[:, s, :], yt[:, p, s, :], ACT.Copy).then_inc(S["y_high"], 1)

        def norm(t, p):
            r = slice(TS if last(t) else 0, P)
            act.wait_ge(S["res_added"], 2 * t + 2)
            c = bass.ds(t, 1)
            act.activation(xsq[r, :], x[r, p, :], ACT.Square, accum_out=ss[r, c]).then_inc(S["out_squared"], 1)
            act.wait_ge(S["out_mean"], t + 1)
            act.activation(sd[r, c], ms[r, c], ACT.Sqrt).then_inc(S["out_std"], 1)

        def tile(t, p):
            if not last(t):
                high(t + 1, 1 - p)
            wait(act, S["out_squared"], t)
            norm(t, p)
            act.wait_ge(S["out_ready"], t + 1)
            dst = y_smp if last(t) else rows(y_rows, t)
            act.dma_start(dst, x[TS if last(t) else 0:P, p, :]).then_inc(S[f"y_out{p}"], 16)
        high(0, 0)
        over_tiles(act, NX, tile)
        act.wait_ge(S["y_out0"], 16 * 9)
        act.wait_ge(S["y_out1"], 16 * 8)

    @block.vector
    def _(dve):
        def low(t, p):
            for i in range(2):
                dve.wait_ge(S["y_high"], 2 * t + i + 1)
                s = slice(8 * i, 8 * i + 8)
                dve.tensor_tensor(yl[:, s, :], yt[:, p, s, :], yh[:, s, :].bitcast(F32), ALU.subtract).then_inc(S["y_split"], 1)

        def split(k):
            dve.wait_ge(S[f"wout_loaded{k % 4}"], 16 * (k // 4 + 1))
            dve.tensor_copy(wh[:, k, :], raw[:, k % 4, :]).then_inc(S["out_high_split"], 1)
            dve.wait_ge(S["out_high_split"], k + 1)
            dve.tensor_tensor(wl[:, k, :], raw[:, k % 4, :], wh[:, k, :].bitcast(F32),
                              ALU.subtract).then_inc(S["out_low_split"], 1)

        def tile(t, p):
            if not last(t):
                low(t + 1, 1 - p)
            r = slice(TS if last(t) else 0, P)
            c = bass.ds(t, 1)
            dve.wait_ge(S[f"res_loaded{p}"], 8 * (t - p) + 16)
            dve.wait_ge(S["y_half_used"], 2 * t + 2)
            for n in range(2):
                s = slice(512 * n, 512 * (n + 1))
                dve.tensor_tensor(x[r, p, s], x[r, p, s], bank[2 * p + n][r, :], ALU.add).then_inc(S["res_added"], 1)
            dve.wait_ge(S["out_squared"], t + 1)
            dve.tensor_scalar(ms[r, c], ss[r, c], 1.0 / D, EPS, ALU.mult, ALU.add).then_inc(S["out_mean"], 1)
            dve.wait_ge(S["out_std"], t + 1)
            dve.reciprocal(rs[r, c], sd[r, c]).then_inc(S["out_rstd"], 1)
            dve.wait_ge(S["out_rstd"], t + 1)
            dve.scalar_tensor_tensor(x[r, p, :], x[r, p, :], rs[r, c], gf[r, :], ALU.mult, ALU.mult).then_inc(S["out_ready"], 1)
        dve.wait_ge(S["gf_loaded"], 16)
        split(0)
        split(1)
        low(0, 0)
        for k in range(2, KO):
            split(k)
        over_tiles(dve, NX, tile)

    ctx.close()


_INS = ["x_prompt", "x_sample", "state_mlstm_C", "state_mlstm_n", "state_mlstm_m", "state_conv", "cache_mem_k",
        "cache_mem_v", "mem_prompt", "g_norm", "w_in", "b_if", "g_head", "conv_w", "conv_b", "g_mem", "w_mem_kv",
        "w_out", "g_final"]
_OUTS = [(1, T, D), (DB, DT, D), (1, 1, H, HD, HD), (1, 1, H, HD), (1, 1, H), (1, 1, 2, CC), (1, 1, NM, H, XD),
         (1, 1, NM, H, XD), (1, DB, H, HD, HD), (1, DB, H, HD), (1, DB, H), (1, DB, 2, CC)]


def kernel(**inputs):
    import numpy as np
    import concourse.bacc as bacc
    from concourse.bass_utils import run_bass_kernel_spmd

    arrays = {f"in_{n}": np.ascontiguousarray(inputs[n]) for n in _INS}
    nc = bacc.Bacc("TRN2", target_bir_lowering=False, num_devices=1)
    args = [nc.dram_tensor(n, a.shape, F32, kind="ExternalInput").ap() for n, a in arrays.items()]
    args += [nc.dram_tensor(f"out_{i}", s, F32, kind="ExternalOutput").ap() for i, s in enumerate(_OUTS)]
    layer(nc, *args)
    r = run_bass_kernel_spmd(nc, [arrays], core_ids=[0])
    return tuple(r.results[0][f"out_{i}"] for i in range(len(_OUTS)))
```

```python
from contextlib import ExitStack

import concourse.bass as bass
from concourse import mybir

F32 = mybir.dt.float32
F32R = mybir.dt.float32r
ALU = mybir.AluOpType
ACT = mybir.ActivationFunctionType
AX = mybir.AxisListType

P = 128
D = 1024
KD = D // P
T = 2048
DB, DT = 8, 8
TS = DB * DT
TT = T + TS
NT = T // P
H = 4
HD = 256
XD = 128
CC = 512
NM = 256
EPS = 1e-6
MASKED = -1e30
XA_SCALE = XD ** -0.5
K_SCALE = HD ** -0.5
COL_QK, COL_TM, COL_IF, COL_CV = 0, 2048, 5120, 5128
COL_XA = COL_CV + 4 * CC
CHUNKS = [(c * 384, 384) for c in range(5)] + [(1920, 192)]


class Semaphores:

    def __init__(self, nc):
        self.nc, self.made = nc, {}

    def __getitem__(self, name):
        if name not in self.made:
            self.made[name] = self.nc.alloc_semaphore(name)
        return self.made[name]

    def phase_done(self):
        self.nc.all_engine_barrier()
        self.nc.clear_and_free_semaphores(list(self.made.values()))
        self.nc.all_engine_barrier()
        self.made = {}


def wait(eng, sem, value):
    if isinstance(value, int) and value <= 0:
        return
    eng.wait_ge(sem, value)


def over_tiles(eng, n, body, last=0):
    body(0, 0)
    body(1, 1)
    pairs = (n - last) // 2
    with eng.Fori(1, pairs) as pair:
        body(2 * pair, 0)
        body(2 * pair + 1, 1)
    for t in range(2 * pairs, n):
        body(t, t % 2)


def layer(nc, x_prompt, x_sample, st_C, st_n, st_m, st_conv, mem_k, mem_v, mem_prompt,
          g_norm, w_in, b_if, g_head, conv_w, conv_b, g_mem, w_mem_kv, w_out, g_final,
          y_prompt, y_sample, C_prompt, n_prompt, m_prompt, conv_prompt, mk_prompt, mv_prompt,
          C_sample, n_sample, m_sample, conv_sample, upto=9):
    ctx = ExitStack()
    with ctx:
        S = Semaphores(nc)
        ctx.enter_context(nc.allow_non_contiguous_dma(reason="small states and gates change their layout"))

        def dram(name, shape):
            return nc.dram_tensor(name, shape, F32, kind="Internal").ap()

        def sb(c, name, shape, dt=F32):
            return c.enter_context(nc.sbuf_tensor(name, shape, dt))

        w = dict(
            qk=dram("scr_qk", (16, P, TT)), xa=dram("scr_xa", (8, P, TT)), tm=dram("scr_tm", (6, TT, 512)),
            yt=dram("scr_yt", (16, P, TT)), gate=dram("scr_gate", (8, TT)), negr=dram("scr_negr", (H, TT)),
            a=dram("scr_a", (H, TT)), g=dram("scr_g", (H, TT)), ws=dram("scr_ws", (H, TT)),
            em=dram("scr_em", (H, TT)), last=dram("scr_last", (2, H * NT)), mprev=dram("scr_mprev", (H * NT,)),
            mkT=dram("scr_mkT", (P, H, NM)),
            wc=dram("scr_wc", (H * NT + H * DB,)))
        bank = [ctx.enter_context(nc.psum_tensor(f"bank{i}", [P, 512], F32)) for i in range(8)]
        ident = sb(ctx, "ident", [P, P])

        with ExitStack() as c01:
            xh = sb(c01, "xh", [P, KD, TT], F32R)
            xl = sb(c01, "xl", [P, KD, TT], F32R)
            raw = sb(c01, "raw", [P, KD, 512])
            with ExitStack() as c:
                prep(nc, S, lambda *a: sb(c, *a), bank, ident, w, xh, xl, raw, x_prompt, x_sample,
                     g_norm, mem_prompt, g_mem, w_mem_kv, w_in, mk_prompt, mv_prompt)
            if upto >= 1:
                with ExitStack() as c:
                    project(nc, S, lambda *a: sb(c, *a), bank, w, xh, xl, raw, w_in, b_if, g_head, conv_w, conv_b,
                            st_conv, st_m, conv_prompt, conv_sample, m_prompt, m_sample)
        S.phase_done()
        if upto >= 2:
            with ExitStack() as c:
                mix(nc, S, lambda *a: sb(c, *a), bank, w, ident, mv_prompt, C_prompt, n_prompt)
        S.phase_done()
        if upto >= 3:
            with ExitStack() as c:
                sample(nc, S, lambda *a: sb(c, *a), bank, w, ident, st_C, st_n, mem_k, mem_v, C_sample, n_sample)
        S.phase_done()
        if upto >= 4:
            with ExitStack() as c:
                output(nc, S, lambda *a: sb(c, *a), bank, w, w_out, x_prompt, x_sample, g_final, y_prompt, y_sample)


def row_bcast(v, n):
    return v.partition_broadcast(n)


def prep(nc, S, sb, bank, ident, w, xh, xl, raw, x_prompt, x_sample, g_norm, mem_prompt, g_mem,
         w_mem_kv, w_in, mk_prompt, mv_prompt):
    NR = NT + 3
    SLOTS = 4
    wkv = sb("wkv", [P, 2, D])
    xin = sb("xin", [P, SLOTS, D])
    gx = sb("gx", [P, D])
    gm = sb("gm", [P, D])
    sq = sb("sq", [P, D])
    ss = sb("ss", [P, NR])
    sd = sb("sd", [P, NR])
    rs = sb("rs", [P, NR])
    eps = sb("p_eps", [P, 1])
    memT = sb("memT", [P, KD, NM])
    mkT = sb("mkT", [P, H, NM])
    kvs = sb("kvs", [P, 4, 512])
    MEM_HALVES = [min(max(u - 3, 0) * 9 // 8, 2 * KD) for u in range(NR + 1)]
    x_rows = x_prompt[0].rearrange("(t p) d -> t p d", p=P)
    x_smp = x_sample.rearrange("b t d -> (b t) d")
    mem_rows = mem_prompt[0].rearrange("(t p) d -> t p d", p=P)
    ctx = ExitStack()
    block = ctx.enter_context(nc.Block())

    def known(u):
        return isinstance(u, int)

    def rows(u):
        return TS if known(u) and u == NR - 1 else P

    def of_memory(u):
        return known(u) and u < 2

    def every(eng, body):
        for u in range(SLOTS):
            body(u, u)
        with eng.Fori(1, NR // SLOTS) as turn:
            for p in range(SLOTS):
                body(SLOTS * turn + p, p)
        for u in range(NR // SLOTS * SLOTS, NR):
            body(u, u % SLOTS)

    @block.sync
    def _(sp):
        def load(u, p):
            n = rows(u)
            wait(sp, S["x_turned"], u - SLOTS + 1)
            if of_memory(u):
                src = mem_rows[u]
            elif known(u) and u == NR - 1:
                src = x_smp
            else:
                src = x_rows[bass.ds(u - 2, 1)].rearrange("a p d -> (a p) d")
            sp.dma_start(xin[:n, p, :], src).then_inc(S[f"x_loaded{p}"], 16)
            if known(u) and u == 0:
                sp.dma_start(gm[:, :], row_bcast(g_mem[0], P)).then_inc(S["g_loaded"], 16)
            if known(u) and u == 1:
                sp.dma_start(gx[:, :], row_bcast(g_norm[0], P)).then_inc(S["g_loaded"], 16)
        every(sp, load)
        for k in range(KD):
            sp.dma_start(raw[:, k, :], weights_ap(w_in, KINDS[0][0], 0, k)).then_inc(S[f"raw_loaded{k}"], 16)

    @block.gpsimd
    def _(pool):
        pool.memset(eps[:, :], EPS).then_inc(S["eps_ready"], 1)
        pool.memset(ident[:, :], 0.0).then_inc(S["ident_zero"], 1)
        pool.wait_ge(S["ident_zero"], 1)
        pool.affine_select(out=ident[:, :], in_=ident[:, :], compare_op=ALU.not_equal, fill=1.0, base=0,
                           pattern=[[-1, P]], channel_multiplier=1).then_inc(S["ident_ready"], 1)
        for k in range(KD):
            wait(pool, S["wkv_used"], k - 1)
            pool.dma_start(wkv[:, k % 2, :], w_mem_kv[0, k * P:(k + 1) * P, :]).then_inc(S[f"wkv_loaded{k % 2}"], 16)

    @block.scalar
    def _(act):
        act.wait_ge(S["eps_ready"], 1)

        def square(u, p):
            n, c = rows(u), bass.ds(u, 1)
            act.wait_ge(S[f"x_loaded{p}"], 4 * (u - p) + 16)
            wait(act, S["squared"], u)
            act.activation(sq[:n, :], xin[:n, p, :], ACT.Square, accum_out=ss[:n, c]).then_inc(S["squared"], 1)
            act.wait_ge(S["squared"], u + 1)
            act.activation(sd[:n, c], ss[:n, c], ACT.Sqrt, scale=1.0 / D, bias=eps[:n, :]).then_inc(S["std_ready"], 1)

        def high(u, q):
            n = rows(u)
            act.wait_ge(S["x_turned"], u + 1)
            for half in range(2):
                dst = memT[:, 4 * half:4 * half + 4, u * P:(u + 1) * P] if of_memory(u) else \
                    xh[:, 4 * half:4 * half + 4, bass.ds((u - 2) * P, n)]
                src = bank[2 * q + half].ap().rearrange("p (k n) -> p k n", k=4)[:, :, 0:n]
                act.activation(dst, src, ACT.Copy).then_inc(S["high_ready"], 1)

        def stage(u, p):
            square(u, p)
            if not (known(u) and u < 2):
                high(u - 2, p % 2)
        every(act, stage)
        high(NR - 2, (NR - 2) % 2)
        act.wait_ge(S["wkv_used"], KD)
        for i in range(4):
            act.activation(kvs[:, i, :], bank[4 + i][:, :], ACT.Copy).then_inc(S["kv_copied"], 1)
        high(NR - 1, (NR - 1) % 2)
        for i in range(4):
            act.wait_ge(S["kv_copied"], i + 1)
            st, kv = i // 2, i % 2
            dst = (mk_prompt, mv_prompt)[kv][0, 0].rearrange("s h d -> s (h d)")[st * P:(st + 1) * P, :]
            act.dma_start(dst, kvs[:, i, :]).then_inc(S["kv_stored"], 16)
        for st in range(2):
            act.wait_ge(S["key_turned"], st + 1)
            act.activation(mkT[:, :, st * P:(st + 1) * P], bank[4 + st].ap().rearrange("p (h s) -> p h s", h=H),
                           ACT.Copy).then_inc(S["mkT_ready"], 1)
        act.wait_ge(S["mkT_ready"], 2)
        act.dma_start(w["mkT"], mkT[:, :, :]).then_inc(S["kv_stored"], 16)
        act.wait_ge(S["kv_stored"], 80)

    @block.vector
    def _(dve):
        dve.wait_ge(S["g_loaded"], 32)

        def norm(u, p):
            n, c = rows(u), bass.ds(u, 1)
            dve.wait_ge(S["std_ready"], u + 1)
            dve.reciprocal(rs[:n, c], sd[:n, c]).then_inc(S["rstd_ready"], 1)
            dve.wait_ge(S["rstd_ready"], u + 1)
            g = gm if of_memory(u) else gx
            dve.scalar_tensor_tensor(xin[:n, p, :], xin[:n, p, :], rs[:n, c], g[:n, :],
                                     ALU.mult, ALU.mult).then_inc(S["x_normed"], 1)

        def low(u, q):
            n = rows(u)
            for half in range(2):
                dve.wait_ge(S["high_ready"], 2 * u + half + 1)
                src = bank[2 * q + half].ap().rearrange("p (k n) -> p k n", k=4)[:, :, 0:n]
                at = bass.ds((u - 2) * P, n)
                dve.tensor_tensor(xl[:, 4 * half:4 * half + 4, at], src,
                                  xh[:, 4 * half:4 * half + 4, at].bitcast(F32), ALU.subtract).then_inc(S["low_ready"], 1)

        def stage(u, p):
            norm(u, p)
            if not (known(u) and u < 4):
                low(u - 2, p % 2)
        every(dve, stage)
        for u in (NR - 2, NR - 1):
            low(u, u % 2)

    @block.tensor
    def _(pe):
        pe.wait_ge(S["ident_ready"], 1)
        for u in range(NR):
            n, q = rows(u), u % 2
            pe.wait_ge(S["x_normed"], u + 1)
            if u in (2, 3):
                pe.wait_ge(S["high_ready"], 2 * (u - 1))
            if u >= 4:
                pe.wait_ge(S["low_ready"], 2 * (u - 3))
            for k in range(KD):
                m = pe.transpose(bank[2 * q + k // 4][:, (k % 4) * P:(k % 4) * P + n],
                                 xin[:n, u % SLOTS, k * P:(k + 1) * P], ident[:n, :n])
            m.then_inc(S["x_turned"], 1)
            for half in range(MEM_HALVES[u], MEM_HALVES[u + 1]):
                k, st = half // 2, half % 2
                if half == 0:
                    pe.wait_ge(S["high_ready"], 4)
                pe.wait_ge(S[f"wkv_loaded{k % 2}"], 16 * (k // 2 + 1))
                for kv in range(2):
                    m = pe.matmul(bank[4 + 2 * st + kv][:, :], memT[:, k, st * P:(st + 1) * P],
                                  wkv[:, k % 2, kv * 512:(kv + 1) * 512], start=(k == 0), stop=(k == KD - 1))
                if st:
                    m.then_inc(S["wkv_used"], 1)
        for st in range(2):
            pe.wait_ge(S["kv_copied"], 2 * st + 1)
            for h in range(H):
                m = pe.transpose(bank[4 + st][:, h * P:(h + 1) * P], kvs[:, 2 * st, h * P:(h + 1) * P], ident[:, :])
            m.then_inc(S["key_turned"], 1)

    ctx.close()


KINDS = [("qx", 1, 24), ("gate", 1, 6), ("conv", 4, 24), ("qk", 4, 24), ("v", 2, 17), ("o", 2, 17), ("z", 2, 17),
         ("zx", 1, 24)]
BANKS = {24: [g % 8 for g in range(24)], 17: [7, 0, 1, 2, 3, 4, 7, 5, 6, 0, 1, 2, 7, 3, 4, 5, 6], 6: list(range(6))}
RING = 4


def weights_ap(w_in, kind, i, k):
    rows = w_in[0, k * P:(k + 1) * P, :]
    if kind == "gate":
        return rows[:, COL_IF:COL_IF + P]
    if kind == "conv":
        return rows[:, COL_CV:COL_CV + 4 * CC].rearrange("p (a c) -> p a c", a=4)[:, :, bass.ds(i * P, P)]
    col = {"qk": COL_QK, "v": COL_TM, "o": COL_TM + D, "z": COL_TM + 2 * D, "qx": COL_XA,
           "zx": COL_XA + 512}[kind]
    return rows[:, bass.ds(col + 512 * i, 512)]


def kind_bases():
    quads, groups, stored, out = 0, 0, [0] * RING, {}
    for kind, n, g in KINDS:
        out[kind] = (quads, groups, list(stored))
        quads, groups = quads + n, groups + n * g
        results = 6 if kind == "conv" else g
        for s in range(RING):
            stored[s] += n * len(range(s, results, RING))
    return out


def bank_user(kind, g):
    order, back = BANKS[dict((k, x) for k, _, x in KINDS)[kind]], []
    kinds = [k for k, _, _ in KINDS]
    if order[g] in order[:g]:
        return g - max(x for x in range(g) if order[x] == order[g])
    before = [kind] if dict((k, x) for k, x, _ in KINDS)[kind] > 1 else []
    before += kinds[kinds.index(kind) - 1:kinds.index(kind)] if kinds.index(kind) else []
    for other in before:
        last = BANKS[dict((k, x) for k, _, x in KINDS)[other]]
        if order[g] in last:
            back.append(g + len(last) - max(x for x in range(len(last)) if last[x] == order[g]))
        else:
            back.append(g + 1)
    return min(back) if back else None


BASE = kind_bases()


def ring_value(kind, i, g):
    results = 6 if kind == "conv" else dict((k, x) for k, _, x in KINDS)[kind]
    s = g % RING
    return 16 * (BASE[kind][2][s] + g // RING) + 16 * len(range(s, results, RING)) * i


class Chain:

    def __init__(self, eng, sem, base=0):
        self.eng, self.sem, self.base, self.n = eng, sem, base, 0

    def step(self, instruction):
        instruction.then_inc(self.sem, 1)
        self.n += 1

    def sync(self):
        wait(self.eng, self.sem, self.base + self.n)


def project(nc, S, sb, bank, w, xh, xl, raw, w_in, b_if, g_head, conv_w, conv_b, st_conv, st_m,
            conv_prompt, conv_sample, m_prompt, m_sample):
    wh = sb("wh", [P, KD, 512], F32R)
    wl = sb("wl", [P, KD, 512], F32R)
    stage = sb("stage", [P, RING, 512])
    work = sb("work", [P, 1920])
    cw = sb("cw", [P, 3, 4])
    cb = sb("cb", [P, 4])
    cst = sb("cst", [P, 4, DB, 2])
    cnew_p = sb("cnew_p", [P, 4, 2])
    cnew_s = sb("cnew_s", [P, 4, DB, 2])
    bif = sb("bif", [8, 1])
    R96 = H * NT + H * DB
    gi, gf, gF, gt = (sb(n, [R96, P]) for n in ("gi", "gf", "gF", "gt"))
    gz = sb("gz", [R96, P])
    gw = work[0:R96, D:D + P]
    gm = sb("gm1", [R96, 1])
    fl, gl, mn, mprev = (sb(n, [H, NT]) for n in ("fl", "gl", "mn", "mprev"))
    cs = work[:, 0:768].rearrange("p (s n) -> p s n", s=2)
    th = work[:, 768:1536].rearrange("p (s n) -> p s n", s=2)
    ut = sb("ut", [P, 2, 386])
    us = sb("us", [P, DB, 10])
    yc = sb("yc", [P, 384])
    sil = work[:, 1536:1920]
    ghb = work[:, 0:D]
    TMK = {"v": 0, "o": 2, "z": 4}
    ng = {k: g for k, _, g in KINDS}
    ctx = ExitStack()
    block = ctx.enter_context(nc.Block())

    def quads(eng, kind, body):
        n = dict((k, x) for k, x, _ in KINDS)[kind]
        if n == 1:
            body(0)
        else:
            with eng.Fori(0, n) as i:
                body(i)

    @block.sync
    def _(sp):
        sp.dma_start(bif[:, :], b_if[0].rearrange("(a b) -> a b", b=1)).then_inc(S["small_loaded"], 16)
        for j in range(3):
            sp.dma_start(cw[:, j, :], conv_w[0, j].rearrange("(j p) -> p j", p=P)).then_inc(S["small_loaded"], 16)
        sp.dma_start(cb[:, :], conv_b[0].rearrange("(j p) -> p j", p=P)).then_inc(S["small_loaded"], 16)
        for j in range(4):
            sp.dma_start(cst[:, j, :, :],
                         st_conv[0, :, :, j * P:(j + 1) * P].rearrange("b w p -> p b w")).then_inc(S["small_loaded"], 16)
        for kind, n, _ in KINDS:
            if kind == "v":
                sp.wait_ge(S["conv_kept"], 4)
                sp.dma_start(ghb, row_bcast(g_head[0], P)).then_inc(S["gain_loaded"], 16)

            def load(i, kind=kind):
                q = BASE[kind][0] + i
                for k in range(KD):
                    wait(sp, S["low_split"], 8 * (q - 1) + k + 1)
                    dst = raw[:, k, :]
                    if kind == "gate":
                        dst = raw[:, k, 0:P]
                    if kind == "conv":
                        dst = dst.rearrange("p (a c) -> p a c", a=4)
                    sp.dma_start(dst, weights_ap(w_in, kind, i, k)).then_inc(S[f"raw_loaded{k}"], 16)
            if kind != KINDS[0][0]:
                quads(sp, kind, load)
        sp.wait_ge(S["conv_kept"], 4)
        for j in range(4):
            sp.dma_start(conv_prompt[0, 0, :, j * P:(j + 1) * P].rearrange("w p -> p w"),
                         cnew_p[:, j, :]).then_inc(S["conv_state_stored"], 16)
            sp.dma_start(conv_sample[0, :, :, j * P:(j + 1) * P].rearrange("b w p -> p b w"),
                         cnew_s[:, j, :, :]).then_inc(S["conv_state_stored"], 16)
        sp.wait_ge(S["conv_state_stored"], 8 * 16)

    def split(dve, q, groups, cols=512):
        def low(k):
            dve.wait_ge(S["high_split"], 8 * q + k + 1)
            dve.tensor_tensor(wl[:, k, 0:cols], raw[:, k, 0:cols], wh[:, k, 0:cols].bitcast(F32),
                              ALU.subtract).then_inc(S["low_split"], 1)
        for k in range(KD):
            dve.wait_ge(S[f"raw_loaded{k}"], 16 * (q + 1))
            if k < KD - 1:
                wait(dve, S["weights_used"], 7 * (q - 1) + k + 1)
            else:
                wait(dve, S["summed"], groups)
            dve.tensor_copy(wh[:, k, 0:cols], raw[:, k, 0:cols]).then_inc(S["high_split"], 1)
            if k:
                low(k - 1)
        low(KD - 1)

    def split_next(dve, kind, i):
        split(dve, BASE[kind][0] + i + 1, BASE[kind][1] + ng[kind] * (i + 1))

    @block.tensor
    def _(pe):
        for kind, n, G in KINDS:
            def quad(i, kind=kind, G=G):
                q, g0 = BASE[kind][0] + i, BASE[kind][1] + G * i
                for g in range(G):
                    back = bank_user(kind, g)
                    if back is not None:
                        pe.wait_ge(S["bank_free"], g0 + g + 1 - back)
                    for k in range(KD):
                        if g == 0:
                            pe.wait_ge(S["low_split"], 8 * q + k + 1)
                        if kind in ("v", "o", "z"):
                            at = min(g * P, TT - P)
                            out = bank[BANKS[G][g]][:, :]
                            ah, al = xh[:, k, at:at + P], xl[:, k, at:at + P]
                            bh, bl = wh[:, k, :], wl[:, k, :]
                        else:
                            (at, m), j = (CHUNKS[g], 0) if kind == "gate" else (CHUNKS[g // 4], g % 4)
                            out = bank[BANKS[G][g]][:, 0:m]
                            ah, al = wh[:, k, j * P:(j + 1) * P], wl[:, k, j * P:(j + 1) * P]
                            bh, bl = xh[:, k, at:at + m], xl[:, k, at:at + m]
                        pe.matmul(out, ah, bh, start=(k == 0), stop=False)
                        pe.matmul(out, ah, bl, start=False, stop=False)
                        mm = pe.matmul(out, al, bh, start=False, stop=(k == KD - 1))
                        if g == G - 1 and k < KD - 1:
                            mm.then_inc(S["weights_used"], 1)
                    mm.then_inc(S["summed"], 1)
            quads(pe, kind, quad)

    def result(kind, i, g):
        s = g % RING
        if kind in ("v", "o", "z"):
            quad = w["tm"][bass.ds(TMK[kind] + i, 1)].rearrange("a t n -> (a t) n")
            if g < NT:
                return stage[:, s, :], quad[g * P:(g + 1) * P, :]
            return stage[P - TS:, s, :], quad[T:TT, :]
        if kind == "gate":
            at, m = CHUNKS[g]
            return stage[0:8, s, 0:m], w["gate"][:, at:at + m]
        if kind == "conv":
            at, m = CHUNKS[g]
            rows = w["yt"][bass.ds(8 + i, 1)]
        else:
            at, m = CHUNKS[g // 4]
            to, b = {"qk": (w["qk"], 4 * i), "qx": (w["xa"], 0), "zx": (w["xa"], 4)}[kind]
            rows = to[bass.ds(b + g % 4, 1)]
        return stage[:, s, 0:m], rows.rearrange("a p t -> (a p) t")[:, at:at + m]

    @block.scalar
    def _(act):
        def store(kind, i, g, ready, value):
            act.wait_ge(S[ready], value)
            src, dst = result(kind, i, g)
            act.dma_start(dst, src).then_inc(S[f"stored{g % RING}"], 16)

        def copy_kind(kind):
            def quad(i):
                G = ng[kind]
                g0 = BASE[kind][1] + G * i
                for g in range(G):
                    act.wait_ge(S["summed"], g0 + g + 1)
                    wait(act, S[f"stored{g % RING}"], ring_value(kind, i, g))
                    if kind == "gate":
                        m = CHUNKS[g][1]
                        act.activation(stage[0:8, g % RING, 0:m], bank[BANKS[G][g]][0:8, 0:m], ACT.Identity,
                                       bias=bif[:, 0:1]).then_inc(S["bank_free"], 1)
                    elif kind == "o":
                        act.activation(stage[:, g % RING, :], bank[BANKS[G][g]][:, :], ACT.Tanh,
                                       scale=0.5).then_inc(S["bank_free"], 1)
                    else:
                        m = 512 if kind == "v" else CHUNKS[g // 4][1]
                        act.activation(stage[:, g % RING, 0:m], bank[BANKS[G][g]][:, 0:m],
                                       ACT.Copy).then_inc(S["bank_free"], 1)
                    if g:
                        store(kind, i, g - 1, "bank_free", g0 + g)
                store(kind, i, G - 1, "bank_free", g0 + G)
            quads(act, kind, quad)

        def gated_kind(kind):
            def quad(i):
                G = ng[kind]
                g0 = BASE[kind][1] + G * i
                ready, c0 = ("silu_ready", G * i) if kind == "z" else ("bank_free", g0)
                for g in range(G):
                    act.wait_ge(S["summed"], g0 + g + 1)
                    wait(act, S[f"stored{g % RING}"], ring_value(kind, i, g))
                    m = 512 if kind == "z" else CHUNKS[g // 4][1]
                    act.activation(stage[:, g % RING, 0:m], bank[BANKS[G][g]][:, 0:m], ACT.Tanh,
                                   scale=0.5).then_inc(S["tanh_ready"], 1)
                    if g:
                        store(kind, i, g - 1, ready, c0 + g)
                store(kind, i, G - 1, ready, c0 + G)
            quads(act, kind, quad)

        act.wait_ge(S["small_loaded"], 16 * 9)
        copy_kind("qx")
        copy_kind("gate")
        def conv(i):
            g0 = BASE["conv"][1] + 24 * i
            for c, (at, m) in enumerate(CHUNKS):
                g = 4 * c
                act.wait_ge(S["summed"], g0 + g + 2)
                act.wait_ge(S["bank_free"], g0 + g - 4)
                act.activation(cs[:, c % 2, 0:m], bank[(g + 1) % 8][:, 0:m], ACT.Copy).then_inc(S["conv_c_ready"], 1)
                act.wait_ge(S["summed"], g0 + g + 4)
                act.activation(th[:, c % 2, 0:m], bank[(g + 3) % 8][:, 0:m], ACT.Tanh,
                               scale=0.5).then_inc(S["conv_t_ready"], 1)
                if c:
                    store("conv", i, c - 1, "conv_y_ready", 6 * i + c)
            store("conv", i, 5, "conv_y_ready", 6 * i + 6)
        quads(act, "conv", conv)
        act.wait_ge(S["gate_abs"], 1)
        act.activation(gt[:, :], gt[:, :], ACT.Exp, scale=-1.0).then_inc(S["gate_exp"], 1)
        act.wait_ge(S["gate_exp"], 1)
        act.activation(gt[:, :], gt[:, :], ACT.Ln, bias=1.0).then_inc(S["gate_log"], 1)
        copy_kind("qk")
        act.wait_ge(S["gate_r"], 2)
        act.wait_ge(S["conv_kept"], 4)
        act.activation(gf[:, :], gz[:, :], ACT.Exp, bias=gm[:, 0:1]).then_inc(S["gate_a"], 1)
        act.activation(gt[:, :], gF[:, :], ACT.Exp, scale=-1.0).then_inc(S["gate_em"], 1)
        act.activation(gw, gi[:, :], ACT.Exp, bias=gz[:, P - 1:P]).then_inc(S["gate_ws"], 1)
        copy_kind("v")
        copy_kind("o")
        gated_kind("z")
        gated_kind("zx")
        for s in range(RING):
            act.wait_ge(S[f"stored{s}"], ring_value("zx", 0, s) + 16 * (ng["zx"] // RING))

    @block.vector
    def _(dve):
        split(dve, 0, 0)
        split(dve, 1, BASE["gate"][1], P)
        split_next(dve, "gate", 0)
        gates = Chain(dve, S["gate_step"])
        gates.step(dve.memset(gi[:, :], MASKED))
        gates.step(dve.memset(gf[:, :], 0.0))
        gates.step(dve.memset(gz[:, :], 0.0))

        def conv(i):
            ch = Chain(dve, S["conv_step"], 42 * i)
            j = bass.ds(i, 1)
            for c, (at, m) in enumerate(CHUNKS):
                p, g = c % 2, 4 * c
                if c == 5:
                    split_next(dve, "conv", i)
                mp = min(m, T - at)
                u = ut[:, p, :]
                dve.wait_ge(S["conv_c_ready"], 6 * i + c + 1)
                dve.wait_ge(S["summed"], BASE["conv"][1] + 24 * i + g + 3)
                ch.step(dve.tensor_tensor(u[:, 2:2 + mp], cs[:, p, 0:mp], bank[(g + 2) % 8][:, 0:mp], ALU.mult))
                if c == 0:
                    ch.step(dve.memset(u[:, 0:2], 0.0))
                else:
                    ch.step(dve.tensor_copy(u[:, 0:2], ut[:, 1 - p, 384:386]))
                if m > mp:
                    ch.step(dve.tensor_tensor(us[:, :, 2:2 + DT], cs[:, p, mp:m].rearrange("p (b t) -> p b t", b=DB),
                                              bank[(g + 2) % 8][:, mp:m].rearrange("p (b t) -> p b t", b=DB), ALU.mult))
                    ch.step(dve.tensor_copy(us[:, :, 0:2], cst[:, j].rearrange("p a b w -> p (a b) w")))
                dve.wait_ge(S["conv_t_ready"], 6 * i + c + 1)
                ch.step(dve.scalar_tensor_tensor(sil[:, 0:m], th[:, p, 0:m], 1.0, bank[(g + 3) % 8][:, 0:m],
                                                 ALU.add, ALU.mult))
                ch.sync()
                y = yc[:, 0:mp]
                ys = yc[:, P:P + TS].rearrange("p (b t) -> p b t", b=DB)
                for tap in range(3):
                    wt = cw[:, tap, j]
                    if tap:
                        ch.step(dve.scalar_tensor_tensor(y, u[:, tap:tap + mp], wt, y, ALU.mult, ALU.add))
                    else:
                        ch.step(dve.tensor_scalar(y, u[:, 0:mp], wt, cb[:, j], ALU.mult, ALU.add))
                    if m > mp:
                        if tap:
                            ch.step(dve.scalar_tensor_tensor(ys, us[:, :, tap:tap + DT], wt, ys, ALU.mult, ALU.add))
                        else:
                            ch.step(dve.tensor_scalar(ys, us[:, :, 0:DT], wt, cb[:, j], ALU.mult, ALU.add))
                    ch.sync()
                dve.scalar_tensor_tensor(yc[:, 0:m], yc[:, 0:m], 0.5, bank[g % 8][:, 0:m],
                                         ALU.mult, ALU.mult).then_inc(S["bank_free"], 4)
                dve.wait_ge(S["bank_free"], BASE["conv"][1] + 24 * i + g + 4)
                wait(dve, S[f"stored{c % RING}"], ring_value("conv", i, c))
                dve.tensor_tensor(stage[:, c % RING, 0:m], yc[:, 0:m], sil[:, 0:m],
                                  ALU.mult).then_inc(S["conv_y_ready"], 1)
                if c < 5:
                    dve.wait_ge(S["conv_y_ready"], 6 * i + c + 1)
            ch.step(dve.tensor_copy(cnew_p[:, j, :].rearrange("p a w -> p (a w)"), ut[:, 1, P:P + 2]))
            dve.tensor_copy(cnew_s[:, j].rearrange("p a b w -> p (a b) w"), us[:, :, DT:DT + 2]).then_inc(S["conv_kept"], 1)
            dve.wait_ge(S["conv_y_ready"], 6 * i + 6)
            dve.wait_ge(S["conv_kept"], i + 1)
            ch.sync()
            assert ch.n == 42, ch.n
        quads(dve, "conv", conv)
        dve.wait_ge(S["gate_loaded"], 16 * 20)
        gates.sync()
        dve.scalar_tensor_tensor(gt[:, :], gf[:, :], -1.0, gf[:, :], ALU.mult, ALU.max).then_inc(S["gate_abs"], 1)
        dve.wait_ge(S["gate_log"], 1)
        gates.step(dve.scalar_tensor_tensor(gf[:, :], gf[:, :], 0.0, gt[:, :], ALU.min, ALU.subtract))
        gates.sync()
        gates.step(dve.memset(gf[H * NT:R96, DT:P], 0.0))
        gates.sync()
        gates.step(dve.tensor_tensor_scan(gF[:, :], gf[:, :], gz[:, :], 0.0, ALU.add, ALU.add))
        gates.sync()
        gates.step(dve.tensor_tensor(gi[:, :], gi[:, :], gF[:, :], ALU.subtract))
        gates.sync()
        dve.tensor_tensor_scan(gt[:, :], gi[:, :], gz[:, :], -3.0e38, ALU.max, ALU.add).then_inc(S["gate_scanned"], 1)
        dve.wait_ge(S["last_loaded"], 32)
        gates.step(dve.tensor_tensor_scan(mn[:, :], gl[:, :], fl[:, :], 0.0, ALU.max, ALU.add))
        gates.step(dve.memset(mprev[:, :], 0.0))
        gates.sync()
        dve.tensor_copy(mprev[:, 1:NT], mn[:, 0:NT - 1]).then_inc(S["m_ready"], 1)
        dve.wait_ge(S["m_loaded"], 16)
        gates.step(dve.tensor_scalar(gt[:, :], gt[:, :], gm[:, 0:1], None, ALU.max))
        gates.sync()
        dve.tensor_scalar(gz[:, :], gt[:, :], -1.0, None, ALU.mult).then_inc(S["gate_r"], 1)
        dve.tensor_tensor(gF[:, :], gF[:, :], gt[:, :], ALU.add).then_inc(S["gate_r"], 1)
        for kind in ("qk", "v", "o"):
            quads(dve, kind, lambda i, kind=kind: split_next(dve, kind, i))
            if kind == "qk":
                dve.wait_ge(S["gate_ws"], 1)
                dve.tensor_scalar(gw, gw, K_SCALE, None, ALU.mult).then_inc(S["gate_ws_scaled"], 1)

        def gate_by_silu(kind, i, g):
            G = ng[kind]
            n = (0 if kind == "z" else 2 * ng["z"]) + G * i + g
            m = 512 if kind == "z" else CHUNKS[g // 4][1]
            s = stage[:, g % RING, 0:m]
            dve.wait_ge(S["tanh_ready"], n + 1)
            r = dve.scalar_tensor_tensor(s, s, 1.0, bank[BANKS[G][g]][:, 0:m], ALU.add, ALU.mult)
            r.then_inc(S["bank_free"], 1)
            if kind == "z":
                dve.wait_ge(S["bank_free"], BASE[kind][1] + G * i + g + 1)
                dve.tensor_tensor(s, s, ghb[:, bass.ds(512 * i, 512)], ALU.mult).then_inc(S["silu_ready"], 1)

        def z(i):
            for g in range(NT):
                gate_by_silu("z", i, g)
            split_next(dve, "z", i)
            gate_by_silu("z", i, NT)
        dve.wait_ge(S["gain_loaded"], 16)
        quads(dve, "z", z)
        for g in range(ng["zx"]):
            gate_by_silu("zx", 0, g)

    @block.gpsimd
    def _(pool):
        def by_head(src_or_dst, tile, rows):
            for h in range(H):
                d = src_or_dst[rows + h]
                yield tile[h * NT:(h + 1) * NT, :], d[0:T].rearrange("(c t) -> c t", t=P)
                r = H * NT + h * DB
                yield tile[r:r + DB, 0:DT], d[T:TT].rearrange("(b t) -> b t", t=DT)

        for s in range(RING):
            pool.wait_ge(S[f"stored{s}"], ring_value("conv", 0, s))
        pool.wait_ge(S["gate_step"], 3)
        for tile, row in ((gi, 0), (gf, H)):
            for part, d in by_head(w["gate"], tile, row):
                pool.dma_start(part, d).then_inc(S["gate_loaded"], 16)
        for h in range(H):
            r = H * NT + h * DB
            pool.dma_start(gm[r:r + DB, :], st_m[0, :, h:h + 1]).then_inc(S["gate_loaded"], 16)
        pool.wait_ge(S["gate_scanned"], 1)
        pool.dma_start(w["last"][0:1, :].rearrange("a r -> r a"), gF[0:H * NT, P - 1:P]).then_inc(S["last_stored"], 16)
        pool.dma_start(w["last"][1:2, :].rearrange("a r -> r a"), gt[0:H * NT, P - 1:P]).then_inc(S["last_stored"], 16)
        pool.wait_ge(S["last_stored"], 32)
        pool.dma_start(fl[:, :], w["last"][0].rearrange("(h c) -> h c", h=H)).then_inc(S["last_loaded"], 16)
        pool.dma_start(gl[:, :], w["last"][1].rearrange("(h c) -> h c", h=H)).then_inc(S["last_loaded"], 16)
        pool.wait_ge(S["m_ready"], 1)
        pool.dma_start(m_prompt.rearrange("a b h -> h (a b)"), mn[:, NT - 1:NT]).then_inc(S["m_stored"], 16)
        pool.dma_start(w["mprev"].rearrange("(h c) -> h c", h=H), mprev[:, :]).then_inc(S["mprev_stored"], 16)
        pool.wait_ge(S["mprev_stored"], 16)
        pool.dma_start(gm[0:H * NT, :], w["mprev"].rearrange("(r a) -> r a", a=1)).then_inc(S["m_loaded"], 16)
        pool.wait_ge(S["gate_r"], 2)
        n = 0
        for h in range(H):
            r = H * NT + h * DB
            pool.dma_start(m_sample[0, :, h:h + 1], gF[r:r + DB, DT - 1:DT]).then_inc(S["gate_stored"], 16)
            n += 1
        for name, tile, ready in (("negr", gz, "gate_r"), ("a", gf, "gate_a"), ("em", gt, "gate_em"),
                                  ("g", gi, "gate_scanned"), ("ws", gw, "gate_ws_scaled")):
            if name != "negr":
                pool.wait_ge(S[ready], 1)
            for part, d in by_head(w[name], tile, 0):
                pool.dma_start(d, part).then_inc(S["gate_stored"], 16)
                n += 1
            if name == "a":
                pool.dma_start(w["wc"].rearrange("(r a) -> r a", a=1), gf[:, P - 1:P]).then_inc(S["gate_stored"], 16)
                n += 1
        pool.wait_ge(S["m_stored"], 16)
        pool.wait_ge(S["gate_stored"], 16 * n)

    ctx.close()


def mix(nc, S, sb, bank, w, ident, mv_prompt, C_prompt, n_prompt):
    HE = HD + 1
    qk = sb("qk", [P, 2, 16, P])
    xq = sb("xq", [P, 2, H, P])
    br = sb("br", [P, 2, 2, H, P])
    v1 = sb("v1", [P, 2, H, HE])
    oz = sb("oz", [P, 2, 4, 512])
    xz = sb("xz", [P, 2, H, P])
    gc = sb("gc", [P, H, NT])
    wsc = sb("wsc", [P, H, NT])
    emc = sb("emc", [P, H, NT])
    wcb = sb("wcb", [P, H * NT])
    mkT = sb("mkT2", [P, H, NM])
    mv = sb("mv", [P, NM // P, H * XD])
    mask = sb("mask", [P, P])
    half, share, eps = (sb(x, [P, H]) for x in ("half", "share", "eps"))
    C = sb("C", [P, H, 2, HE])
    nm = sb("nm", [P, H, P])
    W = sb("W", [P, H, P])
    sw = sb("sw", [P, H, P])
    qs = sb("qs", [P, 8, P])
    kw = sb("kw", [P, H, HD])
    yml = sb("yml", [P, 2, H, HD])
    yst = sb("yst", [P, 8, P])
    xst = sb("xst", [P, H, P])
    pr = sb("pr", [P, H, NM])
    pT = sb("pT", [P, H, 2, P])
    mx, nb, sums, rsum, den, rden, ssq, msq, rinv, coef = (
        sb(x, [P, H]) for x in ("mx", "nb", "sums", "rsum", "den", "rden", "ssq", "msq", "rinv", "coef"))
    junk = sb("junk", [P, HD])
    ctx = ExitStack()
    block = ctx.enter_context(nc.Block())
    EARLY, LATE = 4, 6
    DC_BANKS = (5, 6, 7, 0)

    def early_loaded(t, p):
        return 8 * EARLY * (t - p) + 16 * EARLY

    def late_loaded(t, p):
        return 8 * LATE * (t - p) + 16 * LATE

    def col(t):
        return bass.ds(t * P, P)

    def is_last(t):
        return isinstance(t, int) and t == NT - 1

    def is_first(t):
        return isinstance(t, int) and t == 0

    @block.sync
    def _(sp):
        def early(t, p):
            sem = S[f"early_loaded{p}"]
            wait(sp, S["qs_ready"], 4 * (t - 1))
            wait(sp, S["st_summed"], t - 1)
            wait(sp, S["nm_ready"], t - 1)
            sp.dma_start(qk[:, p, :, :], w["qk"][:, :, col(t)].rearrange("f p t -> p f t")).then_inc(sem, 16)
            sp.dma_start(xq[:, p, :, :], w["xa"][0:H, :, col(t)].rearrange("f p t -> p f t")).then_inc(sem, 16)
            sp.dma_start(br[:, p, 0, :, :], w["negr"][:, col(t)].partition_broadcast(P)).then_inc(sem, 16)
            sp.dma_start(br[:, p, 1, :, :], w["a"][:, col(t)].partition_broadcast(P)).then_inc(sem, 16)

        def late(t, p):
            sem = S[f"late_loaded{p}"]
            wait(sp, S["dC_summed"], 8 * (t - 1))
            wait(sp, S["y_ready"], 4 * (t - 1))
            wait(sp, S["xa_ready"], t - 1)
            for a in range(2):
                sp.dma_start(v1[:, p, 2 * a:2 * a + 2, 0:HD],
                             w["tm"][a, col(t), :].rearrange("t (h e) -> t h e", h=2)).then_inc(sem, 16)
            for a in range(2):
                sp.dma_start(oz[:, p, 2 * a:2 * a + 2, :],
                             w["tm"][2 + 2 * a:4 + 2 * a, col(t), :].rearrange("a t n -> t a n")).then_inc(sem, 16)
            for a in range(2):
                sp.dma_start(xz[:, p, 2 * a:2 * a + 2, :],
                             w["xa"][H + 2 * a:H + 2 * a + 2, :, col(t)].rearrange("f p t -> p f t")).then_inc(sem, 16)

        early(0, 0)
        for tile, name in ((gc, "g"), (wsc, "ws"), (emc, "em")):
            for h in range(H):
                sp.dma_start(tile[:, h, :], w[name][h, 0:T].rearrange("(c t) -> t c", t=P)).then_inc(S["columns_loaded"], 16)
        sp.dma_start(wcb[:, :], row_bcast(w["wc"][0:H * NT], P)).then_inc(S["columns_loaded"], 16)
        sp.dma_start(mkT[:, :, :], w["mkT"]).then_inc(S["columns_loaded"], 16)
        sp.dma_start(mv[:, :, :], mv_prompt[0, 0].rearrange("(a s) h d -> s a (h d)", s=P)).then_inc(S["columns_loaded"], 16)
        early(1, 1)
        late(0, 0)
        late(1, 1)

        with sp.Fori(1, NT // 2) as pair:
            for p in range(2):
                early(2 * pair + p, p)
                late(2 * pair + p, p)
        sp.wait_ge(S["C_updated"], 8 * NT)
        sp.dma_start(C_prompt[0, 0].rearrange("h (a p) e -> p h a e", p=P), C[:, :, :, 0:HD]).then_inc(S["state_stored"], 16)
        sp.dma_start(n_prompt[0, 0].rearrange("h (a p) -> p h a", p=P), C[:, :, :, HD]).then_inc(S["state_stored"], 16)
        sp.wait_ge(S["state_stored"], 32)

    @block.gpsimd
    def _(pool):
        pool.memset(mask[:, :], 0.0).then_inc(S["mask_zero"], 1)
        pool.memset(half[:, :], -0.5).then_inc(S["mask_zero"], 1)
        pool.memset(share[:, :], 0.25 / HD).then_inc(S["mask_zero"], 1)
        pool.memset(eps[:, :], EPS).then_inc(S["mask_zero"], 1)
        for p in range(2):
            pool.memset(v1[:, p, :, HD:HE], 1.0).then_inc(S["ones_ready"], 1)
        pool.memset(C[:, :, :, :], 0.0).then_inc(S["state_zero"], 1)
        pool.wait_ge(S["mask_zero"], 4)
        pool.affine_select(out=mask[:, :], in_=mask[:, :], compare_op=ALU.is_ge, fill=MASKED, base=0,
                           pattern=[[1, P]], channel_multiplier=-1).then_inc(S["mask_ready"], 1)
        pool.wait_ge(S["mask_ready"], 1)

        def ahead(t, p):
            pool.wait_ge(S[f"early_loaded{p}"], early_loaded(t, p))
            wait(pool, S["w_ready"], 4 * t)
            pool.tensor_tensor(nm[:, :, :], br[:, p, 0, :, :], mask[:, :].unsqueeze(1).broadcast_to([P, H, P]),
                               ALU.add).then_inc(S["nm_ready"], 1)
            for h in range(H):
                wait(pool, S["num_summed"], 4 * (t - 1) + h + 1)
                pool.tensor_tensor(qs[:, 2 * h:2 * h + 2, :], qk[:, p, 2 * h:2 * h + 2, :],
                                   br[:, p, 1, h, :].unsqueeze(1).broadcast_to([P, 2, P]),
                                   ALU.mult).then_inc(S["qs_ready"], 1)
        ahead(0, 0)

        def tile(t, p):
            if not is_last(t):
                ahead(t + 1, 1 - p)
            pool.wait_ge(S["squares_ready"], 4 * t + 4)
            pool.tensor_tensor(rinv[:, :], ssq[:, :], share[:, :], ALU.mult).then_inc(S["msq_ready"], 1)
            pool.wait_ge(S["msq_ready"], 2 * t + 1)
            pool.tensor_tensor(msq[:, :], rinv[:, :], eps[:, :], ALU.add).then_inc(S["msq_ready"], 1)
            pool.wait_ge(S["msq_ready"], 2 * t + 2)
            pool.tensor_tensor(rinv[:, :], msq[:, :], half[:, :], ALU.pow).then_inc(S["rinv_ready"], 1)
        over_tiles(pool, NT, tile, last=2)

    @block.tensor
    def _(pe):
        pe.wait_ge(S["ones_ready"], 2)
        pe.wait_ge(S["state_zero"], 1)
        pe.wait_ge(S["columns_loaded"], 16 * 15)

        def turn_keys(t, p):
            pe.wait_ge(S[f"early_loaded{p}"], early_loaded(t, p))
            wait(pe, S["t1_ready"], 4 * (t - 1) + 2)
            wait(pe, S["den_ready"], t)
            for i in range(8):
                m = pe.transpose(bank[1 + i // 4][:, (i % 4) * P:(i % 4 + 1) * P], qk[:, p, 8 + i, :], ident[:, :])
                if i % 4 == 3:
                    m.then_inc(S["k_turned"], 1)

        def products(t, p):
            wait(pe, S["t1_ready"], 4 * t)
            for h in range(H):
                m = pe.matmul(bank[3 + h // 2][:, (h % 2) * NM:(h % 2 + 1) * NM], xq[:, p, h, :], mkT[:, h, :],
                              start=True, stop=True)
                if h % 2:
                    m.then_inc(S["scores_summed"], 1)
            wait(pe, S["yT_ready"], 2 * (t - 1))
            for h in range(H):
                for d in range(2):
                    m = pe.matmul(bank[0][:, h * P:(h + 1) * P], qk[:, p, 8 + 2 * h + d, :], qk[:, p, 2 * h + d, :],
                                  start=(d == 0), stop=(d == 1))
            m.then_inc(S["st_summed"], 1)

        def turn_y(t, p):
            pe.wait_ge(S["y_ready"], 4 * t + 4)
            pe.wait_ge(S["xa_ready"], t + 1)
            for i in range(8):
                m = pe.transpose(bank[(7, 0)[i // 4]][:, (i % 4) * P:(i % 4 + 1) * P],
                                 yml[:, p, i // 2, (i % 2) * P:(i % 2 + 1) * P], ident[:, :])
                if i % 4 == 3:
                    m.then_inc(S["y_turned"], 1)

        def tile(t, p):
            pe.wait_ge(S[f"late_loaded{p}"], late_loaded(t, p))
            pe.wait_ge(S["sw_ready"], t + 1)
            wait(pe, S["C_updated"], 8 * t)
            for h in range(H):
                if h < 2:
                    pe.wait_ge(S["kw_ready"], 4 * t + 2 * h + 2)
                else:
                    pe.wait_ge(S["exp_ready"], 4 * t + 2 * h - 2)
                pe.wait_ge(S["qs_ready"], 4 * t + h + 1)
                num = bank[1 + h][:, 0:HE]
                for d in range(2):
                    pe.matmul(num, qs[:, 2 * h + d, :], C[:, h, d, :], start=(d == 0), stop=False)
                pe.matmul(num, sw[:, h, :], v1[:, p, h, :], start=False, stop=True).then_inc(S["num_summed"], 1)
            wait(pe, S["pT_ready"], 2 * t)
            for j in range(8):
                h, d = j // 2, j % 2
                if j == 2:
                    wait(pe, S["xa_ready"], t)
                if j >= 4:
                    pe.wait_ge(S["C_updated"], 8 * t + j - 3)
                pe.matmul(bank[DC_BANKS[j % 4]][:, 0:HE], kw[:, h, d * P:(d + 1) * P], v1[:, p, h, :],
                          start=True, stop=True).then_inc(S["dC_summed"], 1)
            if not is_last(t):
                turn_keys(t + 1, 1 - p)
            pe.wait_ge(S["C_updated"], 8 * t + 8)
            if not is_first(t):
                turn_y(t - 1, 1 - p)
            pe.wait_ge(S["p_ready"], 4 * t + 4)
            for h in range(H):
                for s in range(2):
                    m = pe.transpose(bank[5 + h // 2][:, (h % 2) * NM + s * P:(h % 2) * NM + (s + 1) * P],
                                     pr[:, h, s * P:(s + 1) * P], ident[:, :])
                if h % 2:
                    m.then_inc(S["p_turned"], 1)
            if not is_last(t):
                products(t + 1, 1 - p)
            wait(pe, S["yT_ready"], 2 * t - 1)
            for h in range(H):
                pe.wait_ge(S["pT_ready"], 2 * t + h // 2 + 1)
                for s in range(2):
                    m = pe.matmul(bank[7][:, h * P:(h + 1) * P], mv[:, s, h * XD:(h + 1) * XD], pT[:, h, s, :],
                                  start=(s == 0), stop=(s == 1))
            m.then_inc(S["pv_summed"], 1)
        turn_keys(0, 0)
        products(0, 0)
        over_tiles(pe, NT, tile, last=2)
        pe.wait_ge(S["yT_ready"], 2 * (NT - 1))
        turn_y(NT - 1, 1)

    @block.scalar
    def _(act):
        act.wait_ge(S["columns_loaded"], 16 * 15)

        def weights(t, p):
            act.wait_ge(S["nm_ready"], t + 1)
            wait(act, S["sw_ready"], t)
            for h in range(H):
                act.activation(W[:, h, :], nm[:, h, :], ACT.Exp, bias=gc[:, h, bass.ds(t, 1)]).then_inc(S["w_ready"], 1)

        def keys(t, p):
            wait(act, S["dC_summed"], 8 * t)
            for h in range(H):
                act.wait_ge(S["k_turned"], 2 * t + h // 2 + 1)
                act.activation(kw[:, h, :], bank[1 + h // 2][:, (h % 2) * HD:(h % 2 + 1) * HD], ACT.Copy,
                               scale=wsc[:, h, bass.ds(t, 1)]).then_inc(S["kw_ready"], 1)

        def exps(t, p):
            act.wait_ge(S["nb_ready"], t + 1)
            wait(act, S["p_turned"], 2 * t)
            for h in range(H):
                act.activation(pr[:, h, :], bank[3 + h // 2][:, (h % 2) * NM:(h % 2 + 1) * NM], ACT.Exp,
                               bias=nb[:, h:h + 1], scale=XA_SCALE, accum_out=sums[:, h:h + 1]).then_inc(S["exp_ready"], 1)

        def y_out(t):
            for i in range(2):
                act.wait_ge(S["y_turned"], 2 * t + i + 1)
                if i == 0:
                    wait(act, S["y_stored"], 16 * t)
                act.activation(yst[:, 4 * i:4 * i + 4, :], bank[(7, 0)[i]].ap().rearrange("p (f t) -> p f t", f=4),
                               ACT.Copy).then_inc(S["yT_ready"], 1)
            act.wait_ge(S["yT_ready"], 2 * t + 2)
            act.dma_start(w["yt"][0:8, :, col(t)].rearrange("f p t -> p f t"), yst[:, :, :]).then_inc(S["y_stored"], 16)

        def x_out(t):
            act.wait_ge(S["xa_ready"], t + 1)
            act.dma_start(w["yt"][12:16, :, col(t)].rearrange("f p t -> p f t"), xst[:, :, :]).then_inc(S["xa_stored"], 16)

        def tile(t, p):
            if not is_last(t):
                weights(t + 1, 1 - p)
            wait(act, S["msq_ready"], 2 * t)
            act.wait_ge(S["den_ready"], t + 1)
            for h in range(H):
                act.wait_ge(S["t1_ready"], 4 * t + h + 1)
                wait(act, S["squares_ready"], 4 * t + h)
                act.activation(junk[:, :], oz[:, p, h // 2, (h % 2) * HD:(h % 2 + 1) * HD], ACT.Square,
                               scale=rden[:, h:h + 1], accum_out=ssq[:, h:h + 1]).then_inc(S["squares_ready"], 1)
            if not is_last(t):
                keys(t + 1, 1 - p)
            if not is_first(t):
                y_out(t - 1)
                x_out(t - 1)
            wait(act, S["pv_summed"], t)
            for i in range(2):
                act.wait_ge(S["p_turned"], 2 * t + i + 1)
                act.activation(pT[:, 2 * i:2 * i + 2, :, :],
                               bank[5 + i].ap().rearrange("p (h s t) -> p h s t", h=2, s=2), ACT.Copy).then_inc(S["pT_ready"], 1)
            if not is_last(t):
                exps(t + 1, 1 - p)
        weights(0, 0)
        keys(0, 0)
        exps(0, 0)
        over_tiles(act, NT, tile, last=2)
        y_out(NT - 1)
        x_out(NT - 1)
        act.wait_ge(S["y_stored"], 16 * NT)
        act.wait_ge(S["xa_stored"], 16 * NT)

    @block.vector
    def _(dve):
        dve.wait_ge(S["columns_loaded"], 16 * 15)
        dve.wait_ge(S["state_zero"], 1)
        STEPS, AHEAD = 10, 2

        def ahead(t, p, ch):
            for i in range(2):
                dve.wait_ge(S["scores_summed"], 2 * t + i + 1)
                ch.step(dve.tensor_reduce(mx[:, 2 * i:2 * i + 2], bank[3 + i].ap().rearrange("p (h s) -> p h s", h=2),
                                          AX.X, ALU.max))
            ch.sync()
            dve.tensor_scalar(nb[:, :], mx[:, :], -XA_SCALE, None, ALU.mult).then_inc(S["nb_ready"], 1)
            dve.wait_ge(S["w_ready"], 4 * t + 4)
            dve.wait_ge(S["st_summed"], t + 1)
            dve.scalar_tensor_tensor(sw[:, :, :], bank[0].ap().rearrange("p (h t) -> p h t", h=H), K_SCALE, W[:, :, :],
                                     ALU.mult, ALU.mult).then_inc(S["sw_ready"], 1)

        def attention_out(t, p):
            dve.wait_ge(S["pv_summed"], t + 1)
            wait(dve, S["xa_stored"], 16 * t)
            dve.scalar_tensor_tensor(xst[:, :, :], bank[7].ap().rearrange("p (h t) -> p h t", h=H), 0.5,
                                     xz[:, p, :, :], ALU.mult, ALU.mult).then_inc(S["xa_ready"], 1)

        def tile(t, p):
            ch = Chain(dve, S["mix_step"], AHEAD + STEPS * t)
            dve.wait_ge(S["exp_ready"], 4 * t + 4)
            ch.step(dve.reciprocal(rsum[:, :], sums[:, :]))
            ch.sync()
            for h in range(H):
                dve.tensor_scalar(pr[:, h, :], pr[:, h, :], rsum[:, h:h + 1], None, ALU.mult).then_inc(S["p_ready"], 1)
            if not is_first(t):
                attention_out(t - 1, 1 - p)

            def t1(h):
                th = oz[:, p, h // 2, (h % 2) * HD:(h % 2 + 1) * HD]
                dve.scalar_tensor_tensor(th, th, 1.0, bank[1 + h][:, 0:HD], ALU.add, ALU.mult).then_inc(S["t1_ready"], 1)
            dve.wait_ge(S[f"late_loaded{p}"], late_loaded(t, p))
            for h in range(H):
                dve.wait_ge(S["num_summed"], 4 * t + h + 1)
                ch.step(dve.tensor_copy(den[:, h:h + 1], bank[1 + h][:, HD:HE]))
                if h < H - 1:
                    t1(h)
            ch.sync()
            wait(dve, S["squares_ready"], 4 * t)
            ch.step(dve.scalar_tensor_tensor(rden[:, :], den[:, :], -1.0, den[:, :], ALU.mult, ALU.max))
            t1(H - 1)
            ch.sync()
            ch.step(dve.tensor_tensor(den[:, :], rden[:, :], emc[:, :, bass.ds(t, 1)].rearrange("p h a -> p (h a)"),
                                      ALU.max))
            ch.sync()
            dve.reciprocal(rden[:, :], den[:, :]).then_inc(S["den_ready"], 1)
            for j in range(8):
                dve.wait_ge(S["dC_summed"], 8 * t + j + 1)
                c = C[:, j // 2, j % 2, :]
                dve.scalar_tensor_tensor(c, c, wcb[:, bass.ds((j // 2) * NT + t, 1)], bank[DC_BANKS[j % 4]][:, 0:HE],
                                         ALU.mult, ALU.add).then_inc(S["C_updated"], 1)
            dve.wait_ge(S["rinv_ready"], t + 1)
            dve.wait_ge(S["den_ready"], t + 1)
            ch.step(dve.scalar_tensor_tensor(coef[:, :], rden[:, :], 0.25, rinv[:, :], ALU.mult, ALU.mult))
            ch.sync()
            wait(dve, S["y_turned"], 2 * (t - 1))
            for h in range(H):
                s = slice((h % 2) * HD, (h % 2 + 1) * HD)
                dve.wait_ge(S["t1_ready"], 4 * t + 4)
                dve.scalar_tensor_tensor(yml[:, p, h, :], oz[:, p, h // 2, s], coef[:, h:h + 1],
                                         oz[:, p, 2 + h // 2, s], ALU.mult, ALU.mult).then_inc(S["y_ready"], 1)
            if not is_last(t):
                ahead(t + 1, 1 - p, ch)
                dve.wait_ge(S["y_ready"], 4 * t + 4)
                assert ch.n == STEPS, ch.n
        ahead(0, 0, Chain(dve, S["mix_step"]))
        over_tiles(dve, NT, tile, last=2)
        attention_out(NT - 1, 1)

    ctx.close()


def sample(nc, S, sb, bank, w, ident, st_C, st_n, mem_k, mem_v, C_sample, n_sample):
    BW = TS + DT
    qk = sb("s_qk", [P, 16, TS])
    tm = sb("s_tm", [TS, 6, 512])
    xa = sb("s_xa", [P, 8, TS])
    nr = sb("s_nr", [TS, H, TS])
    ab = sb("s_ab", [P, H, TS])
    gc, wsc, emc = (sb(x, [TS, H]) for x in ("s_gc", "s_wsc", "s_emc"))
    wcb = sb("s_wcb", [P, H, DB])
    C = sb("s_C", [P, DB, H, 2, HD])
    nrow = sb("s_nrow", [DB * H, HD])
    n0 = sb("s_n0", [P, 2, DB, H])
    K = sb("s_K", [P, 2, 2, H * XD])
    V = sb("s_V", [P, DB, 2, H * XD])
    KT = sb("s_KT", [P, DB, H, NM])
    mask = sb("s_mask", [TS, DB, DT])
    own = sb("s_own", [TS, DB])
    ones = sb("s_ones", [TS, 1])
    half = sb("s_half", [TS, H])
    qm = sb("s_qm", [P, H, 2, DB * BW])
    qxm = sb("s_qxm", [P, H, DB * BW])
    sw = sb("s_sw", [TS, H, TS])
    kw = sb("s_kw", [TS, H * HD])
    kwm = sb("s_kwm", [TS, 2, H * HD])
    yst = qk[:, 0:8, :]
    xst = xa[:, 0:4, :]
    pr = sb("s_pr", [TS, H, NM])
    pT = sb("s_pT", [P, H, 2, TS])
    mx, nb, sums, rsum, den, den2, rden, ssq, msq, rinv, coef = (
        sb("s_" + x, [TS, H]) for x in ("mx", "nb", "sums", "rsum", "den", "den2", "rden", "ssq", "msq", "rinv", "coef"))
    junk = sb("s_junk", [TS, HD])
    ctx = ExitStack()
    block = ctx.enter_context(nc.Block())
    SMALL = 10

    def by_seq(ap):
        return ap.rearrange("p (b t) -> p b t", b=DB)

    def own_part(flat):
        return flat.rearrange("p (b x) -> p b x", x=BW)[:, :, 0:DT]

    @block.sync
    def _(sp):
        sp.dma_start(qk[:, :, :], w["qk"][:, :, T:TT].rearrange("f p t -> p f t")).then_inc(S["s_loaded"], 16)
        sp.dma_start(tm[:, :, :], w["tm"][:, T:TT, :].rearrange("a t n -> t a n")).then_inc(S["s_loaded"], 16)
        sp.dma_start(xa[:, :, :], w["xa"][:, :, T:TT].rearrange("f p t -> p f t")).then_inc(S["s_loaded"], 16)
        sp.dma_start(nr[:, :, :], w["negr"][:, T:TT].partition_broadcast(TS)).then_inc(S["s_loaded"], 16)
        sp.dma_start(ab[:, :, :], w["a"][:, T:TT].partition_broadcast(P)).then_inc(S["s_loaded"], 16)
        for tile, name in ((gc, "g"), (wsc, "ws"), (emc, "em")):
            sp.dma_start(tile[:, :], w[name][:, T:TT].rearrange("h t -> t h")).then_inc(S["s_loaded"], 16)
        sp.dma_start(wcb[:, :, :], w["wc"][H * NT:].rearrange("(h b) -> h b", h=H).partition_broadcast(P)).then_inc(S["s_loaded"], 16)
        sp.dma_start(nrow[:, :], st_n[0].rearrange("b h d -> (b h) d")).then_inc(S["s_loaded"], 16)
        for b in range(DB):
            wait(sp, S["s_K_turned"], b - 1)
            sp.dma_start(K[:, b % 2, :, :],
                         mem_k[0, b].rearrange("(a s) h d -> s a (h d)", s=P)).then_inc(S[f"s_K_loaded{b % 2}"], 16)
        for b in range(DB):
            sp.dma_start(C[:, b, :, :, :],
                         st_C[0, b].rearrange("h (a p) e -> p h a e", p=P)).then_inc(S["s_C_loaded"], 16)
        for b in range(DB):
            sp.dma_start(V[:, b, :, :], mem_v[0, b].rearrange("(a s) h d -> s a (h d)", s=P)).then_inc(S["s_V_loaded"], 16)
        for b in range(DB):
            sp.wait_ge(S["s_C_updated"], H * (b + 1))
            sp.dma_start(C_sample[0, b].rearrange("h (a p) e -> p h a e", p=P),
                         C[:, b, :, :, :]).then_inc(S["s_out"], 16)
        sp.wait_ge(S["s_n_ready"], 1)
        sp.dma_start(n_sample[0].rearrange("b h d -> (b h) d"), nrow[:, :]).then_inc(S["s_out"], 16)
        sp.wait_ge(S["s_y_out"], 1)
        sp.dma_start(w["yt"][0:8, :, T:TT].rearrange("f p t -> p f t"), yst[:, :, :]).then_inc(S["s_out"], 16)
        sp.wait_ge(S["s_x_out"], 1)
        sp.dma_start(w["yt"][12:16, :, T:TT].rearrange("f p t -> p f t"), xst[:, :, :]).then_inc(S["s_out"], 16)
        sp.wait_ge(S["s_out"], 16 * (DB + 3))

    @block.gpsimd
    def _(pool):
        pool.memset(mask[:, :, :], 0.0).then_inc(S["s_set"], 1)
        pool.memset(own[:, :], 1.0).then_inc(S["s_set"], 1)
        pool.memset(ones[:, :], 1.0).then_inc(S["s_set"], 1)
        pool.memset(half[:, :], -0.5).then_inc(S["s_set"], 1)
        pool.memset(qm[:, :, :, :], 0.0).then_inc(S["s_set"], 1)
        pool.memset(qxm[:, :, :], 0.0).then_inc(S["s_set"], 1)
        pool.wait_ge(S["s_set"], 6)
        pool.affine_select(out=mask[:, :, :], in_=mask[:, :, :], compare_op=ALU.is_ge, fill=MASKED, base=0,
                           pattern=[[DT, DB], [1, DT]], channel_multiplier=-1).then_inc(S["s_set"], 1)
        pool.affine_select(out=own[:, :], in_=own[:, :], compare_op=ALU.is_ge, fill=0.0, base=0,
                           pattern=[[-DT, DB]], channel_multiplier=1).then_inc(S["s_set"], 1)
        pool.wait_ge(S["s_set"], 8)
        pool.affine_select(out=mask[:, :, :], in_=mask[:, :, :], compare_op=ALU.is_ge, fill=MASKED, base=0,
                           pattern=[[-DT, DB], [0, DT]], channel_multiplier=1).then_inc(S["s_set"], 1)
        pool.affine_select(out=own[:, :], in_=own[:, :], compare_op=ALU.is_ge, fill=0.0, base=DT - 1,
                           pattern=[[DT, DB]], channel_multiplier=-1).then_inc(S["s_set"], 1)
        pool.wait_ge(S["s_squares"], H)
        pool.tensor_scalar(msq[:, :], ssq[:, :], 0.25 / HD, EPS, ALU.mult, ALU.add).then_inc(S["s_msq"], 1)
        pool.wait_ge(S["s_msq"], 1)
        pool.tensor_tensor(rinv[:, :], msq[:, :], half[:, :], ALU.pow).then_inc(S["s_rinv"], 1)

    @block.tensor
    def _(pe):
        pe.wait_ge(S["s_loaded"], 16 * SMALL)
        pe.wait_ge(S["s_set"], 10)
        for d in range(2):
            m = pe.transpose(bank[5][:, d * DB * H:(d + 1) * DB * H], nrow[:, d * P:(d + 1) * P], ident[:DB * H, :DB * H])
        m.then_inc(S["s_n_turned"], 1)
        for h in range(H):
            for d in range(2):
                m = pe.matmul(bank[0][:TS, h * TS:(h + 1) * TS], qk[:, 8 + 2 * h + d, :], qk[:, 2 * h + d, :],
                              start=(d == 0), stop=(d == 1))
        m.then_inc(S["s_st_summed"], 1)
        for i in range(8):
            m = pe.transpose(bank[(1, 4)[i // 4]][:TS, (i % 4) * P:(i % 4 + 1) * P], qk[:, 8 + i, :], ident[:, :])
        m.then_inc(S["s_k_turned"], 1)
        for b in range(DB):
            pe.wait_ge(S[f"s_K_loaded{b % 2}"], 16 * (b // 2 + 1))
            wait(pe, S["s_KT_ready0"], b - 1)
            wait(pe, S["s_KT_ready1"], b - 1)
            for h in range(H):
                for s in range(2):
                    m = pe.transpose(bank[((2, 6)[b % 2]) + h // 2][:, (h % 2) * NM + s * P:(h % 2) * NM + (s + 1) * P],
                                     K[:, b % 2, s, h * XD:(h + 1) * XD], ident[:, :])
            m.then_inc(S["s_K_turned"], 1)
        pe.wait_ge(S["s_KT_ready0"], DB)
        pe.wait_ge(S["s_KT_ready1"], DB)
        pe.wait_ge(S["s_q_masked"], 1)
        for h in range(H):
            for b in range(DB):
                m = pe.matmul(bank[6 + h // 2][:TS, (h % 2) * NM:(h % 2 + 1) * NM], qxm[:, h, b * TS:(b + 1) * TS],
                              KT[:, b, h, :], start=(b == 0), stop=(b == DB - 1))
            m.then_inc(S["s_scores"], 1)
        pe.wait_ge(S["s_sw_ready"], 1)
        pe.wait_ge(S["s_n_copied"], 1)
        pe.wait_ge(S["s_C_loaded"], 16 * DB)
        for h in range(H):
            num, dn = bank[2 + h // 2][:TS, (h % 2) * HD:(h % 2 + 1) * HD], bank[5][:TS, h:h + 1]
            for b in range(DB):
                for d in range(2):
                    q = qm[:, h, d, b * TS:(b + 1) * TS]
                    pe.matmul(num, q, C[:, b, h, d, :], start=(b + d == 0), stop=False)
                    pe.matmul(dn, q, n0[:, d, b, h:h + 1], start=(b + d == 0), stop=False)
            pe.matmul(dn, sw[:, h, :], ones[:, :], start=False, stop=True)
            m = pe.matmul(num, sw[:, h, :], tm[:, h // 2, (h % 2) * HD:(h % 2 + 1) * HD], start=False, stop=True)
        m.then_inc(S["s_num_summed"], 1)
        pe.wait_ge(S["s_p_ready"], 1)
        for h in range(H):
            for s in range(2):
                m = pe.transpose(bank[6][:, (2 * h + s) * TS:(2 * h + s + 1) * TS], pr[:, h, s * P:(s + 1) * P],
                                 ident[:TS, :TS])
        m.then_inc(S["s_p_turned"], 1)
        for b in range(DB):
            pe.wait_ge(S["s_kw_masked"], b + 1)
            for h in range(H):
                i = b * H + h
                wait(pe, S["s_C_updated"], i - 1)
                for d in range(2):
                    k_d = kwm[:, b % 2, h * HD + d * P:h * HD + (d + 1) * P]
                    pe.matmul(bank[0][:, d * DB * H + i:d * DB * H + i + 1], k_d, ones[:, :], start=True, stop=True)
                    m = pe.matmul(bank[(4, 1)[i % 2]][:, d * HD:(d + 1) * HD], k_d,
                                  tm[:, h // 2, (h % 2) * HD:(h % 2 + 1) * HD], start=True, stop=True)
                m.then_inc(S["s_dC_summed"], 1)
        pe.wait_ge(S["s_pT_ready"], 1)
        pe.wait_ge(S["s_V_loaded"], 16 * DB)
        for h in range(H):
            for b in range(DB):
                for s in range(2):
                    m = pe.matmul(bank[7][:, h * TS + b * DT:h * TS + (b + 1) * DT], V[:, b, s, h * XD:(h + 1) * XD],
                                  pT[:, h, s, b * DT:(b + 1) * DT], start=(s == 0), stop=(s == 1))
        m.then_inc(S["s_pv_summed"], 1)
        pe.wait_ge(S["s_y_ready"], 1)
        for i in range(8):
            m = pe.transpose(bank[2][:, i * TS:(i + 1) * TS], tm[:, 4 + i // 4, (i % 4) * P:(i % 4 + 1) * P], ident[:TS, :TS])
        m.then_inc(S["s_y_turned"], 1)
        pe.wait_ge(S["s_n_updated"], 1)
        for d in range(2):
            m = pe.transpose(bank[3][:DB * H, d * P:(d + 1) * P], n0[:, d].rearrange("p b h -> p (b h)"), ident[:, :])
        m.then_inc(S["s_n_back"], 1)

    @block.scalar
    def _(act):
        act.wait_ge(S["s_loaded"], 16 * SMALL)
        act.wait_ge(S["s_n_turned"], 1)
        act.activation(n0.ap().rearrange("p d b h -> p (d b h)"), bank[5][:, 0:2 * DB * H],
                       ACT.Copy).then_inc(S["s_n_copied"], 1)
        act.wait_ge(S["s_nm_ready"], 1)
        for h in range(H):
            act.activation(nr[:, h, :], nr[:, h, :], ACT.Exp, bias=gc[:, h:h + 1]).then_inc(S["s_w_ready"], 1)
        act.wait_ge(S["s_k_turned"], 1)
        for h in range(H):
            act.activation(kw[:, h * HD:(h + 1) * HD], bank[(1, 4)[h // 2]][:TS, (h % 2) * HD:(h % 2 + 1) * HD],
                           ACT.Copy, scale=wsc[:, h:h + 1]).then_inc(S["s_kw_ready"], 1)
        for b in range(DB):
            act.wait_ge(S["s_K_turned"], b + 1)
            act.activation(KT[:, b, 2:4, :], bank[(2, 6)[b % 2] + 1].ap().rearrange("p (h s) -> p h s", h=2),
                           ACT.Copy).then_inc(S["s_KT_ready1"], 1)
        act.wait_ge(S["s_nb_ready"], 1)
        for h in range(H):
            act.activation(pr[:, h, :], bank[6 + h // 2][:TS, (h % 2) * NM:(h % 2 + 1) * NM], ACT.Exp,
                           bias=nb[:, h:h + 1], scale=XA_SCALE, accum_out=sums[:, h:h + 1]).then_inc(S["s_exp_ready"], 1)
        act.wait_ge(S["s_t1_ready"], 2)
        for h in range(H):
            wait(act, S["s_squares"], h)
            act.activation(junk[:, :], tm[:, 2 + h // 2, (h % 2) * HD:(h % 2 + 1) * HD], ACT.Square,
                           scale=rden[:, h:h + 1], accum_out=ssq[:, h:h + 1]).then_inc(S["s_squares"], 1)
        act.wait_ge(S["s_p_turned"], 1)
        act.activation(pT.ap().rearrange("p h s t -> p (h s t)"), bank[6][:, :], ACT.Copy).then_inc(S["s_pT_ready"], 1)
        act.wait_ge(S["s_y_turned"], 1)
        act.activation(yst.rearrange("p f t -> p (f t)"), bank[2][:, :], ACT.Copy).then_inc(S["s_y_out"], 1)
        act.wait_ge(S["s_n_back"], 1)
        act.activation(nrow[:, :], bank[3][:DB * H, 0:HD], ACT.Copy).then_inc(S["s_n_ready"], 1)

    @block.vector
    def _(dve):
        dve.wait_ge(S["s_loaded"], 16 * SMALL)
        dve.wait_ge(S["s_set"], 10)
        ch = Chain(dve, S["s_step"])
        dve.tensor_tensor(nr[:, :, :], nr[:, :, :],
                          mask.ap().rearrange("p b t -> p (b t)").unsqueeze(1).broadcast_to([TS, H, TS]),
                          ALU.add).then_inc(S["s_nm_ready"], 1)
        for h in range(H):
            for d in range(2):
                ch.step(dve.tensor_tensor(own_part(qm[:, h, d, :]), by_seq(qk[:, 2 * h + d, :]), by_seq(ab[:, h, :]),
                                          ALU.mult))
        for h in range(H):
            ch.step(dve.tensor_copy(own_part(qxm[:, h, :]), by_seq(xa[:, h, :])))
        ch.sync()
        dve.tensor_copy(mx[:, :], gc[:, :]).then_inc(S["s_q_masked"], 1)
        dve.wait_ge(S["s_w_ready"], H)
        dve.wait_ge(S["s_st_summed"], 1)
        dve.scalar_tensor_tensor(sw[:, :, :], bank[0][:TS, 0:H * TS].rearrange("p (h t) -> p h t", h=H), K_SCALE,
                                 nr[:, :, :], ALU.mult, ALU.mult).then_inc(S["s_sw_ready"], 1)
        for b in range(DB):
            dve.wait_ge(S["s_K_turned"], b + 1)
            dve.tensor_copy(KT[:, b, 0:2, :], bank[(2, 6)[b % 2]].ap().rearrange("p (h s) -> p h s", h=2)).then_inc(S["s_KT_ready0"], 1)
        dve.wait_ge(S["s_q_masked"], 1)
        dve.wait_ge(S["s_scores"], H)
        for i in range(2):
            ch.step(dve.tensor_reduce(mx[:, 2 * i:2 * i + 2], bank[6 + i][:TS, :].rearrange("p (h s) -> p h s", h=2),
                                      AX.X, ALU.max))
        ch.sync()
        dve.tensor_scalar(nb[:, :], mx[:, :], -XA_SCALE, None, ALU.mult).then_inc(S["s_nb_ready"], 1)
        dve.wait_ge(S["s_exp_ready"], H)
        ch.step(dve.reciprocal(rsum[:, :], sums[:, :]))
        ch.sync()
        for h in range(H):
            ch.step(dve.tensor_scalar(pr[:, h, :], pr[:, h, :], rsum[:, h:h + 1], None, ALU.mult))
        ch.sync()
        dve.tensor_copy(mx[:, :], gc[:, :]).then_inc(S["s_p_ready"], 1)
        dve.wait_ge(S["s_num_summed"], 1)
        ch.step(dve.tensor_copy(den[:, :], bank[5][:TS, 0:H]))
        ch.sync()
        ch.step(dve.scalar_tensor_tensor(den2[:, :], den[:, :], -1.0, den[:, :], ALU.mult, ALU.max))
        ch.sync()
        ch.step(dve.tensor_tensor(den[:, :], den2[:, :], emc[:, :], ALU.max))
        ch.sync()
        ch.step(dve.reciprocal(rden[:, :], den[:, :]))
        ch.sync()
        for i in range(2):
            th = tm[:, 2 + i, :]
            dve.scalar_tensor_tensor(th, th, 1.0, bank[2 + i][:TS, :], ALU.add, ALU.mult).then_inc(S["s_t1_ready"], 1)
        dve.wait_ge(S["s_kw_ready"], H)

        def kw_mask(b):
            if b >= 2:
                dve.wait_ge(S["s_dC_summed"], H * (b - 1))
            dve.tensor_scalar(kwm[:, b % 2, :], kw[:, :], own[:, b:b + 1], None, ALU.mult).then_inc(S["s_kw_masked"], 1)

        kw_mask(0)
        for b in range(DB):
            if b + 1 < DB:
                kw_mask(b + 1)
            for h in range(H):
                dve.wait_ge(S["s_dC_summed"], b * H + h + 1)
                c = C[:, b, h, :, :].rearrange("p d e -> p (d e)")
                dve.scalar_tensor_tensor(c, c, wcb[:, h, b:b + 1], bank[(4, 1)[(b * H + h) % 2]][:, :], ALU.mult,
                                         ALU.add).then_inc(S["s_C_updated"], 1)
        keep = wcb.ap().rearrange("p h b -> p b h")
        for d in range(2):
            ch.step(dve.tensor_tensor(n0[:, d], n0[:, d], keep, ALU.mult))
        ch.sync()
        for d in range(2):
            ch.step(dve.tensor_tensor(n0[:, d], n0[:, d],
                                      bank[0][:, d * DB * H:(d + 1) * DB * H].rearrange("p (b h) -> p b h", b=DB), ALU.add))
        ch.sync()
        dve.tensor_copy(mx[:, :], gc[:, :]).then_inc(S["s_n_updated"], 1)
        dve.wait_ge(S["s_rinv"], 1)
        ch.step(dve.scalar_tensor_tensor(coef[:, :], rden[:, :], 0.25, rinv[:, :], ALU.mult, ALU.mult))
        ch.sync()
        dve.wait_ge(S["s_t1_ready"], 2)
        for h in range(H):
            s = slice((h % 2) * HD, (h % 2 + 1) * HD)
            ch.step(dve.scalar_tensor_tensor(tm[:, 4 + h // 2, s], tm[:, 2 + h // 2, s], coef[:, h:h + 1], tm[:, 4 + h // 2, s],
                                             ALU.mult, ALU.mult))
        ch.sync()
        dve.wait_ge(S["s_n_updated"], 1)
        dve.tensor_copy(mx[:, :], gc[:, :]).then_inc(S["s_y_ready"], 1)
        dve.wait_ge(S["s_pv_summed"], 1)
        dve.scalar_tensor_tensor(xst[:, :, :], bank[7][:, 0:H * TS].rearrange("p (h t) -> p h t", h=H), 0.5,
                                 xa[:, 4:8, :], ALU.mult, ALU.mult).then_inc(S["s_x_out"], 1)

    ctx.close()


def output(nc, S, sb, bank, w, w_out, x_prompt, x_sample, g_final, y_prompt, y_sample):
    KO = 16
    wh = sb("o_wh", [P, KO, D], F32R)
    wl = sb("o_wl", [P, KO, D], F32R)
    raw = sb("o_raw", [P, 4, D])
    yt = sb("o_yt", [P, 2, KO, P])
    yh = sb("o_yh", [P, KO, P], F32R)
    yl = sb("o_yl", [P, KO, P], F32R)
    x = sb("o_x", [P, 2, D])
    gf = sb("o_gf", [P, D])
    xsq = sb("o_xsq", [P, D])
    ss, ms, sd, rs = (sb("o_" + n, [P, NT + 1]) for n in ("ss", "ms", "sd", "rs"))
    NX = NT + 1
    ctx = ExitStack()
    block = ctx.enter_context(nc.Block())
    x_rows = x_prompt[0].rearrange("(t p) d -> t p d", p=P)
    y_rows = y_prompt[0].rearrange("(t p) d -> t p d", p=P)
    x_smp = x_sample.rearrange("b t d -> (b t) d")
    y_smp = y_sample.rearrange("b t d -> (b t) d")

    def last(t):
        return isinstance(t, int) and t == NT

    def at(t):
        return TT - P if last(t) else t * P

    def rows(ap, t):
        return ap[bass.ds(t, 1)].rearrange("a p d -> (a p) d")

    @block.sync
    def _(sp):
        sp.dma_start(gf[:, :], row_bcast(g_final, P)).then_inc(S["gf_loaded"], 16)

        def load(t, p):
            wait(sp, S["y_split"], 2 * (t - 1))
            sp.dma_start(yt[:, p, :, :], w["yt"][:, :, bass.ds(at(t), P)].rearrange("f p t -> p f t")).then_inc(S[f"yt_loaded{p}"], 16)
            wait(sp, S[f"y_out{p}"], 8 * (t - p))
            if last(t):
                sp.dma_start(x[TS:P, p, :], x_smp).then_inc(S[f"res_loaded{p}"], 16)
            else:
                sp.dma_start(x[:, p, :], rows(x_rows, t)).then_inc(S[f"res_loaded{p}"], 16)

        def weights(k):
            wait(sp, S["out_low_split"], k - 3)
            sp.dma_start(raw[:, k % 4, :], w_out[0, k * P:(k + 1) * P, :]).then_inc(S[f"wout_loaded{k % 4}"], 16)
        for k in range(4):
            weights(k)
        load(0, 0)
        for k in range(4, KO):
            weights(k)
        load(1, 1)
        with sp.Fori(1, NT // 2) as pair:
            load(2 * pair, 0)
            load(2 * pair + 1, 1)
        load(NT, 0)

    @block.tensor
    def _(pe):
        def tile(t, p):
            for k in range(KO):
                if isinstance(t, int) and t == 0:
                    pe.wait_ge(S["out_low_split"], k + 1)
                if k % 8 == 0:
                    pe.wait_ge(S["y_split"], 2 * t + k // 8 + 1)
                    if k == 0:
                        wait(pe, S["res_added"], 2 * (t - 1))
                for n in range(2):
                    out, c = bank[2 * p + n][:, :], slice(512 * n, 512 * (n + 1))
                    pe.matmul(out, yh[:, k, :], wh[:, k, c], start=(k == 0), stop=False)
                    pe.matmul(out, yh[:, k, :], wl[:, k, c], start=False, stop=False)
                    m = pe.matmul(out, yl[:, k, :], wh[:, k, c], start=False, stop=(k == KO - 1))
                if k % 8 == 7:
                    m.then_inc(S["y_half_used"], 1)
        over_tiles(pe, NX, tile)

    @block.scalar
    def _(act):
        def high(t, p):
            act.wait_ge(S[f"yt_loaded{p}"], 8 * (t - p) + 16)
            for i in range(2):
                wait(act, S["y_half_used"], 2 * (t - 1) + i + 1)
                s = slice(8 * i, 8 * i + 8)
                act.activation(yh[:, s, :], yt[:, p, s, :], ACT.Copy).then_inc(S["y_high"], 1)

        def norm(t, p):
            r = slice(TS if last(t) else 0, P)
            act.wait_ge(S["res_added"], 2 * t + 2)
            c = bass.ds(t, 1)
            act.activation(xsq[r, :], x[r, p, :], ACT.Square, accum_out=ss[r, c]).then_inc(S["out_squared"], 1)
            act.wait_ge(S["out_mean"], t + 1)
            act.activation(sd[r, c], ms[r, c], ACT.Sqrt).then_inc(S["out_std"], 1)

        def tile(t, p):
            if not last(t):
                high(t + 1, 1 - p)
            wait(act, S["out_squared"], t)
            norm(t, p)
            act.wait_ge(S["out_ready"], t + 1)
            dst = y_smp if last(t) else rows(y_rows, t)
            act.dma_start(dst, x[TS if last(t) else 0:P, p, :]).then_inc(S[f"y_out{p}"], 16)
        high(0, 0)
        over_tiles(act, NX, tile)
        act.wait_ge(S["y_out0"], 16 * 9)
        act.wait_ge(S["y_out1"], 16 * 8)

    @block.vector
    def _(dve):
        def low(t, p):
            for i in range(2):
                dve.wait_ge(S["y_high"], 2 * t + i + 1)
                s = slice(8 * i, 8 * i + 8)
                dve.tensor_tensor(yl[:, s, :], yt[:, p, s, :], yh[:, s, :].bitcast(F32), ALU.subtract).then_inc(S["y_split"], 1)

        def split(k):
            dve.wait_ge(S[f"wout_loaded{k % 4}"], 16 * (k // 4 + 1))
            dve.tensor_copy(wh[:, k, :], raw[:, k % 4, :]).then_inc(S["out_high_split"], 1)
            dve.wait_ge(S["out_high_split"], k + 1)
            dve.tensor_tensor(wl[:, k, :], raw[:, k % 4, :], wh[:, k, :].bitcast(F32),
                              ALU.subtract).then_inc(S["out_low_split"], 1)

        def tile(t, p):
            if not last(t):
                low(t + 1, 1 - p)
            r = slice(TS if last(t) else 0, P)
            c = bass.ds(t, 1)
            dve.wait_ge(S[f"res_loaded{p}"], 8 * (t - p) + 16)
            dve.wait_ge(S["y_half_used"], 2 * t + 2)
            for n in range(2):
                s = slice(512 * n, 512 * (n + 1))
                dve.tensor_tensor(x[r, p, s], x[r, p, s], bank[2 * p + n][r, :], ALU.add).then_inc(S["res_added"], 1)
            dve.wait_ge(S["out_squared"], t + 1)
            dve.tensor_scalar(ms[r, c], ss[r, c], 1.0 / D, EPS, ALU.mult, ALU.add).then_inc(S["out_mean"], 1)
            dve.wait_ge(S["out_std"], t + 1)
            dve.reciprocal(rs[r, c], sd[r, c]).then_inc(S["out_rstd"], 1)
            dve.wait_ge(S["out_rstd"], t + 1)
            dve.scalar_tensor_tensor(x[r, p, :], x[r, p, :], rs[r, c], gf[r, :], ALU.mult, ALU.mult).then_inc(S["out_ready"], 1)
        dve.wait_ge(S["gf_loaded"], 16)
        split(0)
        split(1)
        low(0, 0)
        for k in range(2, KO):
            split(k)
        over_tiles(dve, NX, tile)

    ctx.close()


_INS = ["x_prompt", "x_sample", "state_mlstm_C", "state_mlstm_n", "state_mlstm_m", "state_conv", "cache_mem_k",
        "cache_mem_v", "mem_prompt", "g_norm", "w_in", "b_if", "g_head", "conv_w", "conv_b", "g_mem", "w_mem_kv",
        "w_out", "g_final"]
_OUTS = [(1, T, D), (DB, DT, D), (1, 1, H, HD, HD), (1, 1, H, HD), (1, 1, H), (1, 1, 2, CC), (1, 1, NM, H, XD),
         (1, 1, NM, H, XD), (1, DB, H, HD, HD), (1, DB, H, HD), (1, DB, H), (1, DB, 2, CC)]


def kernel(**inputs):
    import numpy as np
    import concourse.bacc as bacc
    from concourse.bass_utils import run_bass_kernel_spmd

    arrays = {f"in_{n}": np.ascontiguousarray(inputs[n]) for n in _INS}
    nc = bacc.Bacc("TRN2", target_bir_lowering=False, num_devices=1)
    args = [nc.dram_tensor(n, a.shape, F32, kind="ExternalInput").ap() for n, a in arrays.items()]
    args += [nc.dram_tensor(f"out_{i}", s, F32, kind="ExternalOutput").ap() for i, s in enumerate(_OUTS)]
    layer(nc, *args)
    r = run_bass_kernel_spmd(nc, [arrays], core_ids=[0])
    return tuple(r.results[0][f"out_{i}"] for i in range(len(_OUTS)))
```

```python
from contextlib import ExitStack

import concourse.bass as bass
from concourse import mybir

F32 = mybir.dt.float32
F32R = mybir.dt.float32r
ALU = mybir.AluOpType
ACT = mybir.ActivationFunctionType
AX = mybir.AxisListType

P = 128
D = 1024
KD = D // P
T = 2048
DB, DT = 8, 8
TS = DB * DT
TT = T + TS
NT = T // P
H = 4
HD = 256
XD = 128
CC = 512
NM = 256
EPS = 1e-6
MASKED = -1e30
XA_SCALE = XD ** -0.5
K_SCALE = HD ** -0.5
COL_QK, COL_TM, COL_IF, COL_CV = 0, 2048, 5120, 5128
COL_XA = COL_CV + 4 * CC
CHUNKS = [(0, 384), (384, 384), (768, 192), (960, 384), (1344, 384), (1728, 384)]


class Semaphores:

    def __init__(self, nc):
        self.nc, self.made = nc, {}

    def __getitem__(self, name):
        if name not in self.made:
            self.made[name] = self.nc.alloc_semaphore(name)
        return self.made[name]

    def phase_done(self):
        self.nc.all_engine_barrier()
        self.nc.clear_and_free_semaphores(list(self.made.values()))
        self.nc.all_engine_barrier()
        self.made = {}


def wait(eng, sem, value):
    if isinstance(value, int) and value <= 0:
        return
    eng.wait_ge(sem, value)


def over_tiles(eng, n, body, last=0):
    body(0, 0)
    body(1, 1)
    pairs = (n - last) // 2
    with eng.Fori(1, pairs) as pair:
        body(2 * pair, 0)
        body(2 * pair + 1, 1)
    for t in range(2 * pairs, n):
        body(t, t % 2)


def layer(nc, x_prompt, x_sample, st_C, st_n, st_m, st_conv, mem_k, mem_v, mem_prompt,
          g_norm, w_in, b_if, g_head, conv_w, conv_b, g_mem, w_mem_kv, w_out, g_final,
          y_prompt, y_sample, C_prompt, n_prompt, m_prompt, conv_prompt, mk_prompt, mv_prompt,
          C_sample, n_sample, m_sample, conv_sample):
    ctx = ExitStack()
    with ctx:
        S = Semaphores(nc)
        ctx.enter_context(nc.allow_non_contiguous_dma(reason="small states and gates change their layout"))

        def dram(name, shape):
            return nc.dram_tensor(name, shape, F32, kind="Internal").ap()

        def sb(c, name, shape, dt=F32, side="left"):
            return c.enter_context(nc.sbuf_tensor(name, shape, dt, side=side))

        w = dict(
            qk=dram("scr_qk", (16, P, TT)), xa=dram("scr_xa", (8, P, TT)), tm=dram("scr_tm", (6, TT, 512)),
            yt=dram("scr_yt", (16, P, TT)), gate=dram("scr_gate", (8, TT)), negr=dram("scr_negr", (H, TT)),
            a=dram("scr_a", (H, TT)), g=dram("scr_g", (H, TT)), ws=dram("scr_ws", (H, TT)),
            em=dram("scr_em", (H, TT)), last=dram("scr_last", (2, H * NT)), mprev=dram("scr_mprev", (H * NT,)),
            mkT=dram("scr_mkT", (P, H, NM)),
            wc=dram("scr_wc", (H * NT + H * DB,)))
        bank = [ctx.enter_context(nc.psum_tensor(f"bank{i}", [P, 512], F32)) for i in range(8)]
        ident = sb(ctx, "ident", [P, P])
        columns = gate_columns(lambda *a: sb(ctx, *a))
        raw = sb(ctx, "raw", [P, KD, 512])

        with ExitStack() as c01:
            xh = sb(c01, "xh", [P, KD, TT], F32R)
            xl = sb(c01, "xl", [P, KD, TT], F32R)
            with ExitStack() as c:
                prep(nc, S, lambda *a: sb(c, *a), bank, ident, w, xh, xl, raw, x_prompt, x_sample,
                     g_norm, mem_prompt, g_mem, w_mem_kv, w_in, mk_prompt, mv_prompt)
            with ExitStack() as c:
                project(nc, S, lambda *a: sb(c, *a), bank, w, xh, xl, raw, columns, w_in, b_if, g_head, conv_w,
                        conv_b, st_conv, st_m, conv_prompt, conv_sample, m_prompt, m_sample)
        S.phase_done()
        shared = sb(ctx, "shared", [P, 16, P])
        with ExitStack() as c23:
            tiles = sample_tiles(lambda *a: sb(c23, *a, side="right"))
            with ExitStack() as c:
                mix(nc, S, lambda *a: sb(c, *a), bank, w, ident, raw, columns, mv_prompt, C_prompt, n_prompt,
                    tiles, shared, st_C, st_n, mem_k)
            with ExitStack() as c:
                slots = sb(c, "slots", [P, 16, D])
            wl = sb(ctx, "o_wl", [P, 16, D], F32R)
            with ExitStack() as c:
                sample(nc, S, lambda *a: sb(c, *a), bank, w, ident, raw, shared, slots, tiles, mem_k, mem_v,
                       w_out, C_sample, n_sample)
        with ExitStack() as c:
            output(nc, S, lambda *a: sb(c, *a), bank, w, shared, slots, wl, w_out, x_prompt, x_sample, g_final,
                   y_prompt, y_sample)


def gate_columns(sb):
    return dict(gc=sb("gc", [P, H, NT]), wsc=sb("wsc", [P, H, NT]), emc=sb("emc", [P, H, NT]), wcb=sb("wcb", [P, H * NT]))


def qk_tiles(raw):
    return raw.ap().rearrange("p k n -> p (k n)").rearrange("p (s f t) -> p s f t", s=2, f=16)


def row_bcast(v, n):
    return v.partition_broadcast(n)


def prep(nc, S, sb, bank, ident, w, xh, xl, raw, x_prompt, x_sample, g_norm, mem_prompt, g_mem,
         w_mem_kv, w_in, mk_prompt, mv_prompt):
    NR = NT + 3
    SLOTS = 4
    wkv = sb("wkv", [P, 2, D])
    xin = sb("xin", [P, SLOTS, D])
    gx = sb("gx", [P, D])
    sq = sb("sq", [P, D])
    kvs = sb("kvs", [P, 4, 512])
    mkT = sb("mkT", [P, H, NM])
    gm = sb("gm", [P, D])
    ss = sb("ss", [P, NR])
    sd = sb("sd", [P, NR])
    rs = sb("rs", [P, NR])
    eps = sb("p_eps", [P, 1])
    memT = sb("memT", [P, KD, NM])
    MEM_HALVES = [min(max(u - 3, 0) * 9 // 8, 2 * KD) for u in range(NR + 1)]
    x_rows = x_prompt[0].rearrange("(t p) d -> t p d", p=P)
    x_smp = x_sample.rearrange("b t d -> (b t) d")
    mem_rows = mem_prompt[0].rearrange("(t p) d -> t p d", p=P)
    ctx = ExitStack()
    block = ctx.enter_context(nc.Block())

    def known(u):
        return isinstance(u, int)

    def rows(u):
        return TS if known(u) and u == NR - 1 else P

    def of_memory(u):
        return known(u) and u < 2

    def every(eng, body):
        for u in range(SLOTS):
            body(u, u)
        with eng.Fori(1, NR // SLOTS) as turn:
            for p in range(SLOTS):
                body(SLOTS * turn + p, p)
        for u in range(NR // SLOTS * SLOTS, NR):
            body(u, u % SLOTS)

    @block.sync
    def _(sp):
        def load(u, p):
            n = rows(u)
            wait(sp, S["x_turned"], u - SLOTS + 1)
            if of_memory(u):
                src = mem_rows[u]
            elif known(u) and u == NR - 1:
                src = x_smp
            else:
                src = x_rows[bass.ds(u - 2, 1)].rearrange("a p d -> (a p) d")
            sp.dma_start(xin[:n, p, :], src).then_inc(S[f"x_loaded{p}"], 16)
            if known(u) and u == 0:
                sp.dma_start(gm[:, :], row_bcast(g_mem[0], P)).then_inc(S["gm_loaded"], 16)
            if known(u) and u == 1:
                sp.dma_start(gx[:, :], row_bcast(g_norm[0], P)).then_inc(S["gx_loaded"], 16)
        every(sp, load)
        for k in range(KD):
            sp.dma_start(raw[:, k, :], weights_ap(w_in, KINDS[0][0], 0, k)).then_inc(S[f"raw_loaded{k}"], 16)

    @block.gpsimd
    def _(pool):
        pool.memset(eps[:, :], EPS).then_inc(S["eps_ready"], 1)
        pool.memset(ident[:, :], 0.0).then_inc(S["ident_zero"], 1)
        pool.wait_ge(S["ident_zero"], 1)
        pool.affine_select(out=ident[:, :], in_=ident[:, :], compare_op=ALU.not_equal, fill=1.0, base=0,
                           pattern=[[-1, P]], channel_multiplier=1).then_inc(S["ident_ready"], 1)
        for k in range(KD):
            wait(pool, S["wkv_used"], k - 1)
            pool.dma_start(wkv[:, k % 2, :], w_mem_kv[0, k * P:(k + 1) * P, :]).then_inc(S[f"wkv_loaded{k % 2}"], 16)

    @block.scalar
    def _(act):
        act.wait_ge(S["eps_ready"], 1)

        def square(u, p):
            n, c = rows(u), bass.ds(u, 1)
            act.wait_ge(S[f"x_loaded{p}"], 4 * (u - p) + 16)
            wait(act, S["squared"], u)
            act.activation(sq[:n, :], xin[:n, p, :], ACT.Square, accum_out=ss[:n, c]).then_inc(S["squared"], 1)
            act.wait_ge(S["squared"], u + 1)
            act.activation(sd[:n, c], ss[:n, c], ACT.Sqrt, scale=1.0 / D, bias=eps[:n, :]).then_inc(S["std_ready"], 1)

        def high(u, q):
            n = rows(u)
            act.wait_ge(S["x_turned"], u + 1)
            for half in range(2):
                dst = memT[:, 4 * half:4 * half + 4, u * P:(u + 1) * P] if of_memory(u) else \
                    xh[:, 4 * half:4 * half + 4, bass.ds((u - 2) * P, n)]
                src = bank[2 * q + half].ap().rearrange("p (k n) -> p k n", k=4)[:, :, 0:n]
                act.activation(dst, src, ACT.Copy).then_inc(S["high_ready"], 1)

        def stage(u, p):
            square(u, p)
            if not (known(u) and u < 2):
                high(u - 2, p % 2)
        every(act, stage)
        high(NR - 2, (NR - 2) % 2)
        act.wait_ge(S["wkv_used"], KD)
        for i in range(4):
            act.activation(kvs[:, i, :], bank[4 + i][:, :], ACT.Copy).then_inc(S["kv_copied"], 1)
        high(NR - 1, (NR - 1) % 2)
        for i in range(4):
            act.wait_ge(S["kv_copied"], i + 1)
            st, kv = i // 2, i % 2
            dst = (mk_prompt, mv_prompt)[kv][0, 0].rearrange("s h d -> s (h d)")[st * P:(st + 1) * P, :]
            act.dma_start(dst, kvs[:, i, :]).then_inc(S["kv_stored"], 16)
        for st in range(2):
            act.wait_ge(S["key_turned"], st + 1)
            act.activation(mkT[:, :, st * P:(st + 1) * P], bank[4 + st].ap().rearrange("p (h s) -> p h s", h=H),
                           ACT.Copy).then_inc(S["mkT_ready"], 1)
        act.wait_ge(S["mkT_ready"], 2)
        act.dma_start(w["mkT"], mkT[:, :, :]).then_inc(S["kv_stored"], 16)

    @block.vector
    def _(dve):
        def norm(u, p):
            n, c = rows(u), bass.ds(u, 1)
            dve.wait_ge(S["std_ready"], u + 1)
            dve.reciprocal(rs[:n, c], sd[:n, c]).then_inc(S["rstd_ready"], 1)
            dve.wait_ge(S["rstd_ready"], u + 1)
            g = gm if of_memory(u) else gx
            if known(u) and u in (0, 2):
                dve.wait_ge(S["gx_loaded" if u else "gm_loaded"], 16)
            dve.scalar_tensor_tensor(xin[:n, p, :], xin[:n, p, :], rs[:n, c], g[:n, :],
                                     ALU.mult, ALU.mult).then_inc(S["x_normed"], 1)

        def low(u, q):
            n = rows(u)
            for half in range(2):
                dve.wait_ge(S["high_ready"], 2 * u + half + 1)
                src = bank[2 * q + half].ap().rearrange("p (k n) -> p k n", k=4)[:, :, 0:n]
                at = bass.ds((u - 2) * P, n)
                dve.tensor_tensor(xl[:, 4 * half:4 * half + 4, at], src,
                                  xh[:, 4 * half:4 * half + 4, at].bitcast(F32), ALU.subtract).then_inc(S["low_ready"], 1)

        def stage(u, p):
            norm(u, p)
            if not (known(u) and u < 4):
                low(u - 2, p % 2)
        every(dve, stage)
        for u in (NR - 2, NR - 1):
            low(u, u % 2)

    @block.tensor
    def _(pe):
        pe.wait_ge(S["ident_ready"], 1)
        for u in range(NR):
            n, q = rows(u), u % 2
            pe.wait_ge(S["x_normed"], u + 1)
            if u in (2, 3):
                pe.wait_ge(S["high_ready"], 2 * (u - 1))
            if u >= 4:
                pe.wait_ge(S["low_ready"], 2 * (u - 3))
            for k in range(KD):
                m = pe.transpose(bank[2 * q + k // 4][:, (k % 4) * P:(k % 4) * P + n],
                                 xin[:n, u % SLOTS, k * P:(k + 1) * P], ident[:n, :n])
            m.then_inc(S["x_turned"], 1)
            for half in range(MEM_HALVES[u], MEM_HALVES[u + 1]):
                k, st = half // 2, half % 2
                if half == 0:
                    pe.wait_ge(S["high_ready"], 4)
                pe.wait_ge(S[f"wkv_loaded{k % 2}"], 16 * (k // 2 + 1))
                for kv in range(2):
                    m = pe.matmul(bank[4 + 2 * st + kv][:, :], memT[:, k, st * P:(st + 1) * P],
                                  wkv[:, k % 2, kv * 512:(kv + 1) * 512], start=(k == 0), stop=(k == KD - 1))
                if st:
                    m.then_inc(S["wkv_used"], 1)
        for st in range(2):
            pe.wait_ge(S["kv_copied"], 2 * st + 1)
            for h in range(H):
                m = pe.transpose(bank[4 + st][:, h * P:(h + 1) * P], kvs[:, 2 * st, h * P:(h + 1) * P], ident[:, :])
            m.then_inc(S["key_turned"], 1)

    ctx.close()


KINDS = [("qx", 1, 24), ("gate", 1, 6), ("conv", 4, 24), ("qk", 4, 24), ("v", 2, 17), ("o", 2, 17), ("z", 2, 17),
         ("zx", 1, 24)]
BANKS = {24: [g % 8 for g in range(24)], 17: [7, 0, 1, 2, 3, 4, 7, 5, 6, 0, 1, 2, 7, 3, 4, 5, 6], 6: list(range(6))}
RING = 4


def weights_ap(w_in, kind, i, k):
    rows = w_in[0, k * P:(k + 1) * P, :]
    if kind == "gate":
        return rows[:, COL_IF:COL_IF + P]
    if kind == "conv":
        return rows[:, COL_CV:COL_CV + 4 * CC].rearrange("p (a c) -> p a c", a=4)[:, :, bass.ds(i * P, P)]
    col = {"qk": COL_QK, "v": COL_TM, "o": COL_TM + D, "z": COL_TM + 2 * D, "qx": COL_XA,
           "zx": COL_XA + 512}[kind]
    return rows[:, bass.ds(col + 512 * i, 512)]


def kind_bases():
    quads, groups, stored, out = 0, 0, [0] * RING, {}
    for kind, n, g in KINDS:
        out[kind] = (quads, groups, list(stored))
        quads, groups = quads + n, groups + n * g
        results = 6 if kind == "conv" else g
        for s in range(RING):
            stored[s] += n * len(range(s, results, RING))
    return out


def bank_user(kind, g):
    order, back = BANKS[dict((k, x) for k, _, x in KINDS)[kind]], []
    kinds = [k for k, _, _ in KINDS]
    if order[g] in order[:g]:
        return g - max(x for x in range(g) if order[x] == order[g])
    before = [kind] if dict((k, x) for k, x, _ in KINDS)[kind] > 1 else []
    before += kinds[kinds.index(kind) - 1:kinds.index(kind)] if kinds.index(kind) else []
    for other in before:
        last = BANKS[dict((k, x) for k, _, x in KINDS)[other]]
        if order[g] in last:
            back.append(g + len(last) - max(x for x in range(len(last)) if last[x] == order[g]))
        else:
            back.append(g + 1)
    return min(back) if back else None


BASE = kind_bases()


def ring_value(kind, i, g):
    results = 6 if kind == "conv" else dict((k, x) for k, _, x in KINDS)[kind]
    s = g % RING
    return 16 * (BASE[kind][2][s] + g // RING) + 16 * len(range(s, results, RING)) * i


class Chain:

    def __init__(self, eng, sem, base=0):
        self.eng, self.sem, self.base, self.n = eng, sem, base, 0

    def step(self, instruction):
        instruction.then_inc(self.sem, 1)
        self.n += 1

    def sync(self):
        wait(self.eng, self.sem, self.base + self.n)


def project(nc, S, sb, bank, w, xh, xl, raw, columns, w_in, b_if, g_head, conv_w, conv_b, st_conv, st_m,
            conv_prompt, conv_sample, m_prompt, m_sample):
    wh = sb("wh", [P, KD, 512], F32R)
    wl = sb("wl", [P, KD, 512], F32R)
    stage = sb("stage", [P, RING, 512])
    work = sb("work", [P, 1920])
    cw = sb("cw", [P, 3, 4])
    cb = sb("cb", [P, 4])
    cst = sb("cst", [P, 4, DB, 2])
    cnew_p = sb("cnew_p", [P, 4, 2])
    cnew_s = sb("cnew_s", [P, 4, DB, 2])
    bif = sb("bif", [8, 1])
    R96 = H * NT + H * DB
    gi, gf, gF, gt = (sb(n, [R96, P]) for n in ("gi", "gf", "gF", "gt"))
    gz = sb("gz", [R96, P])
    gw = work[0:R96, D:D + P]
    gm = sb("gm1", [R96, 1])
    fl, gl, mn, mprev = (sb(n, [H, NT]) for n in ("fl", "gl", "mn", "mprev"))
    cs = work[:, 0:768].rearrange("p (s n) -> p s n", s=2)
    th = work[:, 768:1536].rearrange("p (s n) -> p s n", s=2)
    ut = sb("ut", [P, 2, 386])
    us = sb("us", [P, DB, 10])
    yc = sb("yc", [P, 384])
    sil = work[:, 1536:1920]
    ghb = work[:, 0:D]
    TMK = {"v": 0, "o": 2, "z": 4}
    ng = {k: g for k, _, g in KINDS}
    ctx = ExitStack()
    block = ctx.enter_context(nc.Block())

    def quads(eng, kind, body):
        n = dict((k, x) for k, x, _ in KINDS)[kind]
        if n == 1:
            body(0)
        else:
            with eng.Fori(0, n) as i:
                body(i)

    @block.sync
    def _(sp):
        sp.dma_start(bif[:, :], b_if[0].rearrange("(a b) -> a b", b=1)).then_inc(S["small_loaded"], 16)
        for j in range(3):
            sp.dma_start(cw[:, j, :], conv_w[0, j].rearrange("(j p) -> p j", p=P)).then_inc(S["small_loaded"], 16)
        sp.dma_start(cb[:, :], conv_b[0].rearrange("(j p) -> p j", p=P)).then_inc(S["small_loaded"], 16)
        for j in range(4):
            sp.dma_start(cst[:, j, :, :],
                         st_conv[0, :, :, j * P:(j + 1) * P].rearrange("b w p -> p b w")).then_inc(S["small_loaded"], 16)
        for kind, n, _ in KINDS:
            if kind == "v":
                sp.wait_ge(S["conv_kept"], 4)
                sp.dma_start(ghb, row_bcast(g_head[0], P)).then_inc(S["gain_loaded"], 16)

            def load(i, kind=kind):
                q = BASE[kind][0] + i
                for k in range(KD):
                    wait(sp, S["low_split"], 8 * (q - 1) + k + 1)
                    dst = raw[:, k, :]
                    if kind == "gate":
                        dst = raw[:, k, 0:P]
                    if kind == "conv":
                        dst = dst.rearrange("p (a c) -> p a c", a=4)
                    sp.dma_start(dst, weights_ap(w_in, kind, i, k)).then_inc(S[f"raw_loaded{k}"], 16)
            if kind != KINDS[0][0]:
                quads(sp, kind, load)
        sp.wait_ge(S["conv_kept"], 4)
        for j in range(4):
            sp.dma_start(conv_prompt[0, 0, :, j * P:(j + 1) * P].rearrange("w p -> p w"),
                         cnew_p[:, j, :]).then_inc(S["conv_state_stored"], 16)
            sp.dma_start(conv_sample[0, :, :, j * P:(j + 1) * P].rearrange("b w p -> p b w"),
                         cnew_s[:, j, :, :]).then_inc(S["conv_state_stored"], 16)
        sp.wait_ge(S["conv_state_stored"], 8 * 16)
        for s in range(RING):
            sp.wait_ge(S[f"stored{s}"], ring_value("v", 0, s))
        sp.wait_ge(S["low_split"], KD * sum(n for _, n, _ in KINDS))
        for t in range(2):
            sp.dma_start(qk_tiles(raw)[:, t, :, :],
                         w["qk"][:, :, t * P:(t + 1) * P].rearrange("f p t -> p f t")).then_inc(S["qk_loaded"], 16)
        sp.wait_ge(S["qk_loaded"], 32)

    def split(dve, q, groups, cols=512):
        def low(k):
            dve.wait_ge(S["high_split"], 8 * q + k + 1)
            dve.tensor_tensor(wl[:, k, 0:cols], raw[:, k, 0:cols], wh[:, k, 0:cols].bitcast(F32),
                              ALU.subtract).then_inc(S["low_split"], 1)
        for k in range(KD):
            dve.wait_ge(S[f"raw_loaded{k}"], 16 * (q + 1))
            if k < KD - 1:
                wait(dve, S["weights_used"], 7 * (q - 1) + k + 1)
            else:
                wait(dve, S["summed"], groups)
            dve.tensor_copy(wh[:, k, 0:cols], raw[:, k, 0:cols]).then_inc(S["high_split"], 1)
            if k:
                low(k - 1)
        low(KD - 1)

    def split_next(dve, kind, i):
        split(dve, BASE[kind][0] + i + 1, BASE[kind][1] + ng[kind] * (i + 1))

    @block.tensor
    def _(pe):
        for kind, n, G in KINDS:
            def quad(i, kind=kind, G=G):
                q, g0 = BASE[kind][0] + i, BASE[kind][1] + G * i
                for g in range(G):
                    back = bank_user(kind, g)
                    if back is not None:
                        pe.wait_ge(S["bank_free"], g0 + g + 1 - back)
                    for k in range(KD):
                        if g == 0:
                            pe.wait_ge(S["low_split"], 8 * q + k + 1)
                        if kind in ("v", "o", "z"):
                            at = min(g * P, TT - P)
                            out = bank[BANKS[G][g]][:, :]
                            ah, al = xh[:, k, at:at + P], xl[:, k, at:at + P]
                            bh, bl = wh[:, k, :], wl[:, k, :]
                        else:
                            (at, m), j = (CHUNKS[g], 0) if kind == "gate" else (CHUNKS[g // 4], g % 4)
                            out = bank[BANKS[G][g]][:, 0:m]
                            ah, al = wh[:, k, j * P:(j + 1) * P], wl[:, k, j * P:(j + 1) * P]
                            bh, bl = xh[:, k, at:at + m], xl[:, k, at:at + m]
                        pe.matmul(out, ah, bh, start=(k == 0), stop=False)
                        pe.matmul(out, ah, bl, start=False, stop=False)
                        mm = pe.matmul(out, al, bh, start=False, stop=(k == KD - 1))
                        if g == G - 1 and k < KD - 1:
                            mm.then_inc(S["weights_used"], 1)
                    mm.then_inc(S["summed"], 1)
            quads(pe, kind, quad)

    def result(kind, i, g):
        s = g % RING
        if kind in ("v", "o", "z"):
            quad = w["tm"][bass.ds(TMK[kind] + i, 1)].rearrange("a t n -> (a t) n")
            if g < NT:
                return stage[:, s, :], quad[g * P:(g + 1) * P, :]
            return stage[P - TS:, s, :], quad[T:TT, :]
        if kind == "gate":
            at, m = CHUNKS[g]
            return stage[0:8, s, 0:m], w["gate"][:, at:at + m]
        if kind == "conv":
            at, m = CHUNKS[g]
            rows = w["yt"][bass.ds(8 + i, 1)]
        else:
            at, m = CHUNKS[g // 4]
            to, b = {"qk": (w["qk"], 4 * i), "qx": (w["xa"], 0), "zx": (w["xa"], 4)}[kind]
            rows = to[bass.ds(b + g % 4, 1)]
        return stage[:, s, 0:m], rows.rearrange("a p t -> (a p) t")[:, at:at + m]

    @block.scalar
    def _(act):
        def store(kind, i, g, ready, value):
            act.wait_ge(S[ready], value)
            src, dst = result(kind, i, g)
            act.dma_start(dst, src).then_inc(S[f"stored{g % RING}"], 16)

        def copy_kind(kind):
            def quad(i):
                G = ng[kind]
                g0 = BASE[kind][1] + G * i
                for g in range(G):
                    act.wait_ge(S["summed"], g0 + g + 1)
                    wait(act, S[f"stored{g % RING}"], ring_value(kind, i, g))
                    if kind == "gate":
                        m = CHUNKS[g][1]
                        act.activation(stage[0:8, g % RING, 0:m], bank[BANKS[G][g]][0:8, 0:m], ACT.Identity,
                                       bias=bif[:, 0:1]).then_inc(S["bank_free"], 1)
                    elif kind == "o":
                        act.activation(stage[:, g % RING, :], bank[BANKS[G][g]][:, :], ACT.Tanh,
                                       scale=0.5).then_inc(S["bank_free"], 1)
                    else:
                        m = 512 if kind == "v" else CHUNKS[g // 4][1]
                        act.activation(stage[:, g % RING, 0:m], bank[BANKS[G][g]][:, 0:m],
                                       ACT.Copy).then_inc(S["bank_free"], 1)
                    if g:
                        store(kind, i, g - 1, "bank_free", g0 + g)
                store(kind, i, G - 1, "bank_free", g0 + G)
            quads(act, kind, quad)

        def gated_kind(kind):
            def quad(i):
                G = ng[kind]
                g0 = BASE[kind][1] + G * i
                ready, c0 = ("silu_ready", G * i) if kind == "z" else ("bank_free", g0)
                for g in range(G):
                    act.wait_ge(S["summed"], g0 + g + 1)
                    wait(act, S[f"stored{g % RING}"], ring_value(kind, i, g))
                    m = 512 if kind == "z" else CHUNKS[g // 4][1]
                    act.activation(stage[:, g % RING, 0:m], bank[BANKS[G][g]][:, 0:m], ACT.Tanh,
                                   scale=0.5).then_inc(S["tanh_ready"], 1)
                    if g:
                        store(kind, i, g - 1, ready, c0 + g)
                store(kind, i, G - 1, ready, c0 + G)
            quads(act, kind, quad)

        act.wait_ge(S["kv_stored"], 80)
        act.wait_ge(S["small_loaded"], 16 * 9)
        copy_kind("qx")
        copy_kind("gate")
        def conv(i):
            g0 = BASE["conv"][1] + 24 * i
            for c, (at, m) in enumerate(CHUNKS):
                g = 4 * c
                act.wait_ge(S["summed"], g0 + g + 2)
                act.wait_ge(S["bank_free"], g0 + g - 4)
                act.activation(cs[:, c % 2, 0:m], bank[(g + 1) % 8][:, 0:m], ACT.Copy).then_inc(S["conv_c_ready"], 1)
                act.wait_ge(S["summed"], g0 + g + 4)
                act.activation(th[:, c % 2, 0:m], bank[(g + 3) % 8][:, 0:m], ACT.Tanh,
                               scale=0.5).then_inc(S["conv_t_ready"], 1)
                if c:
                    store("conv", i, c - 1, "conv_y_ready", 6 * i + c)
            store("conv", i, 5, "conv_y_ready", 6 * i + 6)
        quads(act, "conv", conv)
        act.wait_ge(S["gate_abs"], 1)
        act.activation(gt[:, :], gt[:, :], ACT.Exp, scale=-1.0).then_inc(S["gate_exp"], 1)
        act.wait_ge(S["gate_exp"], 1)
        act.activation(gt[:, :], gt[:, :], ACT.Ln, bias=1.0).then_inc(S["gate_log"], 1)
        copy_kind("qk")
        act.wait_ge(S["gate_r"], 2)
        act.wait_ge(S["conv_kept"], 4)
        act.activation(gf[:, :], gz[:, :], ACT.Exp, bias=gm[:, 0:1]).then_inc(S["gate_a"], 1)
        act.activation(gt[:, :], gF[:, :], ACT.Exp, scale=-1.0).then_inc(S["gate_em"], 1)
        act.activation(gw, gi[:, :], ACT.Exp, bias=gz[:, P - 1:P]).then_inc(S["gate_ws"], 1)
        copy_kind("v")
        copy_kind("o")
        gated_kind("z")
        gated_kind("zx")
        for s in range(RING):
            act.wait_ge(S[f"stored{s}"], ring_value("zx", 0, s) + 16 * (ng["zx"] // RING))

    @block.vector
    def _(dve):
        split(dve, 0, 0)
        split(dve, 1, BASE["gate"][1], P)
        split_next(dve, "gate", 0)
        gates = Chain(dve, S["gate_step"])
        gates.step(dve.memset(gi[:, :], MASKED))
        gates.step(dve.memset(gf[:, :], 0.0))
        gates.step(dve.memset(gz[:, :], 0.0))

        def conv(i):
            ch = Chain(dve, S["conv_step"], 42 * i)
            j = bass.ds(i, 1)
            for c, (at, m) in enumerate(CHUNKS):
                p, g = c % 2, 4 * c
                if c == 5:
                    split_next(dve, "conv", i)
                mp = min(m, T - at)
                u = ut[:, p, :]
                dve.wait_ge(S["conv_c_ready"], 6 * i + c + 1)
                dve.wait_ge(S["summed"], BASE["conv"][1] + 24 * i + g + 3)
                ch.step(dve.tensor_tensor(u[:, 2:2 + mp], cs[:, p, 0:mp], bank[(g + 2) % 8][:, 0:mp], ALU.mult))
                if c == 0:
                    ch.step(dve.memset(u[:, 0:2], 0.0))
                else:
                    ch.step(dve.tensor_copy(u[:, 0:2], ut[:, 1 - p, CHUNKS[c - 1][1]:CHUNKS[c - 1][1] + 2]))
                if m > mp:
                    ch.step(dve.tensor_tensor(us[:, :, 2:2 + DT], cs[:, p, mp:m].rearrange("p (b t) -> p b t", b=DB),
                                              bank[(g + 2) % 8][:, mp:m].rearrange("p (b t) -> p b t", b=DB), ALU.mult))
                    ch.step(dve.tensor_copy(us[:, :, 0:2], cst[:, j].rearrange("p a b w -> p (a b) w")))
                dve.wait_ge(S["conv_t_ready"], 6 * i + c + 1)
                ch.step(dve.scalar_tensor_tensor(sil[:, 0:m], th[:, p, 0:m], 1.0, bank[(g + 3) % 8][:, 0:m],
                                                 ALU.add, ALU.mult))
                ch.sync()
                y = yc[:, 0:mp]
                ys = yc[:, mp:m].rearrange("p (b t) -> p b t", b=DB) if m > mp else None
                for tap in range(3):
                    wt = cw[:, tap, j]
                    if tap:
                        ch.step(dve.scalar_tensor_tensor(y, u[:, tap:tap + mp], wt, y, ALU.mult, ALU.add))
                    else:
                        ch.step(dve.tensor_scalar(y, u[:, 0:mp], wt, cb[:, j], ALU.mult, ALU.add))
                    if m > mp:
                        if tap:
                            ch.step(dve.scalar_tensor_tensor(ys, us[:, :, tap:tap + DT], wt, ys, ALU.mult, ALU.add))
                        else:
                            ch.step(dve.tensor_scalar(ys, us[:, :, 0:DT], wt, cb[:, j], ALU.mult, ALU.add))
                    ch.sync()
                dve.scalar_tensor_tensor(yc[:, 0:m], yc[:, 0:m], 0.5, bank[g % 8][:, 0:m],
                                         ALU.mult, ALU.mult).then_inc(S["bank_free"], 4)
                dve.wait_ge(S["bank_free"], BASE["conv"][1] + 24 * i + g + 4)
                wait(dve, S[f"stored{c % RING}"], ring_value("conv", i, c))
                dve.tensor_tensor(stage[:, c % RING, 0:m], yc[:, 0:m], sil[:, 0:m],
                                  ALU.mult).then_inc(S["conv_y_ready"], 1)
                if c < 5:
                    dve.wait_ge(S["conv_y_ready"], 6 * i + c + 1)
            ch.step(dve.tensor_copy(cnew_p[:, j, :].rearrange("p a w -> p (a w)"), ut[:, 1, mp:mp + 2]))
            dve.tensor_copy(cnew_s[:, j].rearrange("p a b w -> p (a b) w"), us[:, :, DT:DT + 2]).then_inc(S["conv_kept"], 1)
            dve.wait_ge(S["conv_y_ready"], 6 * i + 6)
            dve.wait_ge(S["conv_kept"], i + 1)
            ch.sync()
            assert ch.n == 42, ch.n
        quads(dve, "conv", conv)
        dve.wait_ge(S["gate_loaded"], 16 * 20)
        gates.sync()
        dve.scalar_tensor_tensor(gt[:, :], gf[:, :], -1.0, gf[:, :], ALU.mult, ALU.max).then_inc(S["gate_abs"], 1)
        dve.wait_ge(S["gate_log"], 1)
        gates.step(dve.scalar_tensor_tensor(gf[:, :], gf[:, :], 0.0, gt[:, :], ALU.min, ALU.subtract))
        gates.sync()
        gates.step(dve.memset(gf[H * NT:R96, DT:P], 0.0))
        gates.sync()
        gates.step(dve.tensor_tensor_scan(gF[:, :], gf[:, :], gz[:, :], 0.0, ALU.add, ALU.add))
        gates.sync()
        gates.step(dve.tensor_tensor(gi[:, :], gi[:, :], gF[:, :], ALU.subtract))
        gates.sync()
        dve.tensor_tensor_scan(gt[:, :], gi[:, :], gz[:, :], -3.0e38, ALU.max, ALU.add).then_inc(S["gate_scanned"], 1)
        dve.wait_ge(S["last_loaded"], 32)
        gates.step(dve.tensor_tensor_scan(mn[:, :], gl[:, :], fl[:, :], 0.0, ALU.max, ALU.add))
        gates.step(dve.memset(mprev[:, :], 0.0))
        gates.sync()
        dve.tensor_copy(mprev[:, 1:NT], mn[:, 0:NT - 1]).then_inc(S["m_ready"], 1)
        dve.wait_ge(S["m_loaded"], 16)
        gates.step(dve.tensor_scalar(gt[:, :], gt[:, :], gm[:, 0:1], None, ALU.max))
        gates.sync()
        dve.tensor_scalar(gz[:, :], gt[:, :], -1.0, None, ALU.mult).then_inc(S["gate_r"], 1)
        dve.tensor_tensor(gF[:, :], gF[:, :], gt[:, :], ALU.add).then_inc(S["gate_r"], 1)
        for kind in ("qk", "v", "o"):
            quads(dve, kind, lambda i, kind=kind: split_next(dve, kind, i))
            if kind == "qk":
                dve.wait_ge(S["gate_ws"], 1)
                dve.tensor_scalar(gw, gw, K_SCALE, None, ALU.mult).then_inc(S["gate_ws_scaled"], 1)

        def gate_by_silu(kind, i, g):
            G = ng[kind]
            n = (0 if kind == "z" else 2 * ng["z"]) + G * i + g
            m = 512 if kind == "z" else CHUNKS[g // 4][1]
            s = stage[:, g % RING, 0:m]
            dve.wait_ge(S["tanh_ready"], n + 1)
            r = dve.scalar_tensor_tensor(s, s, 1.0, bank[BANKS[G][g]][:, 0:m], ALU.add, ALU.mult)
            r.then_inc(S["bank_free"], 1)
            if kind == "z":
                dve.wait_ge(S["bank_free"], BASE[kind][1] + G * i + g + 1)
                dve.tensor_tensor(s, s, ghb[:, bass.ds(512 * i, 512)], ALU.mult).then_inc(S["silu_ready"], 1)

        def z(i):
            for g in range(NT):
                gate_by_silu("z", i, g)
            split_next(dve, "z", i)
            gate_by_silu("z", i, NT)
        dve.wait_ge(S["gain_loaded"], 16)
        quads(dve, "z", z)
        for g in range(ng["zx"]):
            gate_by_silu("zx", 0, g)

    @block.gpsimd
    def _(pool):
        def by_head(src_or_dst, tile, rows):
            for h in range(H):
                d = src_or_dst[rows + h]
                yield tile[h * NT:(h + 1) * NT, :], d[0:T].rearrange("(c t) -> c t", t=P)
                r = H * NT + h * DB
                yield tile[r:r + DB, 0:DT], d[T:TT].rearrange("(b t) -> b t", t=DT)

        for s in range(RING):
            pool.wait_ge(S[f"stored{s}"], ring_value("conv", 0, s))
        pool.wait_ge(S["gate_step"], 3)
        for tile, row in ((gi, 0), (gf, H)):
            for part, d in by_head(w["gate"], tile, row):
                pool.dma_start(part, d).then_inc(S["gate_loaded"], 16)
        for h in range(H):
            r = H * NT + h * DB
            pool.dma_start(gm[r:r + DB, :], st_m[0, :, h:h + 1]).then_inc(S["gate_loaded"], 16)
        pool.wait_ge(S["gate_scanned"], 1)
        pool.dma_start(w["last"][0:1, :].rearrange("a r -> r a"), gF[0:H * NT, P - 1:P]).then_inc(S["last_stored"], 16)
        pool.dma_start(w["last"][1:2, :].rearrange("a r -> r a"), gt[0:H * NT, P - 1:P]).then_inc(S["last_stored"], 16)
        pool.wait_ge(S["last_stored"], 32)
        pool.dma_start(fl[:, :], w["last"][0].rearrange("(h c) -> h c", h=H)).then_inc(S["last_loaded"], 16)
        pool.dma_start(gl[:, :], w["last"][1].rearrange("(h c) -> h c", h=H)).then_inc(S["last_loaded"], 16)
        pool.wait_ge(S["m_ready"], 1)
        pool.dma_start(m_prompt.rearrange("a b h -> h (a b)"), mn[:, NT - 1:NT]).then_inc(S["m_stored"], 16)
        pool.dma_start(w["mprev"].rearrange("(h c) -> h c", h=H), mprev[:, :]).then_inc(S["mprev_stored"], 16)
        pool.wait_ge(S["mprev_stored"], 16)
        pool.dma_start(gm[0:H * NT, :], w["mprev"].rearrange("(r a) -> r a", a=1)).then_inc(S["m_loaded"], 16)
        pool.wait_ge(S["gate_r"], 2)
        n = 0
        for h in range(H):
            r = H * NT + h * DB
            pool.dma_start(m_sample[0, :, h:h + 1], gF[r:r + DB, DT - 1:DT]).then_inc(S["gate_stored"], 16)
            n += 1
        for name, tile, ready in (("negr", gz, "gate_r"), ("a", gf, "gate_a"), ("em", gt, "gate_em"),
                                  ("g", gi, "gate_scanned"), ("ws", gw, "gate_ws_scaled")):
            if name != "negr":
                pool.wait_ge(S[ready], 1)
            for part, d in by_head(w[name], tile, 0):
                pool.dma_start(d, part).then_inc(S["gate_stored"], 16)
                n += 1
            if name == "a":
                pool.dma_start(w["wc"].rearrange("(r a) -> r a", a=1), gf[:, P - 1:P]).then_inc(S["gate_stored"], 16)
                n += 1
        pool.wait_ge(S["m_stored"], 16)
        pool.wait_ge(S["gate_stored"], 16 * n)
        for name, row in (("gc", "g"), ("wsc", "ws"), ("emc", "em")):
            for h in range(H):
                pool.dma_start(columns[name][:, h, :], w[row][h, 0:T].rearrange("(c t) -> t c", t=P)).then_inc(S["columns_loaded"], 16)
        pool.dma_start(columns["wcb"][:, :], row_bcast(w["wc"][0:H * NT], P)).then_inc(S["columns_loaded"], 16)
        pool.wait_ge(S["columns_loaded"], 16 * (3 * H + 1))

    ctx.close()


def mix(nc, S, sb, bank, w, ident, raw, columns, mv_prompt, C_prompt, n_prompt, tiles, shared, st_C, st_n, mem_k):
    HE = HD + 1
    qk = qk_tiles(raw)
    C = sb("C", [P, H, 2, HE])
    yst = sb("yst", [P, 8, P])
    xst = sb("xst", [P, H, P])
    xq = sb("xq", [P, 2, H, P])
    br = sb("br", [P, 2, 2, H, P])
    v1 = sb("v1", [P, 2, H, HE])
    oz = sb("oz", [P, 2, 4, 512])
    xz = sb("xz", [P, 2, H, P])
    gc, wsc, emc, wcb = (columns[x] for x in ("gc", "wsc", "emc", "wcb"))
    mkT = sb("mkT2", [P, H, NM])
    mv = sb("mv", [P, NM // P, H * XD])
    mask = sb("mask", [P, P])
    half, share, eps = (sb(x, [P, H]) for x in ("half", "share", "eps"))
    nm = sb("nm", [P, H, P])
    W = sb("W", [P, H, P])
    sw = sb("sw", [P, H, P])
    qs = sb("qs", [P, 8, P])
    kw = sb("kw", [P, H, HD])
    yml = sb("yml", [P, 2, H, HD])
    pr = sb("pr", [P, H, NM])
    pT = sb("pT", [P, H, 2, P])
    mx, nb, sums, rsum, den, rden, ssq, msq, rinv, coef = (
        sb(x, [P, H]) for x in ("mx", "nb", "sums", "rsum", "den", "rden", "ssq", "msq", "rinv", "coef"))
    junk = sb("junk", [P, HD])
    ctx = ExitStack()
    block = ctx.enter_context(nc.Block())
    EARLY, LATE = 4, 6
    DC_BANKS = (5, 6, 7, 0)

    def early_loaded(t, p):
        return 8 * EARLY * (t - p) + 16 * (EARLY - 1)

    def late_loaded(t, p):
        return 8 * LATE * (t - p) + 16 * LATE

    def col(t):
        return bass.ds(t * P, P)

    def is_last(t):
        return isinstance(t, int) and t == NT - 1

    def y_banks(t):
        return (1, 2) if is_last(t) else (7, 0)

    def is_first(t):
        return isinstance(t, int) and t == 0

    @block.sync
    def _(sp):
        def early(t, p):
            sem = S[f"early_loaded{p}"]
            wait(sp, S["qs_ready"], 4 * (t - 1))
            wait(sp, S["st_summed"], t - 1)
            wait(sp, S["nm_ready"], t - 1)
            if not isinstance(t, int):
                sp.dma_start(qk[:, p, :, :], w["qk"][:, :, col(t)].rearrange("f p t -> p f t")).then_inc(sem, 16)
            sp.dma_start(br[:, p, 0, :, :], w["negr"][:, col(t)].partition_broadcast(P)).then_inc(sem, 16)
            sp.dma_start(br[:, p, 1, :, :], w["a"][:, col(t)].partition_broadcast(P)).then_inc(sem, 16)
            sp.dma_start(xq[:, p, :, :], w["xa"][0:H, :, col(t)].rearrange("f p t -> p f t")).then_inc(sem, 16)

        def late(t, p):
            sem = S[f"late_loaded{p}"]
            wait(sp, S["dC_summed"], 8 * (t - 1))
            wait(sp, S["y_ready"], 4 * (t - 1))
            wait(sp, S["xa_ready"], t - 1)
            for a in range(2):
                sp.dma_start(v1[:, p, 2 * a:2 * a + 2, 0:HD],
                             w["tm"][a, col(t), :].rearrange("t (h e) -> t h e", h=2)).then_inc(sem, 16)
            for a in range(2):
                sp.dma_start(oz[:, p, 2 * a:2 * a + 2, :],
                             w["tm"][2 + 2 * a:4 + 2 * a, col(t), :].rearrange("a t n -> t a n")).then_inc(sem, 16)
            for a in range(2):
                sp.dma_start(xz[:, p, 2 * a:2 * a + 2, :],
                             w["xa"][H + 2 * a:H + 2 * a + 2, :, col(t)].rearrange("f p t -> p f t")).then_inc(sem, 16)

        early(0, 0)
        sp.dma_start(mkT[:, :, :], w["mkT"]).then_inc(S["keys_loaded"], 16)
        late(0, 0)
        sp.dma_start(mv[:, :, :], mv_prompt[0, 0].rearrange("(a s) h d -> s a (h d)", s=P)).then_inc(S["values_loaded"], 16)
        early(1, 1)
        late(1, 1)

        def state(b):
            for h in range(H):
                sp.dma_start(tiles["C"][:, bass.ds(b, 1), h, :, 0:HD],
                             st_C[0, bass.ds(b, 1), h].rearrange("b (a p) e -> p b a e", p=P)).then_inc(S["sample_loaded"], 16)
        with sp.Fori(1, NT // 2) as pair:
            for p in range(2):
                early(2 * pair + p, p)
                late(2 * pair + p, p)
            state(pair)
        state(0)
        load_sample_inputs(sp, S["sample_loaded"], tiles, shared, w, st_n, mem_k)
        sp.wait_ge(S["sample_loaded"], 16 * (SAMPLE_INPUTS + H * DB))
        sp.wait_ge(S["C_updated"], 8 * NT)
        sp.dma_start(C_prompt[0, 0].rearrange("h (a p) e -> p h a e", p=P), C[:, :, :, 0:HD]).then_inc(S["state_stored"], 16)
        sp.dma_start(n_prompt[0, 0].rearrange("h (a p) -> p h a", p=P), C[:, :, :, HD]).then_inc(S["state_stored"], 16)

    @block.gpsimd
    def _(pool):
        pool.memset(mask[:, :], 0.0).then_inc(S["mask_zero"], 1)
        pool.wait_ge(S["mask_zero"], 1)
        pool.affine_select(out=mask[:, :], in_=mask[:, :], compare_op=ALU.is_ge, fill=MASKED, base=0,
                           pattern=[[1, P]], channel_multiplier=-1).then_inc(S["mask_ready"], 1)
        pool.wait_ge(S["mask_ready"], 1)

        def ahead(t, p):
            pool.wait_ge(S[f"early_loaded{p}"], early_loaded(t, p))
            wait(pool, S["w_ready"], 4 * t)
            pool.tensor_tensor(nm[:, :, :], br[:, p, 0, :, :], mask[:, :].unsqueeze(1).broadcast_to([P, H, P]),
                               ALU.add).then_inc(S["nm_ready"], 1)
            for h in range(H):
                wait(pool, S["num_summed"], 4 * (t - 1) + h + 1)
                pool.tensor_tensor(qs[:, 2 * h:2 * h + 2, :], qk[:, p, 2 * h:2 * h + 2, :],
                                   br[:, p, 1, h, :].unsqueeze(1).broadcast_to([P, 2, P]),
                                   ALU.mult).then_inc(S["qs_ready"], 1)
        ahead(0, 0)
        pool.wait_ge(S["set"], 5)

        def tile(t, p):
            if not is_last(t):
                ahead(t + 1, 1 - p)
            pool.wait_ge(S["squares_ready"], 4 * t + 4)
            pool.tensor_tensor(rinv[:, :], ssq[:, :], share[:, :], ALU.mult).then_inc(S["msq_ready"], 1)
            pool.wait_ge(S["msq_ready"], 2 * t + 1)
            pool.tensor_tensor(msq[:, :], rinv[:, :], eps[:, :], ALU.add).then_inc(S["msq_ready"], 1)
            pool.wait_ge(S["msq_ready"], 2 * t + 2)
            pool.tensor_tensor(rinv[:, :], msq[:, :], half[:, :], ALU.pow).then_inc(S["rinv_ready"], 1)
        over_tiles(pool, NT, tile, last=2)

    @block.tensor
    def _(pe):
        def turn_keys(t, p):
            if not is_first(t):
                pe.wait_ge(S[f"early_loaded{p}"], early_loaded(t, p))
            wait(pe, S["t1_ready"], 4 * (t - 1) + 2)
            wait(pe, S["den_ready"], t)
            for i in range(8):
                m = pe.transpose(bank[1 + i // 4][:, (i % 4) * P:(i % 4 + 1) * P], qk[:, p, 8 + i, :], ident[:, :])
                if i % 4 == 3:
                    m.then_inc(S["k_turned"], 1)

        def products(t, p):
            if is_first(t):
                pe.wait_ge(S[f"early_loaded{p}"], early_loaded(t, p))
            wait(pe, S["t1_ready"], 4 * t)
            for h in range(H):
                m = pe.matmul(bank[3 + h // 2][:, (h % 2) * NM:(h % 2 + 1) * NM], xq[:, p, h, :], mkT[:, h, :],
                              start=True, stop=True)
                if h % 2:
                    m.then_inc(S["scores_summed"], 1)
            wait(pe, S["yT_ready"], 2 * (t - 1))
            for h in range(H):
                for d in range(2):
                    m = pe.matmul(bank[0][:, h * P:(h + 1) * P], qk[:, p, 8 + 2 * h + d, :], qk[:, p, 2 * h + d, :],
                                  start=(d == 0), stop=(d == 1))
            m.then_inc(S["st_summed"], 1)

        def turn_y(t, p):
            pe.wait_ge(S["y_ready"], 4 * t + 4)
            if is_last(t):
                pe.wait_ge(S["t1_ready"], 4 * NT)
                pe.wait_ge(S["den_ready"], NT)
            else:
                pe.wait_ge(S["xa_ready"], t + 1)
            for i in range(8):
                m = pe.transpose(bank[y_banks(t)[i // 4]][:, (i % 4) * P:(i % 4 + 1) * P],
                                 yml[:, p, i // 2, (i % 2) * P:(i % 2 + 1) * P], ident[:, :])
                if i % 4 == 3:
                    m.then_inc(S["y_turned"], 1)

        def tile(t, p):
            pe.wait_ge(S[f"late_loaded{p}"], late_loaded(t, p))
            pe.wait_ge(S["sw_ready"], t + 1)
            wait(pe, S["C_updated"], 8 * t)
            for h in range(H):
                if h < 2:
                    pe.wait_ge(S["kw_ready"], 4 * t + 2 * h + 2)
                else:
                    pe.wait_ge(S["exp_ready"], 4 * t + 2 * h - 2)
                pe.wait_ge(S["qs_ready"], 4 * t + h + 1)
                num = bank[1 + h][:, 0:HE]
                for d in range(2):
                    pe.matmul(num, qs[:, 2 * h + d, :], C[:, h, d, :], start=(d == 0), stop=False)
                pe.matmul(num, sw[:, h, :], v1[:, p, h, :], start=False, stop=True).then_inc(S["num_summed"], 1)
            wait(pe, S["pT_ready"], 2 * t)
            for j in range(8):
                h, d = j // 2, j % 2
                if j == 2:
                    wait(pe, S["xa_ready"], t)
                if j >= 4:
                    pe.wait_ge(S["C_updated"], 8 * t + j - 3)
                pe.matmul(bank[DC_BANKS[j % 4]][:, 0:HE], kw[:, h, d * P:(d + 1) * P], v1[:, p, h, :],
                          start=True, stop=True).then_inc(S["dC_summed"], 1)
            if not is_last(t):
                turn_keys(t + 1, 1 - p)
            pe.wait_ge(S["C_updated"], 8 * t + 8)
            if not is_first(t):
                turn_y(t - 1, 1 - p)
            pe.wait_ge(S["p_ready"], 4 * t + 4)
            for h in range(H):
                for s in range(2):
                    m = pe.transpose(bank[5 + h // 2][:, (h % 2) * NM + s * P:(h % 2) * NM + (s + 1) * P],
                                     pr[:, h, s * P:(s + 1) * P], ident[:, :])
                if h % 2:
                    m.then_inc(S["p_turned"], 1)
            if not is_last(t):
                products(t + 1, 1 - p)
            if is_last(t):
                turn_y(t, p)
            wait(pe, S["yT_ready"], 2 * t - 1)
            for h in range(H):
                pe.wait_ge(S["pT_ready"], 2 * t + h // 2 + 1)
                for s in range(2):
                    m = pe.matmul(bank[7][:, h * P:(h + 1) * P], mv[:, s, h * XD:(h + 1) * XD], pT[:, h, s, :],
                                  start=(s == 0), stop=(s == 1))
            m.then_inc(S["pv_summed"], 1)
        turn_keys(0, 0)
        pe.wait_ge(S["keys_loaded"], 16)
        products(0, 0)
        pe.wait_ge(S["values_loaded"], 16)
        pe.wait_ge(S["set"], 6)
        over_tiles(pe, NT, tile, last=2)

    @block.scalar
    def _(act):
        def weights(t, p):
            act.wait_ge(S["nm_ready"], t + 1)
            wait(act, S["sw_ready"], t)
            for h in range(H):
                act.activation(W[:, h, :], nm[:, h, :], ACT.Exp, bias=gc[:, h, bass.ds(t, 1)]).then_inc(S["w_ready"], 1)

        def keys(t, p):
            wait(act, S["dC_summed"], 8 * t)
            for h in range(H):
                act.wait_ge(S["k_turned"], 2 * t + h // 2 + 1)
                act.activation(kw[:, h, :], bank[1 + h // 2][:, (h % 2) * HD:(h % 2 + 1) * HD], ACT.Copy,
                               scale=wsc[:, h, bass.ds(t, 1)]).then_inc(S["kw_ready"], 1)

        def exps(t, p):
            act.wait_ge(S["nb_ready"], t + 1)
            wait(act, S["p_turned"], 2 * t)
            for h in range(H):
                act.activation(pr[:, h, :], bank[3 + h // 2][:, (h % 2) * NM:(h % 2 + 1) * NM], ACT.Exp,
                               bias=nb[:, h:h + 1], scale=XA_SCALE, accum_out=sums[:, h:h + 1]).then_inc(S["exp_ready"], 1)

        def y_out(t):
            for i in range(2):
                act.wait_ge(S["y_turned"], 2 * t + i + 1)
                if i == 0:
                    wait(act, S["y_stored"], 16 * t)
                act.activation(yst[:, 4 * i:4 * i + 4, :], bank[y_banks(t)[i]].ap().rearrange("p (f t) -> p f t", f=4),
                               ACT.Copy).then_inc(S["yT_ready"], 1)
            act.wait_ge(S["yT_ready"], 2 * t + 2)
            act.dma_start(w["yt"][0:8, :, col(t)].rearrange("f p t -> p f t"), yst[:, :, :]).then_inc(S["y_stored"], 16)

        def x_out(t):
            act.wait_ge(S["xa_ready"], t + 1)
            act.dma_start(w["yt"][12:16, :, col(t)].rearrange("f p t -> p f t"), xst[:, :, :]).then_inc(S["xa_stored"], 16)

        def tile(t, p):
            if not is_last(t):
                weights(t + 1, 1 - p)
            wait(act, S["msq_ready"], 2 * t)
            act.wait_ge(S["den_ready"], t + 1)
            for h in range(H):
                act.wait_ge(S["t1_ready"], 4 * t + h + 1)
                wait(act, S["squares_ready"], 4 * t + h)
                act.activation(junk[:, :], oz[:, p, h // 2, (h % 2) * HD:(h % 2 + 1) * HD], ACT.Square,
                               scale=rden[:, h:h + 1], accum_out=ssq[:, h:h + 1]).then_inc(S["squares_ready"], 1)
            if not is_last(t):
                keys(t + 1, 1 - p)
            if not is_first(t):
                y_out(t - 1)
                x_out(t - 1)
            wait(act, S["pv_summed"], t)
            for i in range(2):
                act.wait_ge(S["p_turned"], 2 * t + i + 1)
                act.activation(pT[:, 2 * i:2 * i + 2, :, :],
                               bank[5 + i].ap().rearrange("p (h s t) -> p h s t", h=2, s=2), ACT.Copy).then_inc(S["pT_ready"], 1)
            if not is_last(t):
                exps(t + 1, 1 - p)
        weights(0, 0)
        keys(0, 0)
        exps(0, 0)
        over_tiles(act, NT, tile, last=2)
        y_out(NT - 1)
        x_out(NT - 1)

    @block.vector
    def _(dve):
        for p in range(2):
            dve.memset(v1[:, p, :, HD:HE], 1.0).then_inc(S["set"], 1)
        for tile, value in ((half, -0.5), (share, 0.25 / HD), (eps, EPS)):
            dve.memset(tile[:, :], value).then_inc(S["set"], 1)
        dve.memset(C[:, :, :, :], 0.0).then_inc(S["set"], 1)
        STEPS, AHEAD = 10, 2

        def ahead(t, p, ch):
            for i in range(2):
                dve.wait_ge(S["scores_summed"], 2 * t + i + 1)
                ch.step(dve.tensor_reduce(mx[:, 2 * i:2 * i + 2], bank[3 + i].ap().rearrange("p (h s) -> p h s", h=2),
                                          AX.X, ALU.max))
            ch.sync()
            dve.tensor_scalar(nb[:, :], mx[:, :], -XA_SCALE, None, ALU.mult).then_inc(S["nb_ready"], 1)
            dve.wait_ge(S["w_ready"], 4 * t + 4)
            dve.wait_ge(S["st_summed"], t + 1)
            dve.scalar_tensor_tensor(sw[:, :, :], bank[0].ap().rearrange("p (h t) -> p h t", h=H), K_SCALE, W[:, :, :],
                                     ALU.mult, ALU.mult).then_inc(S["sw_ready"], 1)

        def attention_out(t, p):
            dve.wait_ge(S["pv_summed"], t + 1)
            wait(dve, S["xa_stored"], 16 * t)
            dve.scalar_tensor_tensor(xst[:, :, :], bank[7].ap().rearrange("p (h t) -> p h t", h=H), 0.5,
                                     xz[:, p, :, :], ALU.mult, ALU.mult).then_inc(S["xa_ready"], 1)

        def tile(t, p):
            ch = Chain(dve, S["mix_step"], AHEAD + STEPS * t)
            dve.wait_ge(S["exp_ready"], 4 * t + 4)
            ch.step(dve.reciprocal(rsum[:, :], sums[:, :]))
            ch.sync()
            for h in range(H):
                dve.tensor_scalar(pr[:, h, :], pr[:, h, :], rsum[:, h:h + 1], None, ALU.mult).then_inc(S["p_ready"], 1)
            if not is_first(t):
                attention_out(t - 1, 1 - p)

            def t1(h):
                th = oz[:, p, h // 2, (h % 2) * HD:(h % 2 + 1) * HD]
                dve.scalar_tensor_tensor(th, th, 1.0, bank[1 + h][:, 0:HD], ALU.add, ALU.mult).then_inc(S["t1_ready"], 1)
            dve.wait_ge(S[f"late_loaded{p}"], late_loaded(t, p))
            for h in range(H):
                dve.wait_ge(S["num_summed"], 4 * t + h + 1)
                ch.step(dve.tensor_copy(den[:, h:h + 1], bank[1 + h][:, HD:HE]))
                if h < H - 1:
                    t1(h)
            ch.sync()
            wait(dve, S["squares_ready"], 4 * t)
            ch.step(dve.scalar_tensor_tensor(rden[:, :], den[:, :], -1.0, den[:, :], ALU.mult, ALU.max))
            t1(H - 1)
            ch.sync()
            ch.step(dve.tensor_tensor(den[:, :], rden[:, :], emc[:, :, bass.ds(t, 1)].rearrange("p h a -> p (h a)"),
                                      ALU.max))
            ch.sync()
            dve.reciprocal(rden[:, :], den[:, :]).then_inc(S["den_ready"], 1)
            for j in range(8):
                dve.wait_ge(S["dC_summed"], 8 * t + j + 1)
                c = C[:, j // 2, j % 2, :]
                dve.scalar_tensor_tensor(c, c, wcb[:, bass.ds((j // 2) * NT + t, 1)], bank[DC_BANKS[j % 4]][:, 0:HE],
                                         ALU.mult, ALU.add).then_inc(S["C_updated"], 1)
            dve.wait_ge(S["rinv_ready"], t + 1)
            dve.wait_ge(S["den_ready"], t + 1)
            ch.step(dve.scalar_tensor_tensor(coef[:, :], rden[:, :], 0.25, rinv[:, :], ALU.mult, ALU.mult))
            ch.sync()
            wait(dve, S["y_turned"], 2 * (t - 1))
            for h in range(H):
                s = slice((h % 2) * HD, (h % 2 + 1) * HD)
                dve.wait_ge(S["t1_ready"], 4 * t + 4)
                dve.scalar_tensor_tensor(yml[:, p, h, :], oz[:, p, h // 2, s], coef[:, h:h + 1],
                                         oz[:, p, 2 + h // 2, s], ALU.mult, ALU.mult).then_inc(S["y_ready"], 1)
            if not is_last(t):
                ahead(t + 1, 1 - p, ch)
                dve.wait_ge(S["y_ready"], 4 * t + 4)
                assert ch.n == STEPS, ch.n
        ahead(0, 0, Chain(dve, S["mix_step"]))
        over_tiles(dve, NT, tile, last=2)
        attention_out(NT - 1, 1)

    ctx.close()


PRELOADED, LATER = range(8, 16), range(8)
SAMPLE_INPUTS = 14


def sample_tiles(sb):
    return dict(
        qk=sb("s_qk", [P, 16, TS]), xa=sb("s_xa", [P, 8, TS]),
        v1=sb("s_v1", [TS, H, HD + 1]),
        oz=sb("s_oz", [TS, 4, 512]),
        nr=sb("s_nr", [TS, H, TS]), ab=sb("s_ab", [P, H, TS]),
        gc=sb("s_gc", [TS, H]), wsc=sb("s_wsc", [TS, H]), emc=sb("s_emc", [TS, H]),
        wcb=sb("s_wcb", [P, H, DB]),
        C=sb("s_C", [P, DB, H, 2, HD + 1]),
        nrow=sb("s_nrow", [DB * H, HD]))


def key_tiles(shared):
    return shared.ap().rearrange("p f t -> p (f t)").rearrange("p (b a d) -> p b a d", b=2, a=2)


def load_sample_inputs(sp, sem, s, shared, w, st_n, mem_k):
    moves = [(s["qk"][:, :, :], w["qk"][:, :, T:TT].rearrange("f p t -> p f t")),
             (s["oz"][:, :, :], w["tm"][2:6, T:TT, :].rearrange("a t n -> t a n")),
             (s["xa"][:, :, :], w["xa"][:, :, T:TT].rearrange("f p t -> p f t")),
             (s["nr"][:, :, :], w["negr"][:, T:TT].partition_broadcast(TS)),
             (s["ab"][:, :, :], w["a"][:, T:TT].partition_broadcast(P)),
             (s["gc"][:, :], w["g"][:, T:TT].rearrange("h t -> t h")),
             (s["wsc"][:, :], w["ws"][:, T:TT].rearrange("h t -> t h")),
             (s["emc"][:, :], w["em"][:, T:TT].rearrange("h t -> t h")),
             (s["wcb"][:, :, :], w["wc"][H * NT:].rearrange("(h b) -> h b", h=H).partition_broadcast(P)),
             (s["nrow"][:, :], st_n[0].rearrange("b h d -> (b h) d"))]
    moves += [(s["v1"][:, 2 * a:2 * a + 2, 0:HD], w["tm"][a, T:TT, :].rearrange("t (h e) -> t h e", h=2)) for a in range(2)]
    moves += [(key_tiles(shared)[:, b, :, :], mem_k[0, b].rearrange("(a s) h d -> s a (h d)", s=P)) for b in range(2)]
    assert len(moves) == SAMPLE_INPUTS
    for dst, src in moves:
        sp.dma_start(dst, src).then_inc(sem, 16)


def sample(nc, S, sb, bank, w, ident, raw, shared, slots, tiles, mem_k, mem_v, w_out, C_sample, n_sample):
    BW = TS + DT
    HE = HD + 1
    qk, xa, v1, oz, nr, ab, gc, wsc, emc, wcb, C, nrow = (
        tiles[x] for x in ("qk", "xa", "v1", "oz", "nr", "ab", "gc", "wsc", "emc", "wcb", "C", "nrow"))
    K = key_tiles(shared)
    V = slots[:, 0:DB, :].rearrange("p b (a d) -> p b a d", a=2)
    KT = slots[:, DB:2 * DB, :].rearrange("p b (h s) -> p b h s", h=H)
    n0 = sb("s_n0", [P, 2, DB, H])
    mask = sb("s_mask", [TS, DB, DT])
    own = sb("s_own", [TS, DB])
    half = sb("s_half", [TS, H])
    qm = sb("s_qm", [P, H, 2, DB * BW])
    qxm = sb("s_qxm", [P, H, DB * BW])
    sw = sb("s_sw", [TS, H, TS])
    scratch = raw[:TS, :, :].rearrange("p k n -> p (k n)")
    pr = scratch[:, 0:D].rearrange("p (h s) -> p h s", h=H)
    kw = scratch[:, D:2 * D]
    kwm = scratch[:, 2 * D:4 * D].rearrange("p (s d) -> p s d", s=2)
    yst = qk[:, 0:8, :]
    xst = xa[:, 0:4, :]
    pT = sb("s_pT", [P, H, 2, TS])
    mx, nb, sums, rsum, den, den2, rden, ssq, msq, rinv, coef = (
        sb("s_" + x, [TS, H]) for x in ("mx", "nb", "sums", "rsum", "den", "den2", "rden", "ssq", "msq", "rinv", "coef"))
    junk = sb("s_junk", [TS, HD])
    ctx = ExitStack()
    block = ctx.enter_context(nc.Block())
    NUM_BANKS = (5, 0, 1, 4)
    DC_BANKS = (6, 7, 5, 0)

    def by_seq(ap):
        return ap.rearrange("p (b t) -> p b t", b=DB)

    def own_part(flat):
        return flat.rearrange("p (b x) -> p b x", x=BW)[:, :, 0:DT]

    @block.sync
    def _(sp):
        for b in range(2, DB):
            sp.wait_ge(S["s_K_turned"], b - 1)
            sp.dma_start(K[:, b % 2, :, :],
                         mem_k[0, b].rearrange("(a s) h d -> s a (h d)", s=P)).then_inc(S[f"s_K_loaded{b % 2}"], 16)
        sp.wait_ge(S["state_stored"], 32)
        sp.wait_ge(S["y_stored"], 16 * NT)
        sp.wait_ge(S["xa_stored"], 16 * NT)
        for b in range(DB):
            sp.dma_start(V[:, b, :, :], mem_v[0, b].rearrange("(a s) h d -> s a (h d)", s=P)).then_inc(S["s_V_loaded"], 16)
        sp.wait_ge(S["s_scores"], H)
        for s in PRELOADED:
            sp.dma_start(slots[:, s, :], w_out[0, s * P:(s + 1) * P, :]).then_inc(S["s_out"], 16)
        sp.wait_ge(S["s_K_turned"], DB)
        sp.dma_start(shared[:, :, :], w["yt"][:, :, 0:P].rearrange("f p t -> p f t")).then_inc(S["s_out"], 16)
        for b in range(DB):
            sp.wait_ge(S["s_C_updated"], 2 * H * (b + 1))
            sp.dma_start(C_sample[0, b].rearrange("h (a p) e -> p h a e", p=P),
                         C[:, b, :, :, 0:HD]).then_inc(S["s_out"], 16)
            if b == DB // 2:
                sp.wait_ge(S["s_y_out"], 1)
                sp.dma_start(w["yt"][0:8, :, T:TT].rearrange("f p t -> p f t"), yst).then_inc(S["s_out"], 16)
        sp.wait_ge(S["s_n_ready"], 1)
        sp.dma_start(n_sample[0].rearrange("b h d -> (b h) d"), nrow[:, :]).then_inc(S["s_out"], 16)
        sp.wait_ge(S["s_x_out"], 1)
        sp.dma_start(w["yt"][12:16, :, T:TT].rearrange("f p t -> p f t"), xst).then_inc(S["s_out"], 16)
        sp.wait_ge(S["s_out"], 16 * (DB + 4 + len(PRELOADED)))

    @block.gpsimd
    def _(pool):
        for h in range(H):
            pool.memset(qm[:, h, :, :], 0.0).then_inc(S["s_q_zero"], 1)
        pool.memset(mask[:, :, :], 0.0).then_inc(S["s_set"], 1)
        pool.memset(own[:, :], 1.0).then_inc(S["s_set"], 1)
        pool.memset(half[:, :], -0.5).then_inc(S["s_set"], 1)
        pool.wait_ge(S["s_set"], 3)
        pool.affine_select(out=mask[:, :, :], in_=mask[:, :, :], compare_op=ALU.is_ge, fill=MASKED, base=0,
                           pattern=[[DT, DB], [1, DT]], channel_multiplier=-1).then_inc(S["s_set"], 1)
        pool.affine_select(out=own[:, :], in_=own[:, :], compare_op=ALU.is_ge, fill=0.0, base=0,
                           pattern=[[-DT, DB]], channel_multiplier=1).then_inc(S["s_set"], 1)
        pool.wait_ge(S["s_set"], 5)
        pool.affine_select(out=mask[:, :, :], in_=mask[:, :, :], compare_op=ALU.is_ge, fill=MASKED, base=0,
                           pattern=[[-DT, DB], [0, DT]], channel_multiplier=1).then_inc(S["s_set"], 1)
        pool.affine_select(out=own[:, :], in_=own[:, :], compare_op=ALU.is_ge, fill=0.0, base=DT - 1,
                           pattern=[[DT, DB]], channel_multiplier=-1).then_inc(S["s_set"], 1)
        pool.wait_ge(S["s_squares"], H)
        pool.tensor_scalar(msq[:, :], ssq[:, :], 0.25 / HD, EPS, ALU.mult, ALU.add).then_inc(S["s_msq"], 1)
        pool.wait_ge(S["s_msq"], 1)
        pool.tensor_tensor(rinv[:, :], msq[:, :], half[:, :], ALU.pow).then_inc(S["s_rinv"], 1)

    @block.tensor
    def _(pe):
        def turn_k(b):
            if b >= 2:
                pe.wait_ge(S[f"s_K_loaded{b % 2}"], 16 * (b // 2))
                pe.wait_ge(S["s_KT_ready0"], b - 1)
                pe.wait_ge(S["s_KT_ready1"], b - 1)
            for h in range(H):
                for s in range(2):
                    m = pe.transpose(bank[((2, 6)[b % 2]) + h // 2][:, (h % 2) * NM + s * P:(h % 2) * NM + (s + 1) * P],
                                     K[:, b % 2, s, h * XD:(h + 1) * XD], ident[:, :])
            m.then_inc(S["s_K_turned"], 1)

        def numerator(h):
            pe.wait_ge(S["s_q_masked"], 2 * h + 2)
            if h == 0:
                pe.wait_ge(S["s_n_copied"], 1)
                pe.wait_ge(S["s_ones_ready"], 1)
                pe.wait_ge(S["s_sw_ready"], 1)
            if h == 2:
                pe.wait_ge(S["s_kw_ready"], H)
            num = bank[NUM_BANKS[h]][:TS, 0:HE]
            for b in range(DB):
                for d in range(2):
                    pe.matmul(num, qm[:, h, d, b * TS:(b + 1) * TS], C[:, b, h, d, :], start=(b + d == 0), stop=False)
            pe.matmul(num, sw[:, h, :], v1[:, h, :], start=False, stop=True).then_inc(S["s_num_summed"], 1)

        for d in range(2):
            m = pe.transpose(bank[5][:, d * DB * H:(d + 1) * DB * H], nrow[:, d * P:(d + 1) * P], ident[:DB * H, :DB * H])
        m.then_inc(S["s_n_turned"], 1)
        for h in range(H):
            for d in range(2):
                m = pe.matmul(bank[0][:TS, h * TS:(h + 1) * TS], qk[:, 8 + 2 * h + d, :], qk[:, 2 * h + d, :],
                              start=(d == 0), stop=(d == 1))
        m.then_inc(S["s_st_summed"], 1)
        for i in range(8):
            m = pe.transpose(bank[(1, 4)[i // 4]][:TS, (i % 4) * P:(i % 4 + 1) * P], qk[:, 8 + i, :], ident[:, :])
        m.then_inc(S["s_k_turned"], 1)
        turn_k(0)
        turn_k(1)
        for h in range(H):
            numerator(h)
            if h < H - 1:
                turn_k(2 * h + 2)
                turn_k(2 * h + 3)
        pe.wait_ge(S["s_KT_ready0"], DB)
        pe.wait_ge(S["s_KT_ready1"], DB)
        pe.wait_ge(S["s_qx_masked"], H)
        for h in range(H):
            for b in range(DB):
                m = pe.matmul(bank[2 + h // 2][:TS, (h % 2) * NM:(h % 2 + 1) * NM], qxm[:, h, b * TS:(b + 1) * TS],
                              KT[:, b, h, :], start=(b == 0), stop=(b == DB - 1))
            m.then_inc(S["s_scores"], 1)
        for b in range(DB):
            pe.wait_ge(S["s_kw_masked"], b + 1)
            for h in range(H):
                for d in range(2):
                    j = (b * H + h) * 2 + d
                    if j == 2:
                        pe.wait_ge(S["s_t1_ready"], 2)
                    if j >= 4:
                        pe.wait_ge(S["s_C_updated"], j - 3)
                    pe.matmul(bank[DC_BANKS[j % 4]][:, 0:HE], kwm[:, b % 2, h * HD + d * P:h * HD + (d + 1) * P],
                              v1[:, h, :], start=True, stop=True).then_inc(S["s_dC_summed"], 1)
            if b == 0:
                pe.wait_ge(S["s_t1_ready"], 4)
                pe.wait_ge(S["s_p_ready"], H)
                for h in range(H):
                    for s in range(2):
                        m = pe.transpose(bank[1][:, (2 * h + s) * TS:(2 * h + s + 1) * TS], pr[:, h, s * P:(s + 1) * P],
                                         ident[:TS, :TS])
                m.then_inc(S["s_p_turned"], 1)
            if b == 2:
                pe.wait_ge(S["s_y_ready"], H)
                for i in range(8):
                    m = pe.transpose(bank[2][:, i * TS:(i + 1) * TS], oz[:, 2 + i // 4, (i % 4) * P:(i % 4 + 1) * P],
                                     ident[:TS, :TS])
                m.then_inc(S["s_y_turned"], 1)
        pe.wait_ge(S["s_n_back_ready"], 1)
        for d in range(2):
            m = pe.transpose(bank[3][:DB * H, d * P:(d + 1) * P], n0[:, d].rearrange("p b h -> p (b h)"), ident[:, :])
        m.then_inc(S["s_n_back"], 1)
        pe.wait_ge(S["s_pT_ready"], 1)
        pe.wait_ge(S["s_V_loaded"], 16 * DB)
        for h in range(H):
            for c in range(DB):
                for s in range(2):
                    m = pe.matmul(bank[4][:, h * TS + c * DT:h * TS + (c + 1) * DT], V[:, c, s, h * XD:(h + 1) * XD],
                                  pT[:, h, s, c * DT:(c + 1) * DT], start=(s == 0), stop=(s == 1))
        m.then_inc(S["s_pv_summed"], 1)

    @block.scalar
    def _(act):
        act.wait_ge(S["s_n_turned"], 1)
        act.activation(C[:, :, :, :, HD].rearrange("p b h d -> p d b h"),
                       bank[5][:, 0:2 * DB * H].rearrange("p (d b h) -> p d b h", d=2, b=DB),
                       ACT.Copy).then_inc(S["s_n_copied"], 1)
        act.wait_ge(S["s_nm_ready"], 1)
        for h in range(H):
            act.activation(nr[:, h, :], nr[:, h, :], ACT.Exp, bias=gc[:, h:h + 1]).then_inc(S["s_w_ready"], 1)
        act.wait_ge(S["s_k_turned"], 1)
        for h in range(H):
            act.activation(kw[:, h * HD:(h + 1) * HD], bank[(1, 4)[h // 2]][:TS, (h % 2) * HD:(h % 2 + 1) * HD],
                           ACT.Copy, scale=wsc[:, h:h + 1]).then_inc(S["s_kw_ready"], 1)
        for b in range(DB):
            act.wait_ge(S["s_K_turned"], b + 1)
            act.activation(KT[:, b, 2:4, :], bank[(2, 6)[b % 2] + 1].ap().rearrange("p (h s) -> p h s", h=2),
                           ACT.Copy).then_inc(S["s_KT_ready1"], 1)

        def kw_mask(b):
            if b >= 2:
                act.wait_ge(S["s_dC_summed"], 2 * H * (b - 1))
            act.activation(kwm[:, b % 2, :], kw[:, :], ACT.Copy, scale=own[:, b:b + 1]).then_inc(S["s_kw_masked"], 1)

        act.wait_ge(S["s_set"], 7)
        act.wait_ge(S["s_kw_ready"], H)
        kw_mask(0)
        kw_mask(1)
        act.wait_ge(S["s_nb_ready"], 1)
        for h in range(H):
            act.activation(pr[:, h, :], bank[2 + h // 2][:TS, (h % 2) * NM:(h % 2 + 1) * NM], ACT.Exp,
                           bias=nb[:, h:h + 1], scale=XA_SCALE, accum_out=sums[:, h:h + 1]).then_inc(S["s_exp_ready"], 1)
        act.wait_ge(S["s_den_ready"], 1)
        for h in range(H):
            act.wait_ge(S["s_t1_ready"], h + 1)
            wait(act, S["s_squares"], h)
            act.activation(junk[:, :], oz[:, h // 2, (h % 2) * HD:(h % 2 + 1) * HD], ACT.Square,
                           scale=rden[:, h:h + 1], accum_out=ssq[:, h:h + 1]).then_inc(S["s_squares"], 1)
        act.wait_ge(S["s_p_turned"], 1)
        act.activation(pT.ap().rearrange("p h s t -> p (h s t)"), bank[1][:, :], ACT.Copy).then_inc(S["s_pT_ready"], 1)
        kw_mask(2)
        kw_mask(3)
        act.wait_ge(S["s_y_turned"], 1)
        act.activation(yst.rearrange("p f t -> p (f t)"), bank[2][:, :], ACT.Copy).then_inc(S["s_y_out"], 1)
        for b in range(4, DB):
            kw_mask(b)
        act.wait_ge(S["s_n_back"], 1)
        act.activation(nrow[:, :], bank[3][:DB * H, 0:HD], ACT.Copy).then_inc(S["s_n_ready"], 1)

    @block.vector
    def _(dve):
        ch = Chain(dve, S["s_step"])
        dve.memset(v1[:, :, HD:HE], 1.0).then_inc(S["s_ones_ready"], 1)
        dve.wait_ge(S["s_set"], 7)
        dve.tensor_tensor(nr[:, :, :], nr[:, :, :],
                          mask.ap().rearrange("p b t -> p (b t)").unsqueeze(1).broadcast_to([TS, H, TS]),
                          ALU.add).then_inc(S["s_nm_ready"], 1)
        for h in range(H):
            dve.wait_ge(S["s_q_zero"], h + 1)
            for d in range(2):
                dve.tensor_tensor(own_part(qm[:, h, d, :]), by_seq(qk[:, 2 * h + d, :]), by_seq(ab[:, h, :]),
                                  ALU.mult).then_inc(S["s_q_masked"], 1)
        dve.memset(qxm[:, :, :], 0.0).then_inc(S["s_qx_zero"], 1)
        dve.wait_ge(S["s_w_ready"], H)
        dve.wait_ge(S["s_st_summed"], 1)
        dve.scalar_tensor_tensor(sw[:, :, :], bank[0][:TS, 0:H * TS].rearrange("p (h t) -> p h t", h=H), K_SCALE,
                                 nr[:, :, :], ALU.mult, ALU.mult).then_inc(S["s_sw_ready"], 1)
        dve.wait_ge(S["s_qx_zero"], 1)
        for h in range(H):
            dve.tensor_copy(own_part(qxm[:, h, :]), by_seq(xa[:, h, :])).then_inc(S["s_qx_masked"], 1)

        def t1(h):
            dve.wait_ge(S["s_num_summed"], h + 1)
            ch.step(dve.tensor_copy(den[:, h:h + 1], bank[NUM_BANKS[h]][:TS, HD:HE]))
            ch.sync()
            th = oz[:, h // 2, (h % 2) * HD:(h % 2 + 1) * HD]
            dve.scalar_tensor_tensor(th, th, 1.0, bank[NUM_BANKS[h]][:TS, 0:HD], ALU.add, ALU.mult).then_inc(S["s_t1_ready"], 1)

        def key_half(b):
            dve.wait_ge(S["s_K_turned"], b + 1)
            dve.tensor_copy(KT[:, b, 0:2, :], bank[(2, 6)[b % 2]].ap().rearrange("p (h s) -> p h s", h=2)).then_inc(S["s_KT_ready0"], 1)
        for h in range(H):
            key_half(2 * h)
            key_half(2 * h + 1)
            if h < H - 1:
                t1(h)
        t1(H - 1)
        ch.step(dve.scalar_tensor_tensor(den2[:, :], den[:, :], -1.0, den[:, :], ALU.mult, ALU.max))
        ch.sync()
        ch.step(dve.tensor_tensor(den[:, :], den2[:, :], emc[:, :], ALU.max))
        ch.sync()
        dve.reciprocal(rden[:, :], den[:, :]).then_inc(S["s_den_ready"], 1)
        for i in range(2):
            dve.wait_ge(S["s_scores"], 2 * i + 2)
            ch.step(dve.tensor_reduce(mx[:, 2 * i:2 * i + 2], bank[2 + i][:TS, :].rearrange("p (h s) -> p h s", h=2),
                                      AX.X, ALU.max))
        ch.sync()
        dve.tensor_scalar(nb[:, :], mx[:, :], -XA_SCALE, None, ALU.mult).then_inc(S["s_nb_ready"], 1)

        def update(b):
            for j in range(2 * H * b, 2 * H * (b + 1)):
                h, d = j // 2 % H, j % 2
                dve.wait_ge(S["s_dC_summed"], j + 1)
                c = C[:, b, h, d, :]
                dve.scalar_tensor_tensor(c, c, wcb[:, h, b:b + 1], bank[DC_BANKS[j % 4]][:, 0:HE], ALU.mult,
                                         ALU.add).then_inc(S["s_C_updated"], 1)
        update(0)
        dve.wait_ge(S["s_exp_ready"], H)
        ch.step(dve.reciprocal(rsum[:, :], sums[:, :]))
        ch.sync()
        for h in range(H):
            dve.tensor_scalar(pr[:, h, :], pr[:, h, :], rsum[:, h:h + 1], None, ALU.mult).then_inc(S["s_p_ready"], 1)
        dve.wait_ge(S["s_den_ready"], 1)
        dve.wait_ge(S["s_rinv"], 1)
        ch.step(dve.scalar_tensor_tensor(coef[:, :], rden[:, :], 0.25, rinv[:, :], ALU.mult, ALU.mult))
        ch.sync()
        dve.wait_ge(S["s_t1_ready"], H)
        for h in range(H):
            s = slice((h % 2) * HD, (h % 2 + 1) * HD)
            z = oz[:, 2 + h // 2, s]
            dve.scalar_tensor_tensor(z, oz[:, h // 2, s], coef[:, h:h + 1], z, ALU.mult, ALU.mult).then_inc(S["s_y_ready"], 1)
        update(1)
        for b in range(2, DB):
            update(b)
        dve.wait_ge(S["s_C_updated"], 2 * H * DB)
        dve.tensor_copy(n0[:, :, :, :], C[:, :, :, :, HD].rearrange("p b h d -> p d b h")).then_inc(S["s_n_back_ready"], 1)
        dve.wait_ge(S["s_pv_summed"], 1)
        dve.scalar_tensor_tensor(xst, bank[4][:, 0:H * TS].rearrange("p (h t) -> p h t", h=H), 0.5,
                                 xa[:, 4:8, :], ALU.mult, ALU.mult).then_inc(S["s_x_out"], 1)

    ctx.close()


def output(nc, S, sb, bank, w, shared, slots, wl, w_out, x_prompt, x_sample, g_final, y_prompt, y_sample):
    KO = 16
    wh = sb("o_wh", [P, KO, D], F32R)
    ORDER = [*PRELOADED, *LATER]
    yt = (shared, sb("o_yt", [P, KO, P]))
    yh = sb("o_yh", [P, KO, P], F32R)
    yl = sb("o_yl", [P, KO, P], F32R)
    x = sb("o_x", [P, 2, D])
    gf = sb("o_gf", [P, D])
    xsq = sb("o_xsq", [P, D])
    ss, ms, sd, rs = (sb("o_" + n, [P, NT + 1]) for n in ("ss", "ms", "sd", "rs"))
    NX = NT + 1
    ctx = ExitStack()
    block = ctx.enter_context(nc.Block())
    x_rows = x_prompt[0].rearrange("(t p) d -> t p d", p=P)
    y_rows = y_prompt[0].rearrange("(t p) d -> t p d", p=P)
    x_smp = x_sample.rearrange("b t d -> (b t) d")
    y_smp = y_sample.rearrange("b t d -> (b t) d")

    def last(t):
        return isinstance(t, int) and t == NT

    def at(t):
        return TT - P if last(t) else t * P

    def rows(ap, t):
        return ap[bass.ds(t, 1)].rearrange("a p d -> (a p) d")

    @block.sync
    def _(sp):
        def load(t, p):
            wait(sp, S["y_split"], 2 * (t - 1))
            if not isinstance(t, int) or t > 0:
                sp.dma_start(yt[p][:, :, :], w["yt"][:, :, bass.ds(at(t), P)].rearrange("f p t -> p f t")).then_inc(S[f"yt_loaded{p}"], 16)
            wait(sp, S[f"y_out{p}"], 8 * (t - p))
            if last(t):
                sp.dma_start(x[TS:P, p, :], x_smp).then_inc(S[f"res_loaded{p}"], 16)
            else:
                sp.dma_start(x[:, p, :], rows(x_rows, t)).then_inc(S[f"res_loaded{p}"], 16)

        load(0, 0)
        for s in LATER:
            sp.dma_start(slots[:, s, :], w_out[0, s * P:(s + 1) * P, :]).then_inc(S[f"wout_loaded{s}"], 16)
        sp.dma_start(gf[:, :], row_bcast(g_final, P)).then_inc(S["gf_loaded"], 16)
        load(1, 1)
        with sp.Fori(1, NT // 2) as pair:
            load(2 * pair, 0)
            load(2 * pair + 1, 1)
        load(NT, 0)

    @block.tensor
    def _(pe):
        def tile(t, p):
            for k in range(KO):
                if isinstance(t, int) and t == 0:
                    pe.wait_ge(S["out_low_split"], k + 1)
                if k % 8 == 0:
                    pe.wait_ge(S["y_split"], 2 * t + k // 8 + 1)
                    if k == 0:
                        wait(pe, S["res_added"], 2 * (t - 1))
                for n in range(2):
                    out, c = bank[2 * p + n][:, :], slice(512 * n, 512 * (n + 1))
                    s = ORDER[k]
                    pe.matmul(out, yh[:, s, :], wh[:, s, c], start=(k == 0), stop=False)
                    pe.matmul(out, yh[:, s, :], wl[:, s, c], start=False, stop=False)
                    m = pe.matmul(out, yl[:, s, :], wh[:, s, c], start=False, stop=(k == KO - 1))
                if k % 8 == 7:
                    m.then_inc(S["y_half_used"], 1)
        over_tiles(pe, NX, tile)

    @block.scalar
    def _(act):
        def high(t, p):
            wait(act, S[f"yt_loaded{p}"], 8 * (t - p) + 16 * p)
            for i in range(2):
                wait(act, S["y_half_used"], 2 * (t - 1) + i + 1)
                s = slice(8 - 8 * i, 16 - 8 * i)
                act.activation(yh[:, s, :], yt[p][:, s, :], ACT.Copy).then_inc(S["y_high"], 1)

        def norm(t, p):
            r = slice(TS if last(t) else 0, P)
            act.wait_ge(S["res_added"], 2 * t + 2)
            c = bass.ds(t, 1)
            act.activation(xsq[r, :], x[r, p, :], ACT.Square, accum_out=ss[r, c]).then_inc(S["out_squared"], 1)
            act.wait_ge(S["out_mean"], t + 1)
            act.activation(sd[r, c], ms[r, c], ACT.Sqrt).then_inc(S["out_std"], 1)

        def tile(t, p):
            if not last(t):
                high(t + 1, 1 - p)
            wait(act, S["out_squared"], t)
            norm(t, p)
            act.wait_ge(S["out_ready"], t + 1)
            dst = y_smp if last(t) else rows(y_rows, t)
            act.dma_start(dst, x[TS if last(t) else 0:P, p, :]).then_inc(S[f"y_out{p}"], 16)

        def weights_high(k):
            s = ORDER[k]
            if s in LATER:
                act.wait_ge(S[f"wout_loaded{s}"], 16)
            act.activation(wh[:, s, :], slots[:, s, :], ACT.Copy).then_inc(S["out_high_split"], 1)
        weights_high(0)
        high(0, 0)
        for k in range(1, KO):
            weights_high(k)
        over_tiles(act, NX, tile)
        act.wait_ge(S["y_out0"], 16 * 9)
        act.wait_ge(S["y_out1"], 16 * 8)

    @block.vector
    def _(dve):
        def low(t, p):
            for i in range(2):
                dve.wait_ge(S["y_high"], 2 * t + i + 1)
                s = slice(8 - 8 * i, 16 - 8 * i)
                dve.tensor_tensor(yl[:, s, :], yt[p][:, s, :], yh[:, s, :].bitcast(F32), ALU.subtract).then_inc(S["y_split"], 1)

        def weights_low(k):
            s = ORDER[k]
            dve.wait_ge(S["out_high_split"], k + 1)
            dve.tensor_tensor(wl[:, s, :], slots[:, s, :], wh[:, s, :].bitcast(F32), ALU.subtract).then_inc(S["out_low_split"], 1)

        def tile(t, p):
            if not last(t):
                low(t + 1, 1 - p)
            r = slice(TS if last(t) else 0, P)
            c = bass.ds(t, 1)
            dve.wait_ge(S[f"res_loaded{p}"], 8 * (t - p) + 16)
            dve.wait_ge(S["y_half_used"], 2 * t + 2)
            for n in range(2):
                s = slice(512 * n, 512 * (n + 1))
                dve.tensor_tensor(x[r, p, s], x[r, p, s], bank[2 * p + n][r, :], ALU.add).then_inc(S["res_added"], 1)
            dve.wait_ge(S["out_squared"], t + 1)
            dve.tensor_scalar(ms[r, c], ss[r, c], 1.0 / D, EPS, ALU.mult, ALU.add).then_inc(S["out_mean"], 1)
            dve.wait_ge(S["out_std"], t + 1)
            dve.reciprocal(rs[r, c], sd[r, c]).then_inc(S["out_rstd"], 1)
            dve.wait_ge(S["out_rstd"], t + 1)
            dve.scalar_tensor_tensor(x[r, p, :], x[r, p, :], rs[r, c], gf[r, :], ALU.mult, ALU.mult).then_inc(S["out_ready"], 1)
        weights_low(0)
        low(0, 0)
        for k in range(1, KO):
            weights_low(k)
        dve.wait_ge(S["gf_loaded"], 16)
        over_tiles(dve, NX, tile)

    ctx.close()


_INS = ["x_prompt", "x_sample", "state_mlstm_C", "state_mlstm_n", "state_mlstm_m", "state_conv", "cache_mem_k",
        "cache_mem_v", "mem_prompt", "g_norm", "w_in", "b_if", "g_head", "conv_w", "conv_b", "g_mem", "w_mem_kv",
        "w_out", "g_final"]
_OUTS = [(1, T, D), (DB, DT, D), (1, 1, H, HD, HD), (1, 1, H, HD), (1, 1, H), (1, 1, 2, CC), (1, 1, NM, H, XD),
         (1, 1, NM, H, XD), (1, DB, H, HD, HD), (1, DB, H, HD), (1, DB, H), (1, DB, 2, CC)]


def kernel(**inputs):
    import numpy as np
    import concourse.bacc as bacc
    from concourse.bass_utils import run_bass_kernel_spmd

    arrays = {f"in_{n}": np.ascontiguousarray(inputs[n]) for n in _INS}
    nc = bacc.Bacc("TRN2", target_bir_lowering=False, num_devices=1)
    args = [nc.dram_tensor(n, a.shape, F32, kind="ExternalInput").ap() for n, a in arrays.items()]
    args += [nc.dram_tensor(f"out_{i}", s, F32, kind="ExternalOutput").ap() for i, s in enumerate(_OUTS)]
    layer(nc, *args)
    r = run_bass_kernel_spmd(nc, [arrays], core_ids=[0])
    return tuple(r.results[0][f"out_{i}"] for i in range(len(_OUTS)))
```
